# Optimizing a Trainium2 kernel written in Bass

```python
import math
import jax, jax.numpy as jnp
from jax import lax
import numpy as np

D_MODEL = 1024
BATCH = 1
SEQ = 256
DEPTH = 2

N_MEM = 256
HEAD_DIM = 64
ROT_DIM = HEAD_DIM // 4
ROPE_THETA = 500000.0
EPS = 1e-6
NEG_INF = -1e30
N_MIXERS = 3

A_HEADS = D_MODEL // HEAD_DIM
A_WIDTH = A_HEADS * HEAD_DIM
A_PATTERNS = ((128, 1), (512, 4), (2048, 16))
A_BLOCK = 64

B_HEADS = D_MODEL // (2 * HEAD_DIM)
B_WIDTH = B_HEADS * 2 * HEAD_DIM
B_QBLOCK = 128

C_HEADS = D_MODEL // HEAD_DIM
C_KV_HEADS = max(1, C_HEADS // 8)
C_GROUP = C_HEADS // C_KV_HEADS
C_Q_WIDTH = C_HEADS * HEAD_DIM
C_KV_WIDTH = C_KV_HEADS * HEAD_DIM
C_RADIUS = 128
C_BLOCK = 128

X_HEADS = 4
X_HEAD_DIM = D_MODEL // X_HEADS

_FF_RAW = -(-8 * D_MODEL // 3)
D_FF = -(-_FF_RAW // 256) * 256

N_A = len(range(0, DEPTH, N_MIXERS))
N_B = len(range(1, DEPTH, N_MIXERS))
N_C = len(range(2, DEPTH, N_MIXERS))


def rms_norm(x, g):
    xf = x.astype(jnp.float32)
    y = xf * lax.rsqrt(jnp.mean(xf * xf, axis=-1, keepdims=True) + EPS)
    return (y * g.astype(jnp.float32)).astype(x.dtype)

def split_heads(t, n):
    b, s, _ = t.shape
    return t.reshape(b, s, n, -1).transpose(0, 2, 1, 3)

def merge_heads(t):
    b, n, s, d = t.shape
    return t.transpose(0, 2, 1, 3).reshape(b, s, n * d)

def rope_tables(positions):
    inv_freq = ROPE_THETA ** (-jnp.arange(0, ROT_DIM, 2, dtype=jnp.float32) / ROT_DIM)
    ang = positions.astype(jnp.float32)[..., None] * inv_freq
    return jnp.cos(ang), jnp.sin(ang)

def apply_partial_rope(t, cos, sin):
    shape = (cos.shape[0],) + (1,) * (t.ndim - 3) + cos.shape[1:]
    c = cos.reshape(shape).astype(t.dtype)
    s = sin.reshape(shape).astype(t.dtype)
    half = ROT_DIM // 2
    t1, t2, rest = t[..., :half], t[..., half:ROT_DIM], t[..., ROT_DIM:]
    return jnp.concatenate([t1 * c - t2 * s, t2 * c + t1 * s, rest], axis=-1)

def banded_attention(q, k, v, radius, block, sink=None):
    L = q.shape[-2]
    nb = -(-L // block)
    pad = nb * block - L

    def pad_seq(t, lo, hi):
        return jnp.pad(t, [(0, 0)] * (t.ndim - 2) + [(lo, hi), (0, 0)])

    qb = pad_seq(q, 0, pad).reshape(q.shape[:-2] + (nb, block, q.shape[-1]))

    def band(t):
        tp = pad_seq(t, block, block + pad).reshape(t.shape[:-2] + (nb + 2, block, t.shape[-1]))
        return jnp.concatenate([tp[..., :-2, :, :], tp[..., 1:-1, :, :], tp[..., 2:, :, :]], axis=-2)

    kb, vb = band(k), band(v)
    s = jnp.einsum('...gnqd,...nkd->...gnqk', qb, kb,
                   preferred_element_type=jnp.float32) * (q.shape[-1] ** -0.5)
    qpos = jnp.arange(nb * block).reshape(nb, block, 1)
    kpos = (jnp.arange(nb)[:, None, None] - 1) * block + jnp.arange(3 * block)[None, None, :]
    valid = (jnp.abs(kpos - qpos) <= radius) & (kpos >= 0) & (kpos < L)
    s = jnp.where(valid, s, NEG_INF)
    m = jnp.max(s, axis=-1, keepdims=True)
    if sink is not None:
        sink = sink.astype(jnp.float32)
        m = jnp.maximum(m, sink)
    p = jnp.exp(s - m)
    denom = jnp.sum(p, axis=-1, keepdims=True)
    if sink is not None:
        denom = denom + jnp.exp(sink - m)
    o = jnp.einsum('...gnqk,...nkd->...gnqd', p.astype(v.dtype), vb,
                   preferred_element_type=jnp.float32) / denom
    lse = (m + jnp.log(denom))[..., 0]
    o = o.reshape(o.shape[:-3] + (nb * block, o.shape[-1]))[..., :L, :]
    lse = lse.reshape(lse.shape[:-2] + (nb * block,))[..., :L]
    return o, lse

def dilated_attention_mixer(u, w_in, w_out, cos, sin):
    b, s_len, _ = u.shape
    q, k, v = jnp.split(u @ w_in, 3, axis=-1)
    q = apply_partial_rope(split_heads(q, A_HEADS), cos, sin)
    k = apply_partial_rope(split_heads(k, A_HEADS), cos, sin)
    v = split_heads(v, A_HEADS)
    outs, lses = [], []
    for window, dil in A_PATTERNS:
        radius = window // (2 * dil)

        def by_residue(t):
            return t.reshape(b, A_HEADS, s_len // dil, dil, HEAD_DIM).swapaxes(2, 3)

        o, lse = banded_attention(by_residue(q)[..., None, :, :], by_residue(k), by_residue(v),
                                  radius, A_BLOCK)
        outs.append(o[..., 0, :, :].swapaxes(2, 3).reshape(b, A_HEADS, s_len, HEAD_DIM))
        lses.append(lse[..., 0, :].swapaxes(2, 3).reshape(b, A_HEADS, s_len))
    w = jax.nn.softmax(jnp.stack(lses), axis=0)
    o = jnp.einsum('pbhs,pbhsd->bhsd', w, jnp.stack(outs))
    return merge_heads(o).astype(u.dtype) @ w_out

def differential_attention_mixer(u, w_in, w_out, lam_q1, lam_k1, lam_q2, lam_k2, sub_g,
                                 cos, sin, layer_idx):
    b, s_len, _ = u.shape
    q, k, v = jnp.split(u @ w_in, 3, axis=-1)

    def qk_heads(t):
        return t.reshape(b, s_len, B_HEADS, 2, HEAD_DIM).transpose(0, 2, 3, 1, 4)

    q = apply_partial_rope(qk_heads(q), cos, sin)
    k = apply_partial_rope(qk_heads(k), cos, sin)
    v = split_heads(v, B_HEADS)
    lam_init = 0.8 - 0.6 * math.exp(-0.3 * layer_idx)
    f32 = jnp.float32
    lam = (jnp.exp(jnp.sum(lam_q1.astype(f32) * lam_k1.astype(f32)))
           - jnp.exp(jnp.sum(lam_q2.astype(f32) * lam_k2.astype(f32))) + lam_init)
    nqb = s_len // B_QBLOCK
    qb = q.reshape(b, B_HEADS, 2, nqb, B_QBLOCK, HEAD_DIM).transpose(3, 0, 1, 2, 4, 5)
    scale = HEAD_DIM ** -0.5

    def one_block(qblk):
        sc = jnp.einsum('bhcqd,bhckd->bhcqk', qblk, k, preferred_element_type=f32) * scale
        p = jax.nn.softmax(sc, axis=-1)
        a = p[:, :, 0] - lam * p[:, :, 1]
        return jnp.einsum('bhqk,bhkd->bhqd', a.astype(v.dtype), v, preferred_element_type=f32)

    o = lax.map(one_block, qb)
    o = o.transpose(1, 2, 0, 3, 4).reshape(b, B_HEADS, s_len, 2 * HEAD_DIM)
    o = rms_norm(o, sub_g) * (1.0 - lam_init)
    return merge_heads(o).astype(u.dtype) @ w_out

def windowed_gqa_sink_mixer(u, w_in, w_out, sink, cos, sin):
    b, s_len, _ = u.shape
    qkv = u @ w_in
    q = qkv[..., :C_Q_WIDTH]
    k = qkv[..., C_Q_WIDTH:C_Q_WIDTH + C_KV_WIDTH]
    v = qkv[..., C_Q_WIDTH + C_KV_WIDTH:]
    q = apply_partial_rope(split_heads(q, C_HEADS), cos, sin)
    k = apply_partial_rope(split_heads(k, C_KV_HEADS), cos, sin)
    v = split_heads(v, C_KV_HEADS)
    q = q.reshape(b, C_KV_HEADS, C_GROUP, s_len, HEAD_DIM)
    o, _ = banded_attention(q, k, v, C_RADIUS, C_BLOCK,
                            sink=sink.reshape(1, C_KV_HEADS, C_GROUP, 1, 1, 1))
    o = o.reshape(b, C_HEADS, s_len, HEAD_DIM)
    return merge_heads(o).astype(u.dtype) @ w_out

def memory_cross_attention(u, mem_n, wq, wkv, wo):
    q = split_heads(u @ wq, X_HEADS)
    k, v = jnp.split(mem_n @ wkv, 2, axis=-1)
    k = split_heads(k, X_HEADS)
    v = split_heads(v, X_HEADS)
    s = jnp.einsum('bhqd,bhkd->bhqk', q, k,
                   preferred_element_type=jnp.float32) * (X_HEAD_DIM ** -0.5)
    p = jax.nn.softmax(s, axis=-1)
    o = jnp.einsum('bhqk,bhkd->bhqd', p.astype(v.dtype), v)
    return merge_heads(o) @ wo

def swiglu_ffn(u, w_gate_up, w_down):
    g, up = jnp.split(u @ w_gate_up, 2, axis=-1)
    return (jax.nn.silu(g) * up) @ w_down

def first_inputs(seed: int = 0) -> dict:
    key = jax.random.key(seed)
    ks = iter(jax.random.split(key, 32))

    def nrm(shape, scale):
        return jax.random.normal(next(ks), shape, jnp.float32) * scale

    def dense(shape):
        return nrm(shape, shape[-2] ** -0.5)

    def gain(shape):
        return 1.0 + nrm(shape, 0.05)

    x = nrm((BATCH, SEQ, D_MODEL), 1.0)
    mem = nrm((BATCH, N_MEM, D_MODEL), 1.0)
    offset = jax.random.randint(next(ks), (BATCH, 1), 0, 4096, dtype=jnp.int32)
    positions = jnp.arange(SEQ, dtype=jnp.int32)[None, :] + offset
    return {
        "x": x, "mem": mem, "positions": positions,
        "mix_pre_g": gain((DEPTH, D_MODEL)), "mix_post_g": gain((DEPTH, D_MODEL)),
        "mem_pre_g": gain((DEPTH, D_MODEL)), "mem_kv_g": gain((DEPTH, D_MODEL)),
        "mem_post_g": gain((DEPTH, D_MODEL)),
        "ffn_pre_g": gain((DEPTH, D_MODEL)), "ffn_post_g": gain((DEPTH, D_MODEL)),
        "a_w_in": dense((N_A, D_MODEL, 3 * A_WIDTH)), "a_w_out": dense((N_A, A_WIDTH, D_MODEL)),
        "b_w_in": dense((N_B, D_MODEL, 3 * B_WIDTH)), "b_w_out": dense((N_B, B_WIDTH, D_MODEL)),
        "b_lam_q1": nrm((N_B, HEAD_DIM), 0.1), "b_lam_k1": nrm((N_B, HEAD_DIM), 0.1),
        "b_lam_q2": nrm((N_B, HEAD_DIM), 0.1), "b_lam_k2": nrm((N_B, HEAD_DIM), 0.1),
        "b_sub_g": gain((N_B, 2 * HEAD_DIM)),
        "c_w_in": dense((N_C, D_MODEL, C_Q_WIDTH + 2 * C_KV_WIDTH)),
        "c_w_out": dense((N_C, C_Q_WIDTH, D_MODEL)),
        "c_sink": nrm((N_C, C_HEADS), 0.5),
        "x_wq": dense((DEPTH, D_MODEL, D_MODEL)), "x_wkv": dense((DEPTH, D_MODEL, 2 * D_MODEL)),
        "x_wo": dense((DEPTH, D_MODEL, D_MODEL)),
        "w_gate_up": dense((DEPTH, D_MODEL, 2 * D_FF)), "w_down": dense((DEPTH, D_FF, D_MODEL)),
    }

def first_block(x, mem, positions, mix_pre_g, mix_post_g, mem_pre_g, mem_kv_g, mem_post_g,
              ffn_pre_g, ffn_post_g, a_w_in, a_w_out, b_w_in, b_w_out, b_lam_q1, b_lam_k1,
              b_lam_q2, b_lam_k2, b_sub_g, c_w_in, c_w_out, c_sink, x_wq, x_wkv, x_wo,
              w_gate_up, w_down):
    cos, sin = rope_tables(positions)
    h = x
    for i in range(DEPTH):
        kind, j = i % N_MIXERS, i // N_MIXERS
        u = rms_norm(h, mix_pre_g[i])
        if kind == 0:
            y = dilated_attention_mixer(u, a_w_in[j], a_w_out[j], cos, sin)
        elif kind == 1:
            y = differential_attention_mixer(u, b_w_in[j], b_w_out[j], b_lam_q1[j], b_lam_k1[j],
                                             b_lam_q2[j], b_lam_k2[j], b_sub_g[j], cos, sin, i)
        else:
            y = windowed_gqa_sink_mixer(u, c_w_in[j], c_w_out[j], c_sink[j], cos, sin)
        h = h + rms_norm(y, mix_post_g[i])
        u = rms_norm(h, mem_pre_g[i])
        y = memory_cross_attention(u, rms_norm(mem, mem_kv_g[i]), x_wq[i], x_wkv[i], x_wo[i])
        h = h + rms_norm(y, mem_post_g[i])
        u = rms_norm(h, ffn_pre_g[i])
        y = swiglu_ffn(u, w_gate_up[i], w_down[i])
        h = h + rms_norm(y, ffn_post_g[i])
    return h


N_META = 16
DN_HEADS = 4
DN_DK = 128
DN_DV = 128
DN_KEY = DN_HEADS * DN_DK
DN_VAL = DN_HEADS * DN_DV
CONV_W = 4
CHUNK = 64
SA_HEADS = 8
SA_DH = 64
SA_W = SA_HEADS * SA_DH
IDX_HEADS = 8
IDX_DH = 64
K_MAX = 256
Q_BLOCK = 128
ROPE_THETA_2 = 10000.0
MIX_W = DN_VAL + SA_W
N_GROUPS = 4
EXP_PER_GROUP = 8
N_EXPERTS = N_GROUPS * EXP_PER_GROUP
TOP_K_IN_GROUP = 2
D_EXPERT = 256
DEEPNORM_ALPHA = (2.0 * DEPTH) ** 0.25
DEEPNORM_BETA = (8.0 * DEPTH) ** -0.25

SPLIT_SIZES = (DN_KEY, DN_KEY, DN_VAL, DN_VAL, DN_HEADS, DN_HEADS,
               SA_W, SA_W, SA_W, IDX_HEADS * IDX_DH, IDX_DH, IDX_HEADS)
SPLIT_POINTS = tuple(int(s) for s in np.cumsum(SPLIT_SIZES)[:-1])
D_IN_PROJ = int(sum(SPLIT_SIZES))
VALUE_COLS = (2, 8)


F32 = jnp.float32

def layer_norm(x, g, b, eps=1e-5):
    xf = x.astype(F32)
    mu = jnp.mean(xf, -1, keepdims=True)
    var = jnp.mean(jnp.square(xf - mu), -1, keepdims=True)
    return ((xf - mu) * lax.rsqrt(var + eps) * g + b).astype(x.dtype)

def rope_tables_2(n_pos, dim):
    inv = 1.0 / (ROPE_THETA_2 ** (jnp.arange(0, dim, 2, dtype=F32) / dim))
    ang = jnp.arange(n_pos, dtype=F32)[:, None] * inv[None, :]
    ang = jnp.concatenate([ang, ang], -1)
    return jnp.cos(ang), jnp.sin(ang)

def apply_rope(x, cos, sin):
    half = x.shape[-1] // 2
    rot = jnp.concatenate([-x[..., half:], x[..., :half]], -1)
    shape = (1, cos.shape[0]) + (1,) * (x.ndim - 3) + (cos.shape[-1],)
    return (x * cos.reshape(shape) + rot * sin.reshape(shape)).astype(x.dtype)

def causal_dwconv(x, w):
    c = x.shape[-1]
    return lax.conv_general_dilated(x, w[:, None, :].astype(x.dtype), window_strides=(1,),
                                    padding=[(CONV_W - 1, 0)],
                                    dimension_numbers=('NWC', 'WIO', 'NWC'),
                                    feature_group_count=c)

def l2norm(x, eps=1e-6):
    return x * lax.rsqrt(jnp.sum(x * x, -1, keepdims=True) + eps)

def chunk_gated_delta_rule(q, k, v, g, beta):
    bsz, seq, h, dk = q.shape
    dv = v.shape[-1]
    n = seq // CHUNK

    def chunks(t):
        t = t.reshape((bsz, n, CHUNK, h) + t.shape[3:])
        return jnp.moveaxis(t, 3, 2)

    q, k, v, g, beta = (chunks(t) for t in (q, k, v, g, beta))
    q = q * dk ** -0.5
    gc = jnp.cumsum(g, axis=-1)
    pos = jnp.arange(CHUNK)
    tril = pos[:, None] >= pos[None, :]
    strict = pos[:, None] > pos[None, :]
    decay = jnp.exp(jnp.where(tril, gc[..., :, None] - gc[..., None, :], -jnp.inf))
    kb = k * beta[..., None]
    lower = jnp.where(strict, jnp.einsum('bnhid,bnhjd->bnhij', kb, k) * decay, 0.0)
    eye = jnp.eye(CHUNK, dtype=q.dtype)
    tmat = lax.linalg.triangular_solve(eye + lower, jnp.broadcast_to(eye, lower.shape),
                                       left_side=True, lower=True, unit_diagonal=True)
    u = tmat @ (v * beta[..., None])
    w = tmat @ (kb * jnp.exp(gc)[..., None])
    q_dec = q * jnp.exp(gc)[..., None]
    a_qk = jnp.where(tril, jnp.einsum('bnhid,bnhjd->bnhij', q, k) * decay, 0.0)
    g_last = gc[..., -1]
    k_dec = k * jnp.exp(g_last[..., None] - gc)[..., None]

    def step(state, inp):
        u_n, w_n, qd_n, a_n, kd_n, gl_n = inp
        v_new = u_n - jnp.einsum('bhck,bhkv->bhcv', w_n, state)
        o_n = jnp.einsum('bhck,bhkv->bhcv', qd_n, state) + jnp.einsum('bhij,bhjv->bhiv', a_n, v_new)
        state = state * jnp.exp(gl_n)[..., None, None] + jnp.einsum('bhck,bhcv->bhkv', kd_n, v_new)
        return state, o_n

    xs = tuple(jnp.moveaxis(t, 1, 0) for t in (u, w, q_dec, a_qk, k_dec, g_last))
    s0 = jnp.zeros((bsz, h, dk, dv), q.dtype)
    _, o = lax.scan(step, s0, xs)
    o = jnp.moveaxis(o, 0, 1)
    return jnp.moveaxis(o, 3, 2).reshape(bsz, seq, h, dv)

def deltanet_group(q, k, v, z, b_logit, a_logit, conv_w, a_log, dt_bias, norm_g):
    bsz, seq, _ = q.shape
    qkv = jax.nn.silu(causal_dwconv(jnp.concatenate([q, k, v], -1), conv_w)).astype(F32)
    q, k, v = jnp.split(qkv, [DN_KEY, 2 * DN_KEY], axis=-1)
    q = l2norm(q.reshape(bsz, seq, DN_HEADS, DN_DK))
    k = l2norm(k.reshape(bsz, seq, DN_HEADS, DN_DK))
    v = v.reshape(bsz, seq, DN_HEADS, DN_DV)
    beta = jax.nn.sigmoid(b_logit.astype(F32))
    g = -jnp.exp(a_log.astype(F32)) * jax.nn.softplus(a_logit.astype(F32) + dt_bias.astype(F32))
    pad = (-N_META) % CHUNK
    padf = lambda t: jnp.pad(t, ((0, 0), (pad, 0)) + ((0, 0),) * (t.ndim - 2))
    o = chunk_gated_delta_rule(padf(q), padf(k), padf(v), padf(g), padf(beta))[:, pad:]
    o = o * lax.rsqrt(jnp.mean(o * o, -1, keepdims=True) + 1e-6) * norm_g
    o = o.reshape(bsz, seq, DN_VAL) * jax.nn.silu(z.astype(F32))
    return o.astype(z.dtype)

def dsa_group(q, k, v, qi, ki, wi, cos, sin, cos_i, sin_i, k_top):
    bsz, seq, _ = q.shape
    q = apply_rope(q.reshape(bsz, seq, SA_HEADS, SA_DH), cos, sin)
    k = apply_rope(k.reshape(bsz, seq, SA_HEADS, SA_DH), cos, sin)
    v = v.reshape(bsz, seq, SA_HEADS, SA_DH)
    qi = apply_rope(qi.reshape(bsz, seq, IDX_HEADS, IDX_DH), cos_i, sin_i)
    ki = apply_rope(ki, cos_i, sin_i)
    wi = wi.astype(F32) * IDX_HEADS ** -0.5
    n_blk = -(-seq // Q_BLOCK)
    lq = n_blk * Q_BLOCK

    def blocks(t):
        t = jnp.pad(t, ((0, 0), (0, lq - seq)) + ((0, 0),) * (t.ndim - 2))
        return jnp.moveaxis(t.reshape((bsz, n_blk, Q_BLOCK) + t.shape[2:]), 1, 0)

    key_pos = jnp.arange(seq)
    q_pos = jnp.arange(lq).reshape(n_blk, Q_BLOCK)
    gather = jax.vmap(lambda arr, idx: arr[idx])

    def attend(args):
        qb, qib, wib, pos = args
        causal = key_pos[None, :] <= pos[:, None]
        rel = jax.nn.relu(jnp.einsum('bqhd,bsd->bqhs', qib, ki, preferred_element_type=F32) * IDX_DH ** -0.5)
        score = jnp.einsum('bqhs,bqh->bqs', rel, wib)
        score = jnp.where(causal[None], score, -jnp.inf)
        _, sel = lax.top_k(score, k_top)
        k_sel = gather(k, sel)
        v_sel = gather(v, sel)
        valid = sel <= pos[None, :, None]
        logits = jnp.einsum('bqhd,bqkhd->bhqk', qb, k_sel, preferred_element_type=F32) * SA_DH ** -0.5
        logits = jnp.where(valid[:, None], logits, -jnp.inf)
        p = jax.nn.softmax(logits, axis=-1)
        return jnp.einsum('bhqk,bqkhd->bqhd', p.astype(v.dtype), v_sel)

    out = lax.map(attend, (blocks(q), blocks(qi), blocks(wi), q_pos))
    return jnp.moveaxis(out, 0, 1).reshape(bsz, lq, SA_W)[:, :seq]

def hier_moe(h, w_grp, b_grp, w_rtr, b_rtr, w1, w3, w2):
    bsz, seq, d = h.shape
    t = h.reshape(-1, d)
    grp_prob = jax.nn.softmax((t @ w_grp).astype(F32) + b_grp, axis=-1)
    g_prob, g_sel = lax.top_k(grp_prob, 1)
    exp_logits = ((t @ w_rtr).astype(F32) + b_rtr).reshape(-1, N_GROUPS, EXP_PER_GROUP)
    in_grp = jnp.take_along_axis(exp_logits, g_sel[:, :, None], axis=1)[:, 0]
    e_prob, e_sel = lax.top_k(jax.nn.softmax(in_grp, axis=-1), TOP_K_IN_GROUP)
    gate = g_prob * e_prob / jnp.sum(e_prob, -1, keepdims=True)
    expert_id = g_sel * EXP_PER_GROUP + e_sel
    combine = jnp.sum(jax.nn.one_hot(expert_id, N_EXPERTS, dtype=F32) * gate[..., None], axis=1)
    hid = jax.nn.silu(jnp.einsum('td,edf->tef', t, w1)) * jnp.einsum('td,edf->tef', t, w3)
    y = jnp.einsum('tef,efd->td', hid * combine[..., None].astype(hid.dtype), w2)
    return y.reshape(bsz, seq, d)

def second_inputs(seed: int = 0) -> dict:
    key = jax.random.key(seed)
    ks = jax.random.split(key, 20)
    nrm = lambda k, shape, s: jax.random.normal(k, shape, F32) * s
    d_sc = D_MODEL ** -0.5
    col_scale = np.concatenate([np.full((s,), DEEPNORM_BETA if i in VALUE_COLS else 1.0, np.float32)
                                for i, s in enumerate(SPLIT_SIZES)])
    dt = jnp.exp(jax.random.uniform(ks[5], (DEPTH, DN_HEADS), F32, math.log(1e-3), math.log(1e-1)))
    return {
        'x': nrm(ks[0], (BATCH, SEQ, D_MODEL), 1.0),
        'meta_tokens': nrm(ks[1], (N_META, D_MODEL), 1.0),
        'w_in': nrm(ks[2], (DEPTH, D_MODEL, D_IN_PROJ), d_sc) * jnp.asarray(col_scale),
        'conv_w': nrm(ks[3], (DEPTH, CONV_W, 2 * DN_KEY + DN_VAL), CONV_W ** -0.5),
        'a_log': jnp.log(jax.random.uniform(ks[4], (DEPTH, DN_HEADS), F32, 1.0, 16.0)),
        'dt_bias': dt + jnp.log(-jnp.expm1(-dt)),
        'dn_norm_g': 1.0 + nrm(ks[6], (DEPTH, DN_DV), 0.02),
        'w_out': nrm(ks[7], (DEPTH, MIX_W, D_MODEL), MIX_W ** -0.5 * DEEPNORM_BETA),
        'ln1_g': 1.0 + nrm(ks[8], (DEPTH, D_MODEL), 0.02),
        'ln1_b': nrm(ks[9], (DEPTH, D_MODEL), 0.02),
        'w_grp': nrm(ks[10], (DEPTH, D_MODEL, N_GROUPS), d_sc),
        'b_grp': nrm(ks[11], (DEPTH, N_GROUPS), 0.01),
        'w_rtr': nrm(ks[12], (DEPTH, D_MODEL, N_EXPERTS), d_sc),
        'b_rtr': nrm(ks[13], (DEPTH, N_EXPERTS), 0.01),
        'w1': nrm(ks[14], (DEPTH, N_EXPERTS, D_MODEL, D_EXPERT), d_sc),
        'w3': nrm(ks[15], (DEPTH, N_EXPERTS, D_MODEL, D_EXPERT), d_sc),
        'w2': nrm(ks[16], (DEPTH, N_EXPERTS, D_EXPERT, D_MODEL), D_EXPERT ** -0.5 * DEEPNORM_BETA),
        'ln2_g': 1.0 + nrm(ks[17], (DEPTH, D_MODEL), 0.02),
        'ln2_b': nrm(ks[18], (DEPTH, D_MODEL), 0.02),
    }

def second_block(x, meta_tokens, w_in, conv_w, a_log, dt_bias, dn_norm_g, w_out, ln1_g, ln1_b,
              w_grp, b_grp, w_rtr, b_rtr, w1, w3, w2, ln2_g, ln2_b):
    bsz, seq, _ = x.shape
    total = seq + N_META
    k_top = min(K_MAX, seq // 4)
    meta = jnp.broadcast_to(meta_tokens[None].astype(x.dtype), (bsz, N_META, D_MODEL))
    h = jnp.concatenate([meta, x], axis=1)
    cos, sin = rope_tables_2(total, SA_DH)
    cos_i, sin_i = rope_tables_2(total, IDX_DH)
    for l in range(DEPTH):
        proj = h @ w_in[l]
        dq, dk, dv, dz, db, da, sq, sk, sv, iq, ik, iw = jnp.split(proj, SPLIT_POINTS, axis=-1)
        o_dn = deltanet_group(dq, dk, dv, dz, db, da, conv_w[l], a_log[l], dt_bias[l], dn_norm_g[l])
        o_sa = dsa_group(sq, sk, sv, iq, ik, iw, cos, sin, cos_i, sin_i, k_top)
        mix = jnp.concatenate([o_dn, o_sa.astype(o_dn.dtype)], axis=-1) @ w_out[l]
        h = layer_norm(DEEPNORM_ALPHA * h + mix, ln1_g[l], ln1_b[l])
        ffn = hier_moe(h, w_grp[l], b_grp[l], w_rtr[l], b_rtr[l], w1[l], w3[l], w2[l])
        h = layer_norm(DEEPNORM_ALPHA * h + ffn, ln2_g[l], ln2_b[l])
    return h[:, N_META:]


def setup_inputs(seed=0):
    out = dict(first_inputs(seed))
    for name, value in second_inputs(seed + 1).items():
        if name != "x":
            out[name + "_2"] = value
    return out


def reference(
    x, mem, positions, mix_pre_g, mix_post_g, mem_pre_g, mem_kv_g, mem_post_g, ffn_pre_g,
    ffn_post_g, a_w_in, a_w_out, b_w_in, b_w_out, b_lam_q1, b_lam_k1, b_lam_q2, b_lam_k2,
    b_sub_g, c_w_in, c_w_out, c_sink, x_wq, x_wkv, x_wo, w_gate_up, w_down, meta_tokens_2,
    w_in_2, conv_w_2, a_log_2, dt_bias_2, dn_norm_g_2, w_out_2, ln1_g_2, ln1_b_2, w_grp_2,
    b_grp_2, w_rtr_2, b_rtr_2, w1_2, w3_2, w2_2, ln2_g_2, ln2_b_2,
):
    x = first_block(
        x, mem, positions, mix_pre_g, mix_post_g, mem_pre_g, mem_kv_g, mem_post_g, ffn_pre_g,
        ffn_post_g, a_w_in, a_w_out, b_w_in, b_w_out, b_lam_q1, b_lam_k1, b_lam_q2, b_lam_k2,
        b_sub_g, c_w_in, c_w_out, c_sink, x_wq, x_wkv, x_wo, w_gate_up, w_down,
    )
    return second_block(
        x, meta_tokens_2, w_in_2, conv_w_2, a_log_2, dt_bias_2, dn_norm_g_2, w_out_2, ln1_g_2,
        ln1_b_2, w_grp_2, b_grp_2, w_rtr_2, b_rtr_2, w1_2, w3_2, w2_2, ln2_g_2, ln2_b_2,
    )


_drawn_inputs = setup_inputs


def setup_inputs(seed=0):
    import zlib

    import numpy as np

    out = dict(_drawn_inputs(seed))
    spreads = {}
    factors = {'b_lam_q1': 5.668, 'dn_norm_g_2': 6.242, 'b_grp_2': 8.0, 'b_rtr_2': 4.083}
    for name, (base, spread) in spreads.items():
        noise = np.random.default_rng([zlib.crc32(name.encode()), seed]).standard_normal(out[name].shape)
        drawn = base * np.exp(spread * noise) if base else spread * noise
        out[name] = __import__('jax').numpy.asarray(drawn.astype(out[name].dtype))
    for name, factor in factors.items():
        out[name] = (out[name] * factor).astype(out[name].dtype)
    return out
```

```python
import math
from contextlib import ExitStack

import numpy as np
import concourse.bass as bass
from concourse import mybir

F32 = mybir.dt.float32
I32 = mybir.dt.int32
ALU = mybir.AluOpType
ACT = mybir.ActivationFunctionType
AX = mybir.AxisListType

P = 128
DM = 1024
KT = DM // P
S1 = 256
META = 16
S2 = S1 + META
DEPTH = 2
DFF = 2816
FT = DFF // P
HD = 64
SLOTS = 6
SLOT_W = 4096
BANKS = 8
BANK_W = 512
NEG = -1e30
SPLIT = dict(dq=0, dk=512, dv=1024, dz=1536, db=2048, da=2052, sq=2056, sk=2568, sv=3080,
             iq=3592, ik=4104, iw=4168)
D_IN = 4176
DH = 4
SH = 8
TOPK = 64
NE = 32
DE = 256
ALPHA = (2.0 * DEPTH) ** 0.25
TOK = [(0, 128), (128, 128), (256, 16)]
LAM_INIT = 0.8 - 0.6 * math.exp(-0.3 * 1)
PATTERNS = ((128, 1), (512, 4), (2048, 16))

TABLES = dict(ident=128, rot1=128, rot2=128, invf=1, maskA=512)
TABLES2 = dict(triu=128, cos2=272, sin2=272, causal=816, decay=128, strict=128,
               levels=7 * 128, iota=32, group=32, edges=9)


def offsets(widths):
    at, out = 0, {}
    for k, w in widths.items():
        out[k] = (at, w)
        at += w
    return out, at


def tables():
    i = np.arange(128)
    one = {k: np.zeros((128, w), np.float32) for k, w in TABLES.items()}
    two = {k: np.zeros((128, w), np.float32) for k, w in TABLES2.items()}
    one["ident"][i, i] = 1.0
    for m in range(128):
        r = m % 64
        if r < 8:
            one["rot1"][m + 8, m] = -1.0
        elif r < 16:
            one["rot1"][m - 8, m] = 1.0
        if r < 32:
            one["rot2"][m + 32, m] = -1.0
        else:
            one["rot2"][m - 32, m] = 1.0
    inv = (np.float32(500000.0) ** (-np.arange(0, 16, 2, dtype=np.float32) / np.float32(16))).astype(np.float32)
    one["invf"][:, 0] = np.where(i % 64 < 16, inv[i % 8], 0.0)
    q, k = np.arange(S1)[:, None], np.arange(S1)[None, :]
    count = sum(((abs(q - k) % d == 0) & (abs(q - k) // d <= w // (2 * d))).astype(np.float64)
                for w, d in PATTERNS)
    m = np.where(count > 0, np.log(np.maximum(count, 1)) * math.sqrt(HD), NEG).astype(np.float32)
    one["maskA"][:] = m.reshape(2, 128, S1).transpose(1, 0, 2).reshape(128, 512)
    t, j = i[:, None], i[None, :]
    two["triu"][:] = t <= j
    inv2 = (1.0 / (np.float32(10000.0) ** (np.arange(0, 64, 2, dtype=np.float32) / np.float32(64)))).astype(np.float32)
    ang = (np.arange(S2, dtype=np.float32)[None, :] * inv2[i % 32][:, None]).astype(np.float32)
    two["cos2"][:] = np.cos(ang)
    two["sin2"][:] = np.sin(ang)
    for n, (t0, c) in enumerate(TOK):
        two["causal"][:c, n * S2:(n + 1) * S2] = np.where(np.arange(S2)[None, :] <= t0 + np.arange(c)[:, None], 0, NEG)
    two["decay"][:] = np.where(j >= t, 0, NEG)
    two["strict"][:] = j > t
    for n in range(7):
        s = 1 << n
        two["levels"][:, n * 128:(n + 1) * 128] = (t // (2 * s) == j // (2 * s)) & (t % (2 * s) < s) & (j % (2 * s) >= s)
    two["iota"][:] = np.arange(NE)
    two["edges"][:] = 32 * np.arange(9)
    two["group"][:] = np.arange(NE) // 8
    return (np.concatenate(list(one.values()), 1), np.concatenate(list(two.values()), 1))


ROUND = 12582912.0
TWO_PI = (6.28125, 8117 / 4194304, 2 * math.pi - 6.28125 - 8117 / 4194304)
CONSTS = 26
O_DONE = {(0, "A"): 8, (0, "X"): 12, (1, "B"): 20, (1, "X"): 24}


def build(nc, A, out):
    ctx = ExitStack()
    with ctx:
        def sb(name, shape, dt=F32, stack=ctx):
            return stack.enter_context(nc.sbuf_tensor(name, shape, dt))

        def sem(name):
            return ctx.enter_context(nc.semaphore(name))

        O1, W1 = offsets(TABLES)
        O2, W2 = offsets(TABLES2)

        ring = sb("weight_ring", [P, SLOTS, SLOT_W])
        hT = sb("hT", [P, KT, S2])
        tab1 = sb("tables1", [P, W1])
        ones = sb("ones", [P, P])
        eps6 = sb("eps6", [P, 1])
        gains = sb("gains", [P, 113 + 2 * 81])
        std = sb("std", [P, S2])
        rstd = sb("rstd", [P, S2])
        uT = sb("uT", [P, KT, S2])
        yT = sb("yT", [P, KT, S2])
        sq = sb("sq", [P, KT, S2])
        oT = sb("oT", [P, KT, S2])
        first = ExitStack()
        memn = sb("memn", [P, KT, S1], stack=first)
        probs = sb("probs", [P, 3, 2, 2 * S1], stack=first)
        probsT = sb("probsT", [P, 2, 2 * S1], stack=first)
        rope = sb("rope", [P, 2, S1], stack=first)
        rot_tmp = sb("rot_tmp", [P, 2 * S1], stack=first)
        small = sb("small", [P, 64], stack=first)
        lamv = sb("lamv", [P, 4, HD], stack=first)
        pos_i = sb("pos_i", [P, S1], I32, stack=first)
        grows = sb("gain_rows", [P, 3, P], stack=first)
        qkv = sb("qkv", [P, 3, KT * S1], stack=first)
        first.close()
        ident = tab1[:, O1["ident"][0]:O1["ident"][0] + P]
        rot1 = tab1[:, O1["rot1"][0]:O1["rot1"][0] + P]
        rot2 = tab1[:, O1["rot2"][0]:O1["rot2"][0] + P]
        invf = tab1[:, O1["invf"][0]:O1["invf"][0] + 1]
        maskA = tab1[:, O1["maskA"][0]:O1["maskA"][0] + 2 * S1]
        hx = hT[:, :, META:S2]
        qT = qkv[:, 0, :].rearrange("p (k t) -> p k t", k=KT)
        kT = qkv[:, 1, :].rearrange("p (k t) -> p k t", k=KT)
        vt = qkv[:, 2, :].rearrange("p (t n) -> p t n", t=2)
        hid = qkv[:, :, :].rearrange("p a n -> p (a n)")[:, 0:FT * S1].rearrange("p (f t) -> p f t", f=FT)
        flat = lambda x: x[:, :, :].rearrange("p k t -> p (k t)")[:, 0:2 * DM].rearrange("p (t n) -> p t n", t=2)
        xin, memin, uT_flat = flat(yT), flat(oT), flat(uT)
        rmax = small[:, 0:12].rearrange("p (a c j) -> p a c j", a=3, c=2)
        nmax = small[:, 12:24].rearrange("p (a c j) -> p a c j", a=3, c=2)
        den = small[:, 24:36].rearrange("p (a c j) -> p a c j", a=3, c=2)
        rden = small[:, 36:48].rearrange("p (a c j) -> p a c j", a=3, c=2)
        lam = small[:, 48:49]
        lam_parts = small[:, 50:54]
        ps = ctx.enter_context(nc.psum_tensor("ps", [P, BANKS, BANK_W], F32))

        second = ExitStack()
        tab2 = sb("tables2", [P, W2], stack=second)
        small_w = sb("small_w", [P, KT, 144], stack=second)
        router_w = sb("router_w", [P, KT, 36], stack=second)
        rows2 = sb("rows2", [P, DEPTH, 44], stack=second)
        z_gate = sb("z_gate", [P, DH, S2], stack=second)
        chosen = sb("chosen", [P, 3, NE], stack=second)
        rank1 = sb("rank1", [P, 3, NE], stack=second)
        rank = sb("rank", [P, 3, NE], stack=second)
        group_max = sb("group_max", [P, 8], stack=second)
        over_edge = sb("over_edge", [P, 8, 8], stack=second)
        passes = sb("passes", [P, 8], stack=second)
        starts = sb("starts", [P, 9], stack=second)
        pass_at = sb("pass_at", [P, 1], stack=second)
        steps = sb("steps", [P, DEPTH, 16], I32, stack=second)
        tok = sb("tok", [P, 3, 16], stack=second)
        gate_log = sb("gate_log", [P, 3, 8], stack=second)
        gate_exp = sb("gate_exp", [P, 3, 8], stack=second)
        gate_x = sb("gate_x", [P, 3, 4], stack=second)
        g_tok = sb("g_tok", [P, 3, 4], stack=second)
        beta = sb("beta", [P, 3, 4], stack=second)
        neg_a = sb("neg_a", [P, 4], stack=second)
        cum = sb("cum", [P, 3, 12], stack=second)
        ecum = sb("ecum", [P, 3, 12], stack=second)
        logits = sb("logits", [P, 3, 36], stack=second)
        grp8 = sb("grp8", [P, 3, 8], stack=second)
        top8 = sb("top8", [P, 2, 3, 8], stack=second)
        idx8 = sb("idx8", [P, 2, 3, 8], mybir.dt.uint32, stack=second)
        idxf = sb("idxf", [P, 2, 3, 8], stack=second)
        rexp = sb("rexp", [P, 3, 8], stack=second)
        gates = sb("gates", [P, 3, 4], stack=second)
        comb = sb("comb", [P, 2, 3, NE], stack=second)
        stat2 = sb("stat2", [P, 4, 3], stack=second)
        best = sb("best", [P, 3, 8], stack=second)
        eps5 = sb("eps5", [P, 1], stack=second)
        eps128 = sb("eps128", [P, 1], stack=second)
        middle = ExitStack()
        qs = sb("qs", [P, 4, S2], stack=middle)
        ks = sb("ks", [P, 4, S2], stack=middle)
        vs = sb("vs", [P, 3, 512], stack=middle)
        iq = sb("iq", [P, 4, S2], stack=middle)
        ik = sb("ik", [P, 1, S2], stack=middle)
        rot2_tmp = sb("rot2_tmp", [P, S2], stack=middle)
        work = sb("work", [P, 3232], stack=middle)
        middle.close()
        h_tok = sb("h_tok", [P, 3, DM], stack=second)
        x_g = sb("x_g", [P, KT, P], stack=second)
        sel = sb("sel", [P, 3, P], stack=second)
        sel_gate = sb("sel_gate", [P, 3, P], stack=second)
        scatter = sb("scatter", [P, S2], stack=second)
        e_out = sb("e_out", [P, DM], stack=second)
        e_silu = sb("e_silu", [P, DE], stack=second)
        e_hid = sb("e_hid", [P, DE], stack=second)
        e_hidT = sb("e_hidT", [P, 2, P], stack=second)
        second.close()
        meta_rows = z_gate[:, :, :].rearrange("p h t -> p (h t)")[0:META, 0:DM]

        def T2(name):
            return tab2[:, O2[name][0]:O2[name][0] + O2[name][1]]

        heads = lambda x: x.rearrange("p (h t) -> p h t", h=DH)
        triu, decay_mask, strict = T2("triu"), T2("decay"), T2("strict")
        cos2, sin2, iota, group, edges = T2("cos2"), T2("sin2"), T2("iota"), T2("group"), T2("edges")
        causal = T2("causal").rearrange("p (n t) -> p n t", n=3)
        levels = T2("levels").rearrange("p (s t) -> p s t", s=7)
        relu_s = work[:, 0:544].rearrange("p (a t) -> p a t", a=2)
        score = work[:, 544:1360].rearrange("p (n t) -> p n t", n=3)
        probs2 = work[:, 1360:2176].rearrange("p (a t) -> p a t", a=3)
        probsT2 = work[:, 2176:2944].rearrange("p (a k t) -> p a k t", a=2, k=3)
        LT = work[:, 0:1536].rearrange("p (n c) -> p n c", n=3)
        QK = work[:, 1536:3072].rearrange("p (n c) -> p n c", n=3)
        dn = ring[:, 4:6, :].rearrange("p s n -> p (s n)")
        conv_in = dn[:, 0:3300].rearrange("p (i t) -> p i t", i=12)
        Tm = dn[:, 0:1536].rearrange("p (n c) -> p n c", n=3)
        TT = dn[:, 1536:3072].rearrange("p (n c) -> p n c", n=3)
        cv_v = dn[:, 3300:4388].rearrange("p (i t) -> p i t", i=4)
        v_new = dn[:, 3300:3812]
        k_tok = dn[:, 4388:5924].rearrange("p (n c) -> p n c", n=3)
        v_beta = dn[:, 5924:7460].rearrange("p (n c) -> p n c", n=3)
        state = dn[:, 7460:7972]
        cv_qk = uT
        yflat = yT[:, :, :].rearrange("p k t -> p (k t)")
        sflat = sq[:, :, :].rearrange("p k t -> p (k t)")
        oflat = oT[:, :, :].rearrange("p k t -> p (k t)")
        Xs = yflat[:, 0:1536].rearrange("p (n c) -> p n c", n=3)
        decay = yflat[:, 1536:2048]
        As = sflat[:, 0:1536].rearrange("p (n c) -> p n c", n=3)
        k_be = As
        w_T = LT
        egc = sflat[:, 1536:2048]
        beta_strict = oflat[:, 1088:1600]
        yacc = yT

        full = [sem(f"psum_full{b}") for b in range(BANKS)]
        free = [sem(f"psum_free{b}") for b in range(BANKS)]
        loaded = [sem(f"weights_loaded{s}") for s in range(SLOTS)]
        const_in = sem("const_in")
        memset_done = sem("memset_done")
        gain_cols = sem("gain_cols")
        rope_ready = sem("rope_ready")
        rope_args = sem("rope_args")
        x_in = sem("x_in")
        mem_in = sem("mem_in")
        x_ready = sem("x_ready")
        pre_sq = sem("pre_sq")
        post_sq = sem("post_sq")
        std_ready = sem("std_ready")
        u_ready = sem("u_ready")
        mem_u = sem("mem_u")
        memn_ready = sem("memn_ready")
        h_ready = sem("h_ready")
        q_raw = sem("q_raw")
        qk_ready = sem("qk_ready")
        xqk_raw = sem("xqk_raw")
        v_ready = sem("v_ready")
        max_ready = sem("max_ready")
        exp_ready = sem("exp_ready")
        p_ready = sem("p_ready")
        pt_ready = sem("pt_ready")
        o_ready = sem("o_ready")
        lam_args = sem("lam_args")
        lam_exp = sem("lam_exp")
        sub_sq = sem("sub_sq")
        sub_std = sem("sub_std")
        sub_done = sem("sub_done")
        silu_ready = sem("silu_ready")
        hid_ready = sem("hid_ready")
        out_sb = sem("out_sb")
        stored = sem("stored")
        const2_in = [sem(f"const2_in{l}") for l in range(DEPTH)]
        small_in = sem("small_in")
        router_in = sem("router_in")
        meta_in = sem("meta_in")
        meta_ready = sem("meta_ready")
        zeros2 = sem("zeros2")
        ready2 = sem("ready2")
        tok_ready = sem("tok_ready")
        sp_args = sem("sp_args")
        sp_logs = sem("sp_logs")
        gb_ready = sem("gb_ready")
        conv_raw = sem("conv_raw")
        conv_acc = sem("conv_acc")
        conv_out = sem("conv_out")
        l2_sq = sem("l2_sq")
        l2_root = sem("l2_root")
        qk_unit = sem("qk_unit")
        cum_ready = sem("cum_ready")
        ecum_ready = sem("ecum_ready")
        decay_args = sem("decay_args")
        decay_ready = sem("decay_ready")
        egc_ready = sem("egc_ready")
        qk_dec = sem("qk_dec")
        lt_ready = sem("lt_ready")
        as_ready = sem("as_ready")
        x_sb = sem("x_sb")
        t_ready = sem("t_ready")
        kbe_ready = sem("kbe_ready")
        tokens_ready = sem("tokens_ready")
        w_ready = sem("w_ready")
        vn_ready = sem("vn_ready")
        state_ready = sem("state_ready")
        od_ready = sem("od_ready")
        on_sq = sem("on_sq")
        on_root = sem("on_root")
        dn_done = sem("dn_done")
        raw2 = sem("raw2")
        rot_done = sem("rot_done")
        vs_ready = sem("vs_ready")
        relu_ready = sem("relu_ready")
        relu_used = sem("relu_used")
        max2 = sem("max2")
        exp2 = sem("exp2")
        p2 = sem("p2")
        pt2 = sem("pt2")
        sa_ready = sem("sa_ready")
        mix_ready = sem("mix_ready")
        mean_ready = sem("mean_ready")
        cent_ready = sem("cent_ready")
        ln_sq = sem("ln_sq")
        ln_root = sem("ln_root")
        ln_done = sem("ln_done")
        rt_args = sem("rt_args")
        rt_exp = sem("rt_exp")
        comb_ready = sem("comb_ready")
        htok_ready = sem("htok_ready")
        steps_ready = sem("steps_ready")
        loop_full = [sem(f"loop_full{b}") for b in range(BANKS)]
        loop_free = [sem(f"loop_free{b}") for b in range(BANKS)]
        sel_ready = sem("sel_ready")
        xg_ready = sem("xg_ready")
        esilu_ready = sem("esilu_ready")
        ehid_ready = sem("ehid_ready")
        ehidT_ready = sem("ehidT_ready")
        scatter_ready = sem("scatter_ready")
        eout_ready = sem("eout_ready")
        group_done = sem("group_done")

        use = [0] * BANKS
        tiles = {}
        turn = [0]

        def take(*key, bank=None):
            if bank is None:
                bank = turn[0] % BANKS
                turn[0] += 1
            use[bank] += 1
            tiles[key] = (bank, use[bank])

        slot_loads = [0] * SLOTS
        chunks = {}
        chunk_order = []
        last_tile = [None] * SLOTS
        slot_turn = [0]

        def chunk(key, parts, last, slot=None):
            if slot is None:
                slot = slot_turn[0] % SLOTS
                slot_turn[0] += 1
            slot_loads[slot] += 16 * len(parts)
            chunks[key] = (slot, slot_loads[slot])
            chunk_order.append((slot, parts, last_tile[slot]))
            last_tile[slot] = last

        def items(kind):
            return {"A": 16, "B": 8, "X": 4}[kind]

        def attention_order(kind):
            n = items(kind)
            order = [("S", 0), ("S", 1)]
            for m in range(n):
                order.append(("T", m))
                if m + 2 < n:
                    order.append(("S", m + 2))
                order.append(("V", m))
            return order

        def score_tiles(kind):
            return 2 if kind == "B" else 1

        def plan_attention(l, kind):
            for what, m in attention_order(kind):
                if what == "S":
                    for c in range(score_tiles(kind)):
                        take("S", l, kind, m, c)
                elif what == "T":
                    take("T", l, kind, m)
                elif kind != "A" or m % 2 == 0:
                    take("V", l, kind, m)

        def rotary_order():
            order = []
            for g in range(8):
                order.append(("qk", g))
                if g:
                    order.append(("rot", g - 1))
            return order + [("rot", 7)]

        def cols(w, a, b):
            return w[:, a:b].rearrange("(k p) n -> p k n", p=P)

        for c in range(4):
            take("xT", c)
        for c in range(4):
            take("memT", c)
        take("gT")
        take("norm", 0)
        for l in range(DEPTH):
            kind = "AB"[l]
            w_in = A["a_w_in"][0] if l == 0 else A["b_w_in"][0]
            w_out = A["a_w_out"][0] if l == 0 else A["b_w_out"][0]
            n0 = 1 + 6 * l
            take("norm", n0)
            for what, g in rotary_order():
                take(what, l, g)
            for c in range(2):
                for t in range(2):
                    take("v", l, c, t)
            for c in range(4):
                chunk(("qk", l, c), [(0, 8, 512, cols(w_in, 512 * c, 512 * c + 512))], ("qk", l, 2 * c + 1))
            for c in range(2):
                chunk(("v", l, c), [(0, 8, 512, cols(w_in, 2048 + 512 * c, 2560 + 512 * c))], ("v", l, c, 1))
            plan_attention(l, kind)
            if kind == "B":
                for c in range(4):
                    take("sub", c)
            for g in range(4):
                take("o", l, g)
            for c in range(2):
                chunk(("o", l, c), [(0, 8, 512, cols(w_out, 512 * c, 512 * c + 512))], ("o", l, 2 * c + 1))
            take("norm", n0 + 1)
            wkv = A["x_wkv"][l]
            for g in range(4):
                take("mk", l, g)
            for c in range(2):
                chunk(("mk", l, c), [(0, 8, 512, cols(wkv, 512 * c, 512 * c + 512))], ("mk", l, 2 * c + 1))
            for c in range(2):
                for t in range(2):
                    take("mv", l, c, t)
                chunk(("mv", l, c), [(0, 8, 512, cols(wkv, 1024 + 512 * c, 1536 + 512 * c))], ("mv", l, c, 1))
            take("norm", n0 + 2)
            for g in range(4):
                take("xq", l, g)
            for c in range(2):
                chunk(("xq", l, c), [(0, 8, 512, cols(A["x_wq"][l], 512 * c, 512 * c + 512))], ("xq", l, 2 * c + 1))
            plan_attention(l, "X")
            for g in range(4):
                take("xo", l, g)
            for c in range(2):
                chunk(("xo", l, c), [(0, 8, 512, cols(A["x_wo"][l], 512 * c, 512 * c + 512))], ("xo", l, 2 * c + 1))
            take("norm", n0 + 3)
            take("norm", n0 + 4)
            gu = A["w_gate_up"][l]
            for c in range(11):
                take("g", l, c)
                take("u", l, c)
                chunk(("gu", l, c), [(0, 8, 256, cols(gu, 256 * c, 256 * c + 256)),
                                     (2048, 8, 256, cols(gu, DFF + 256 * c, DFF + 256 * c + 256))], ("u", l, c))
            wd = A["w_down"][l]
            for g in range(4):
                take("d", l, g)
                chunk(("d", l, g, 0), [(0, 16, 256, cols(wd[0:2048], 256 * g, 256 * g + 256))], ("d", l, g))
                chunk(("d", l, g, 1), [(0, 6, 256, cols(wd[2048:DFF], 256 * g, 256 * g + 256))], ("d", l, g))
            take("norm", n0 + 5)

        take("metaT")
        chunk_order.append(("second", None, None))
        PROJ = [("dq", 0), ("dk", 4), ("dv", 8), ("dz", 12)]
        ROT = [("sq", 4), ("sk", 4), ("iq", 4), ("ik", 1)]
        LV = [7, 7, 4]
        units = [(n, h) for n in range(3) for h in range(SH)]
        loop_entry = {}
        expert_s = {}
        LB = dict(gather=(0, 1), up=2, hidT=3, scatter=4, down=(5, 6), out=(7, 0, 1, 2, 7, 0, 1, 2))
        L_USES = [3, 3, 3, 1, 1, 1, 1, 2]
        L_OUT = [1, 2, 2, 2, 2, 3, 3, 3]
        as_at, t_at, x_at = [{}, {}], [{}, {}], [{}, {}]

        def unit_order():
            order = [("S", 0), ("S", 1)]
            for m in range(len(units)):
                order.append(("T", m))
                if m + 2 < len(units):
                    order.append(("S", m + 2))
                order.append(("V", m))
            return order

        def rot_tiles():
            names = [(nm, i) for nm, cnt in ROT for i in range(cnt)]
            order = []
            for j, key in enumerate(names):
                order.append(("proj",) + key + (j,))
                if j:
                    order.append(("rot2",) + names[j - 1] + (j - 1,))
            return order + [("rot2",) + names[-1] + (len(names) - 1,)]

        for l in range(DEPTH):
            w2in = A["w_in_2"][l]
            take("sm", l)
            for nm, at in PROJ:
                for i in range(4):
                    take("c", l, at + i)
                chunk((nm, l), [(0, 8, 512, cols(w2in, SPLIT[nm], SPLIT[nm] + 512))], ("c", l, at + 3),
                      slot=PROJ.index((nm, at)))
            for what, nm, i, j in rot_tiles():
                take(what, l, nm, i)
            for s_, nm in enumerate(("sq", "sk", "iq")):
                chunk((nm, l), [(0, 8, 512, cols(w2in, SPLIT[nm], SPLIT[nm] + 512))], ("proj", l, nm, 3), slot=s_)
            chunk(("sv", l), [(0, 8, 512, cols(w2in, SPLIT["sv"], SPLIT["sv"] + 512))], ("sv", l, 2), slot=3)
            for n in range(3):
                take("sv", l, n)
            for i in range(8):
                take("l2", l, i)
            take("gcc", l)
            for n in range(3):
                take("gcb", l, n)
                take("bb", l, n)
                take("KK", l, n)
                take("KQ", l, n)
                take("kt", l, n)
                take("vt", l, n)
            for lv in range(7):
                for n in range(3):
                    if lv < LV[n]:
                        as_at[l][(lv, n)] = t_at[l][(lv, n)] = sum(LV) * l + len(as_at[l]) + 1
                        if lv:
                            x_at[l][(lv, n)] = (sum(LV) - 3) * l + len(x_at[l]) + 1
                        take("X", l, lv, n)
                if lv:
                    for n in range(3):
                        if lv < LV[n]:
                            take("Y", l, lv, n)
                            take("Z", l, lv, n)
            for n in range(3):
                take("W", l, n)
            for n in range(3):
                take("vn", l, n)
                take("od", l, n)
                if n < 2:
                    take("su", l, n)
            for h in range(DH):
                take("on", l, h)
            for n in range(3):
                for h in range(SH):
                    take("ix", l, n, h)
            for what, m in unit_order():
                if what != "V" or m % 2 == 0:
                    take("a" + what, l, m)
            for c in range(2):
                for i in range(4):
                    take("wo", l, 4 * c + i)
                chunk(("wo", l, c), [(0, 8, 512, cols(A["w_out_2"][l], 512 * c, 512 * c + 512))], ("wo", l, 4 * c + 3), slot=c)
            take("mu", l, 0)
            take("va", l, 0)
            take("rt", l)
            take("rk", l)
            for n in range(3):
                for c in range(2):
                    take("ht", l, n, c)
            expert_s[l] = list(slot_loads)
            loop_entry[l] = list(use)
            chunk_order.append(("experts", l, list(last_tile)))
            for s_ in range(SLOTS):
                slot_loads[s_] += 8 * (16 if s_ >= 4 else 32)
                last_tile[s_] = ("mu", l, 1)
            take("mu", l, 1)
            take("va", l, 1)
        for t in range(2):
            for c in range(2):
                take("outT", t, c)

        block = ctx.enter_context(nc.Block())

        @block.sync
        def _(sp):
            sp.dma_start(tab1[:, :], A["tables1"]).then_inc(const_in, 16)
            sp.dma_start(xin, A["x"][0].rearrange("(t p) n -> p t n", p=P)).then_inc(x_in, 16)
            sp.dma_start(memin, A["mem"][0].rearrange("(t p) n -> p t n", p=P)).then_inc(mem_in, 16)
            for n, name in enumerate(("mix_pre_g", "mix_post_g", "mem_pre_g", "mem_kv_g", "mem_post_g",
                                      "ffn_pre_g", "ffn_post_g")):
                sp.dma_start(grows[16 * n:16 * n + 16, 0, :],
                             A[name].rearrange("l (k p) -> (l k) p", p=P)).then_inc(const_in, 16)
            sp.dma_start(grows[112:113, 0, :], A["b_sub_g"]).then_inc(const_in, 16)
            for l in range(DEPTH):
                sp.dma_start(grows[0:48, 1 + l, :],
                             A["conv_w_2"][l].rearrange("w (t p) -> (w t) p", p=P)).then_inc(const_in, 16)
                sp.dma_start(grows[48:49, 1 + l, :], A["dn_norm_g_2"][l:l + 1]).then_inc(const_in, 16)
                for n, name in enumerate(("ln1_g_2", "ln1_b_2", "ln2_g_2", "ln2_b_2")):
                    sp.dma_start(grows[49 + 8 * n:57 + 8 * n, 1 + l, :],
                                 A[name][l].rearrange("(k p) -> k p", p=P)).then_inc(const_in, 16)
            sp.dma_start(pos_i[:, :], A["positions"][0:1, :].to_broadcast([P, S1])).then_inc(const_in, 16)
            for n, name in enumerate(("b_lam_q1", "b_lam_k1", "b_lam_q2", "b_lam_k2")):
                sp.dma_start(lamv[:, n, :], A[name].to_broadcast([P, HD])).then_inc(const_in, 16)
            def narrow_weights(l):
                w = A["w_in_2"][l]
                for at, c0, n in ((0, SPLIT["ik"], 64), (64, SPLIT["ik"], 72), (136, SPLIT["db"], 8)):
                    sp.dma_start(small_w[:, :, at:at + n], cols(w, c0, c0 + n)).then_inc(small_in, 16)
                sp.dma_start(router_w[:, :, 0:4], cols(A["w_grp_2"][l], 0, 4)).then_inc(router_in, 16)
                sp.dma_start(router_w[:, :, 4:36], cols(A["w_rtr_2"][l], 0, NE)).then_inc(router_in, 16)
            for slot, parts, last, *more in chunk_order:
                if slot == "second":
                    b, u = tiles[("xo", 1, 3)]
                    sp.wait_ge(full[b], u)
                    sp.dma_start(tab2[:, :], A["tables2"]).then_inc(const2_in[0], 16)
                    for l in range(DEPTH):
                        for at, name, n in ((0, "b_grp_2", 4), (4, "b_rtr_2", NE), (36, "a_log_2", 4), (40, "dt_bias_2", 4)):
                            sp.dma_start(rows2[:, l, at:at + n], A[name][l:l + 1, :].to_broadcast([P, n])).then_inc(const2_in[0], 16)
                    sp.dma_start(meta_rows, A["meta_tokens_2"]).then_inc(meta_in, 16)
                    narrow_weights(0)
                    continue
                if slot == "experts":
                    l, before = parts, last

                    def expert_loads(g):
                        for s_ in range(SLOTS):
                            if s_ < 4:
                                for at, name in ((0, "w1_2"), (2048, "w3_2")):
                                    src = A[name][l, bass.ds(g * 4 + s_, 1)].rearrange("o (k p) n -> p (o k) n", p=P)
                                    sp.dma_start(ring[:, s_, at:at + 2048].rearrange("p (k n) -> p k n", k=KT), src)\
                                        .then_inc(loaded[s_], 16)
                            else:
                                src = A["w2_2"][l, bass.ds(g * 4 + 2 * (s_ - 4), 2)].rearrange("e (k p) n -> p (e k) n", p=P)
                                sp.dma_start(ring[:, s_, :].rearrange("p (k n) -> p k n", k=4), src).then_inc(loaded[s_], 16)
                            yield s_
                    for s_ in range(4):
                        b, u = tiles[before[s_]]
                        sp.wait_ge(full[b], u)
                    b, u = tiles[("wo", l, 7)]
                    sp.wait_ge(full[b], u)
                    for _ in expert_loads(0):
                        pass
                    sp.wait_ge(steps_ready, l + 1)
                    with nc.sync.Fori(1, 8) as g:
                        end = sp.value_load(steps[0:1, l, bass.ds(g, 1)], min_val=1, max_val=1000)
                        sp.wait_ge(ehid_ready, end)
                        for s_ in expert_loads(g):
                            if s_ == 3:
                                sp.wait_ge(loop_full[LB["down"][1]], end)
                    if l == 0:
                        b, u = tiles[("rt", 0)]
                        sp.wait_ge(full[b], u)
                        narrow_weights(1)
                    continue
                if last is not None:
                    b, u = tiles[last]
                    sp.wait_ge(full[b], u)
                for at, k, width, src in parts:
                    sp.dma_start(ring[:, slot, at:at + k * width].rearrange("p (k n) -> p k n", k=k),
                                 src).then_inc(loaded[slot], 16)

            for t in range(2):
                sp.wait_ge(out_sb, 2 * t + 2)
                sp.dma_start(out[0, P * t:P * t + P, :], uT_flat[:, t, :]).then_inc(stored, 16)
            sp.wait_ge(stored, 32)

        @block.tensor
        def _(pe):
            def begin(*key):
                b, u = tiles[key]
                if u > 1:
                    pe.wait_ge(free[b], u - 1)
                return b

            def weights(*key):
                s, n = chunks[key]
                pe.wait_ge(loaded[s], n)
                return s

            def project(key, slot, at, step, src, ks, width=S1, two=2):
                b = begin(*key)
                for nt in range(two):
                    for k in range(ks):
                        last = nc.tensor.matmul(ps[:, b, nt * width:(nt + 1) * width],
                                                ring[:, slot, at + k * step + nt * P:at + k * step + nt * P + P],
                                                src(k), start=(k == 0), stop=(k == ks - 1))
                last.then_inc(full[b], 1)

            def project_tok(key, slot, src, t0, tn):
                b = begin(*key)
                for k in range(KT):
                    last = nc.tensor.matmul(ps[0:tn, b, :], src[:, k, t0:t0 + tn],
                                            ring[:, slot, k * 512:k * 512 + 512], start=(k == 0), stop=(k == KT - 1))
                last.then_inc(full[b], 1)

            def sum_squares(n, sem_, base, groups, width):
                b = begin("norm", n)
                for k in range(KT):
                    if k % (KT // groups) == 0:
                        pe.wait_ge(sem_, base + k // (KT // groups) + 1)
                    last = nc.tensor.matmul(ps[:, b, 0:width], ones[:, :], sq[:, k, 0:width],
                                            start=(k == 0), stop=(k == KT - 1))
                last.then_inc(full[b], 1)

            def attention(l, kind):
                base_s = {"A": 0, "B": 20, "X": 16 if l == 0 else 28}[kind]
                for what, m in attention_order(kind):
                    if what == "S":
                        for c in range(score_tiles(kind)):
                            b = begin("S", l, kind, m, c)
                            for j in range(2):
                                o = ps[:, b, j * S1:(j + 1) * S1]
                                if kind == "X":
                                    for a in range(2):
                                        last = nc.tensor.matmul(o, qT[:, 2 * m + a, j * P:(j + 1) * P],
                                                                kT[:, 2 * m + a, :], start=(a == 0), stop=(a == 1))
                                else:
                                    ft, p0 = (m // 2, HD * (m % 2)) if kind == "A" else (m, HD * c)
                                    last = nc.tensor.matmul(o, qT[p0:p0 + HD, ft, j * P:(j + 1) * P],
                                                            kT[p0:p0 + HD, ft, :], start=True, stop=True)
                            last.then_inc(full[b], 1)
                    elif what == "T":
                        pe.wait_ge(p_ready, base_s + m + 1)
                        b = begin("T", l, kind, m)
                        for j in range(2):
                            for kt in range(2):
                                last = nc.tensor.transpose(ps[:, b, kt * S1 + j * P:kt * S1 + (j + 1) * P],
                                                           probs[:, m % 3, 0, j * S1 + kt * P:j * S1 + (kt + 1) * P],
                                                           ident)
                        last.then_inc(full[b], 1)
                    else:
                        pe.wait_ge(pt_ready, base_s + m + 1)
                        pT = probsT[:, m % 2, :]
                        if kind == "A":
                            p0 = HD * (m % 2)
                            b = begin("V", l, kind, m) if m % 2 == 0 else tiles[("V", l, kind, m - 1)][0]
                            for kt in range(2):
                                last = nc.tensor.matmul(ps[p0:p0 + HD, b, 0:S1], vt[:, kt, HD * m:HD * m + HD],
                                                        pT[:, kt * S1:(kt + 1) * S1], start=(kt == 0), stop=(kt == 1))
                            if m % 2:
                                last.then_inc(full[b], 1)
                        else:
                            b = begin("V", l, kind, m)
                            nv = 1 if kind == "B" else 2
                            for nt in range(nv):
                                for kt in range(2):
                                    v0 = P * (nv * m + nt)
                                    last = nc.tensor.matmul(ps[:, b, nt * S1:(nt + 1) * S1], vt[:, kt, v0:v0 + P],
                                                            pT[:, kt * S1:(kt + 1) * S1], start=(kt == 0), stop=(kt == 1))
                            last.then_inc(full[b], 1)

            pe.wait_ge(const_in, 16 * CONSTS)
            for name, src, arrived in (("xT", xin, x_in), ("memT", memin, mem_in)):
                pe.wait_ge(arrived, 16)
                for c in range(4):
                    b = begin(name, c)
                    for a in range(2):
                        for t in range(2):
                            last = nc.tensor.transpose(ps[:, b, a * S1 + t * P:a * S1 + (t + 1) * P],
                                                       src[:, t, (2 * c + a) * P:(2 * c + a + 1) * P], ident)
                    last.then_inc(full[b], 1)
            b = begin("gT")
            nc.tensor.transpose(ps[:, b, 0:113], grows[0:113, 0, :], ident[0:113, 0:113])
            for l in range(DEPTH):
                last = nc.tensor.transpose(ps[:, b, 113 + 81 * l:194 + 81 * l], grows[0:81, 1 + l, :], ident[0:81, 0:81])
            last.then_inc(full[b], 1)
            pe.wait_ge(memset_done, 1)
            sum_squares(0, pre_sq, 0, 2, S1)

            u_of = lambda k: uT[:, k, 0:S1]
            for l in range(DEPTH):
                kind = "AB"[l]
                n0 = 1 + 6 * l
                p0 = 1 + 3 * l

                def u_tiles(p):
                    seen = set()

                    def src(k):
                        if k not in seen:
                            seen.add(k)
                            pe.wait_ge(u_ready, 8 * p + k + 1)
                        return uT[:, k, 0:S1]
                    return src

                sum_squares(n0, pre_sq, 2 * p0, 2, S1)
                src = u_tiles(p0 - 1)
                for what, g in rotary_order():
                    if what == "qk":
                        s = weights("qk", l, g // 2)
                        project(("qk", l, g), s, 256 * (g % 2), 512, src, KT)
                    else:
                        pe.wait_ge(q_raw, 8 * l + g + 1)
                        b = begin("rot", l, g)
                        qk = (qT if g < 4 else kT)[:, 2 * (g % 4):2 * (g % 4) + 2, :].rearrange("p a t -> p (a t)")
                        nc.tensor.matmul(ps[:, b, :], rot1, qk, start=True, stop=True).then_inc(full[b], 1)
                for c in range(2):
                    s = weights("v", l, c)
                    for t in range(2):
                        project_tok(("v", l, c, t), s, uT, t * P, P)
                pe.wait_ge(qk_ready, 8 * l + 8)
                pe.wait_ge(v_ready, 8 * l + 4)
                attention(l, kind)
                if kind == "B":
                    pe.wait_ge(sub_sq, 1)
                    for c in range(4):
                        b = begin("sub", c)
                        nc.tensor.matmul(ps[:, b, :].rearrange("p (a t) -> p a t", a=2), ones[:, :],
                                         sq[:, 2 * c:2 * c + 2, 0:S1], start=True, stop=True).then_inc(full[b], 1)
                    pe.wait_ge(sub_done, 1)
                o_src = lambda k: oT[:, k, 0:S1]
                if kind == "A":
                    pe.wait_ge(o_ready, 8)
                for g in range(4):
                    s = weights("o", l, g // 2)
                    project(("o", l, g), s, 256 * (g % 2), 512, o_src, KT)
                sum_squares(n0 + 1, post_sq, 4 * (3 * l), 4, S1)
                pe.wait_ge(mem_u, l + 1)
                for g in range(4):
                    s = weights("mk", l, g // 2)
                    project(("mk", l, g), s, 256 * (g % 2), 512, u_of, KT)
                for c in range(2):
                    s = weights("mv", l, c)
                    for t in range(2):
                        project_tok(("mv", l, c, t), s, uT, t * P, P)
                sum_squares(n0 + 2, pre_sq, 2 * (p0 + 1), 2, S1)
                src = u_tiles(p0)
                for g in range(4):
                    s = weights("xq", l, g // 2)
                    project(("xq", l, g), s, 256 * (g % 2), 512, src, KT)
                pe.wait_ge(xqk_raw, 8 * l + 8)
                pe.wait_ge(v_ready, 8 * l + 8)
                attention(l, "X")
                pe.wait_ge(o_ready, O_DONE[(l, "X")])
                for g in range(4):
                    s = weights("xo", l, g // 2)
                    project(("xo", l, g), s, 256 * (g % 2), 512, o_src, KT)
                sum_squares(n0 + 3, post_sq, 4 * (3 * l + 1), 4, S1)
                sum_squares(n0 + 4, pre_sq, 2 * (p0 + 2), 2, S1)
                src = u_tiles(p0 + 1)
                for c in range(11):
                    s = weights("gu", l, c)
                    project(("g", l, c), s, 0, 256, src, KT)
                    project(("u", l, c), s, 2048, 256, src, KT)
                for g in range(4):
                    s = weights("d", l, g, 0)
                    s1 = weights("d", l, g, 1)
                    b = begin("d", l, g)
                    for nt in range(2):
                        for k in range(FT):
                            if g == 0 and nt == 0 and k % 2 == 0:
                                pe.wait_ge(hid_ready, 11 * l + k // 2 + 1)
                            sl, kk = (s, k) if k < 16 else (s1, k - 16)
                            last = nc.tensor.matmul(ps[:, b, nt * S1:(nt + 1) * S1],
                                                    ring[:, sl, kk * 256 + nt * P:kk * 256 + nt * P + P],
                                                    hid[:, k, :], start=(k == 0), stop=(k == FT - 1))
                    last.then_inc(full[b], 1)
                sum_squares(n0 + 5, post_sq, 4 * (3 * l + 2), 4, S1)
            pe.wait_ge(const2_in[0], 16 * 9)
            pe.wait_ge(meta_in, 16)
            b = begin("metaT")
            for k in range(KT):
                last = nc.tensor.transpose(ps[:, b, 16 * k:16 * k + 16], meta_rows[:, k * P:(k + 1) * P], ident[0:16, 0:16])
            last.then_inc(full[b], 1)

            def project2(key, slot, at, step, dst_n=S2):
                b = begin(*key)
                for k in range(KT):
                    last = nc.tensor.matmul(ps[:, b, 0:S2], ring[:, slot, at + k * step:at + k * step + P], hT[:, k, :],
                                            start=(k == 0), stop=(k == KT - 1))
                last.then_inc(full[b], 1)

            def each_head(key, fn):
                b = begin(*key)
                for h in range(DH):
                    last = fn(b, h)
                last.then_inc(full[b], 1)

            def sum_features(key, src, arrived, base):
                b = begin(*key)
                for k in range(KT):
                    if arrived is not None and k % 4 == 0:
                        pe.wait_ge(arrived, base + k // 4 + 1)
                    last = nc.tensor.matmul(ps[:, b, 0:S2], ones[:, :], src[:, k, :], start=(k == 0), stop=(k == KT - 1))
                last.then_inc(full[b], 1)

            for l in range(DEPTH):
                if l == 0:
                    pe.wait_ge(h_ready, 6)
                    pe.wait_ge(meta_ready, 1)
                else:
                    pe.wait_ge(ln_done, 2)
                pe.wait_ge(small_in, 48 * (l + 1))
                b = begin("sm", l)
                for n, (t0, L) in enumerate(TOK):
                    for k in range(KT):
                        last = nc.tensor.matmul(ps[0:L, b, 16 * n:16 * n + 16], hT[:, k, t0:t0 + L], small_w[:, k, 128:144],
                                                start=(k == 0), stop=(k == KT - 1))
                last.then_inc(full[b], 1)
                for nm, at in PROJ:
                    s = weights(nm, l)
                    for i in range(4):
                        project2(("c", l, at + i), s, i * P, 512)
                for what, nm, i, j in rot_tiles():
                    if what == "proj":
                        if nm == "ik":
                            b = begin("proj", l, nm, i)
                            for k in range(KT):
                                last = nc.tensor.matmul(ps[:, b, 0:S2], small_w[:, k, 0:P], hT[:, k, :], start=(k == 0), stop=(k == KT - 1))
                            last.then_inc(full[b], 1)
                        else:
                            project2(("proj", l, nm, i), weights(nm, l), i * P, 512)
                    else:
                        pe.wait_ge(raw2, 13 * l + j + 1)
                        b = begin("rot2", l, nm, i)
                        nc.tensor.matmul(ps[:, b, 0:S2], rot2, dict(sq=qs, sk=ks, iq=iq, ik=ik)[nm][:, i, :],
                                         start=True, stop=True).then_inc(full[b], 1)
                s = weights("sv", l)
                for n, (t0, L) in enumerate(TOK):
                    project_tok(("sv", l, n), s, hT, t0, L)
                for i in range(8):
                    pe.wait_ge(l2_sq, 8 * l + i + 1)
                    b = begin("l2", l, i)
                    nc.tensor.matmul(ps[:, b, 0:S2], ones[:, :], sq[:, i, :], start=True, stop=True).then_inc(full[b], 1)
                pe.wait_ge(gb_ready, l + 1)
                b = begin("gcc", l)
                for n, (t0, L) in enumerate(TOK):
                    last = nc.tensor.matmul(ps[0:L, b, 4 * n:4 * n + 4], triu[0:L, 0:L], g_tok[0:L, n, :], start=True, stop=True)
                last.then_inc(full[b], 1)
                pe.wait_ge(conv_out, 12 * l + 12)
                pe.wait_ge(qk_unit, 8 * l + 8)
                for n, (t0, L) in enumerate(TOK):
                    each_head(("gcb", l, n), lambda b, h: nc.tensor.matmul(
                        ps[:, b, h * P:h * P + L], g_tok[0:L, n, h:h + 1].broadcast_to([L, P]), triu[0:L, 0:L], start=True, stop=True))
                    each_head(("bb", l, n), lambda b, h: nc.tensor.matmul(
                        ps[:, b, h * P:h * P + L], beta[0:L, n, h:h + 1].broadcast_to([L, P]), ident[0:L, 0:L], start=True, stop=True))
                    each_head(("KK", l, n), lambda b, h: nc.tensor.matmul(
                        ps[0:L, b, h * P:h * P + L], cv_qk[:, 4 + h, t0:t0 + L], cv_qk[:, 4 + h, t0:t0 + L], start=True, stop=True))
                    each_head(("KQ", l, n), lambda b, h: nc.tensor.matmul(
                        ps[0:L, b, h * P:h * P + L], cv_qk[:, 4 + h, t0:t0 + L], cv_qk[:, h, t0:t0 + L], start=True, stop=True))
                    each_head(("kt", l, n), lambda b, h: nc.tensor.transpose(
                        ps[0:L, b, h * P:(h + 1) * P], cv_qk[:, 4 + h, t0:t0 + L], ident))
                    each_head(("vt", l, n), lambda b, h: nc.tensor.transpose(
                        ps[0:L, b, h * P:(h + 1) * P], cv_v[:, h, t0:t0 + L], ident))
                asn, tn, xn = as_at[l], t_at[l], x_at[l]
                for lv in range(7):
                    live = [n for n in range(3) if lv < LV[n]]
                    for n in live:
                        L = TOK[n][1]
                        pe.wait_ge(as_ready, asn[(lv, n)])
                        if lv:
                            pe.wait_ge(t_ready, tn[(lv - 1, n)])
                        each_head(("X", l, lv, n), lambda b, h: nc.tensor.matmul(
                            ps[0:L, b, h * P:h * P + L], As[0:L, n, h * P:h * P + L],
                            ident[0:L, 0:L] if lv == 0 else Tm[0:L, n, h * P:h * P + L], start=True, stop=True))
                    if lv:
                        for n in live:
                            L = TOK[n][1]
                            pe.wait_ge(x_sb, xn[(lv, n)])
                            each_head(("Y", l, lv, n), lambda b, h: nc.tensor.matmul(
                                ps[0:L, b, h * P:h * P + L], TT[0:L, n, h * P:h * P + L], Xs[0:L, n, h * P:h * P + L], start=True, stop=True))
                            each_head(("Z", l, lv, n), lambda b, h: nc.tensor.matmul(
                                ps[0:L, b, h * P:h * P + L], Xs[0:L, n, h * P:h * P + L], TT[0:L, n, h * P:h * P + L], start=True, stop=True))
                pe.wait_ge(t_ready, sum(LV) * (l + 1))
                for n, (t0, L) in enumerate(TOK):
                    pe.wait_ge(kbe_ready, 3 * l + n + 1)
                    each_head(("W", l, n), lambda b, h: nc.tensor.matmul(
                        ps[:, b, h * P:h * P + L], k_be[0:L, n, h * P:(h + 1) * P], TT[0:L, n, h * P:h * P + L], start=True, stop=True))
                pe.wait_ge(tokens_ready, l + 1)
                for n, (t0, L) in enumerate(TOK):
                    if n:
                        pe.wait_ge(w_ready, 3 * l + n + 1)
                        pe.wait_ge(state_ready, 2 * l + n)

                    def new_values(b, h):
                        o = ps[0:L, b, h * P:(h + 1) * P]
                        last = nc.tensor.matmul(o, TT[0:L, n, h * P:h * P + L], v_beta[0:L, n, h * P:(h + 1) * P], start=True, stop=(n == 0))
                        if n:
                            last = nc.tensor.matmul(o, w_T[:, n, h * P:h * P + L], state[:, h * P:(h + 1) * P], start=False, stop=True)
                        return last
                    each_head(("vn", l, n), new_values)
                    pe.wait_ge(vn_ready, 3 * l + n + 1)

                    def outputs(b, h):
                        o = ps[:, b, h * P:h * P + L]
                        if n:
                            nc.tensor.matmul(o, state[:, h * P:(h + 1) * P], cv_qk[:, h, t0:t0 + L], start=True, stop=False)
                        return nc.tensor.matmul(o, v_new[0:L, h * P:(h + 1) * P], QK[0:L, n, h * P:h * P + L], start=(n == 0), stop=True)
                    each_head(("od", l, n), outputs)
                    if n < 2:
                        each_head(("su", l, n), lambda b, h: nc.tensor.matmul(
                            ps[:, b, h * P:(h + 1) * P], k_tok[0:L, n, h * P:(h + 1) * P], v_new[0:L, h * P:(h + 1) * P], start=True, stop=True))
                pe.wait_ge(on_sq, l + 1)
                for h in range(DH):
                    b = begin("on", l, h)
                    nc.tensor.matmul(ps[:, b, 0:S2], ones[:, :], sq[:, h, :], start=True, stop=True).then_inc(full[b], 1)
                pe.wait_ge(rot_done, 13 * l + 13)
                for n, (t0, L) in enumerate(TOK):
                    for h in range(SH):
                        p0 = HD * (h % 2)
                        b = begin("ix", l, n, h)
                        nc.tensor.matmul(ps[0:L, b, 0:S2], iq[p0:p0 + HD, h // 2, t0:t0 + L], ik[p0:p0 + HD, 0, :],
                                         start=True, stop=True).then_inc(full[b], 1)
                pe.wait_ge(vs_ready, 3 * l + 3)
                for what, m in unit_order():
                    n, h = units[m]
                    t0, L = TOK[n]
                    p0 = HD * (h % 2)
                    if what == "S":
                        b = begin("aS", l, m)
                        nc.tensor.matmul(ps[0:L, b, 0:t0 + L], qs[p0:p0 + HD, h // 2, t0:t0 + L], ks[p0:p0 + HD, h // 2, 0:t0 + L],
                                         start=True, stop=True).then_inc(full[b], 1)
                    elif what == "T":
                        pe.wait_ge(p2, 24 * l + m + 1)
                        b = begin("aT", l, m)
                        for kt in range(n + 1):
                            kl = TOK[kt][1]
                            last = nc.tensor.transpose(ps[0:kl, b, kt * P:kt * P + L], probs2[0:L, m % 3, kt * P:kt * P + kl], ident[0:L, 0:L])
                        last.then_inc(full[b], 1)
                    else:
                        pe.wait_ge(pt2, 24 * l + m + 1)
                        b = begin("aV", l, m) if m % 2 == 0 else tiles[("aV", l, m - 1)][0]
                        for kt in range(n + 1):
                            kl = TOK[kt][1]
                            last = nc.tensor.matmul(ps[p0:p0 + HD, b, 0:L], vs[0:kl, kt, HD * h:HD * h + HD], probsT2[0:kl, m % 2, kt, 0:L],
                                                    start=(kt == 0), stop=(kt == n))
                        if m % 2:
                            last.then_inc(full[b], 1)
                pe.wait_ge(dn_done, l + 1)
                pe.wait_ge(sa_ready, 12 * l + 12)
                for c in range(2):
                    s = weights("wo", l, c)
                    for i in range(4):
                        b = begin("wo", l, 4 * c + i)
                        for k in range(KT):
                            last = nc.tensor.matmul(ps[:, b, 0:S2], ring[:, s, k * 512 + i * P:k * 512 + i * P + P], oT[:, k, :],
                                                    start=(k == 0), stop=(k == KT - 1))
                        last.then_inc(full[b], 1)
                pe.wait_ge(mix_ready, 2 * l + 1)
                sum_features(("mu", l, 0), hT, None, 0)
                sum_features(("va", l, 0), sq, ln_sq, 4 * l)
                pe.wait_ge(ln_done, 2 * l + 1)
                pe.wait_ge(router_in, 32 * (l + 1))
                b = begin("rt", l)
                for n, (t0, L) in enumerate(TOK):
                    for k in range(KT):
                        last = nc.tensor.matmul(ps[0:L, b, 36 * n:36 * n + 36], hT[:, k, t0:t0 + L], router_w[:, k, :],
                                                start=(k == 0), stop=(k == KT - 1))
                last.then_inc(full[b], 1)
                for n, (t0, L) in enumerate(TOK):
                    for c in range(2):
                        if c == 0 and n == 0:
                            pe.wait_ge(comb_ready, l + 1)
                            b = begin("rk", l)
                            for a, (_, La) in enumerate(TOK):
                                for a1 in range(a + 1):
                                    last = nc.tensor.matmul(ps[0:La, b, a * NE:(a + 1) * NE], (strict if a1 == a else ones)[0:TOK[a1][1], 0:La],
                                                            chosen[0:TOK[a1][1], a1, :], start=(a1 == 0), stop=(a1 == a))
                            for a, (_, La) in enumerate(TOK):
                                last = nc.tensor.matmul(ps[:, b, 3 * NE:4 * NE], ones[0:La, :], chosen[0:La, a, :], start=(a == 0), stop=(a == 2))
                            last.then_inc(full[b], 1)
                        b = begin("ht", l, n, c)
                        for k in range(4):
                            last = nc.tensor.transpose(ps[0:L, b, k * P:(k + 1) * P], hT[:, 4 * c + k, t0:t0 + L], ident)
                        last.then_inc(full[b], 1)
                for b in range(BANKS):
                    pe.wait_ge(free[b], loop_entry[l][b])
                pe.wait_ge(steps_ready, l + 1)
                pe.wait_ge(htok_ready, 6 * (l + 1))
                with nc.tensor.Fori(0, 8) as g:
                    first_step = pe.value_load(steps[0:1, l, bass.ds(g, 1)], min_val=0, max_val=1000)
                    end_step = pe.value_load(steps[0:1, l, bass.ds(g + 1, 1)], min_val=1, max_val=1000)
                    with nc.tensor.Fori(first_step, end_step) as s:
                        def begin_l(b, nth):
                            pe.wait_ge(loop_free[b], s * L_USES[b] + nth)
                            return b

                        pe.wait_ge(sel_ready, s + 1)
                        for a in range(2):
                            b = begin_l(LB["gather"][a], 1)
                            for k in range(4):
                                for n, (t0, L) in enumerate(TOK):
                                    last = nc.tensor.matmul(ps[:, b, k * P:(k + 1) * P], h_tok[0:L, n, (4 * a + k) * P:(4 * a + k + 1) * P],
                                                            sel[0:L, n, :], start=(n == 0), stop=(n == 2))
                            last.then_inc(loop_full[b], 1)
                        b = begin_l(LB["scatter"], 1)
                        for n, (t0, L) in enumerate(TOK):
                            last = nc.tensor.transpose(ps[:, b, t0:t0 + L], sel_gate[0:L, n, :], ident[0:L, 0:L])
                        last.then_inc(loop_full[b], 1)
                        b = begin_l(LB["up"], 1)
                        for j in range(4):
                            pe.wait_ge(loaded[j], g * 32 + (expert_s[l][j] + 32))
                        for k in range(KT):
                            if k % 4 == 0:
                                pe.wait_ge(xg_ready, s * 2 + (k // 4 + 1))
                            for j in range(4):
                                last = nc.tensor.matmul(ps[32 * j:32 * j + 32, b, :].rearrange("p (a n) -> p a n", a=2),
                                                        x_g[:, k, 32 * j:32 * j + 32],
                                                        ring[:, j, :].rearrange("p (a k n) -> p k a n", a=2, k=KT)[:, k],
                                                        start=(k == 0), stop=(k == KT - 1))
                        last.then_inc(loop_full[b], 1)
                        pe.wait_ge(ehid_ready, s + 1)
                        b = begin_l(LB["hidT"], 1)
                        for f in range(2):
                            last = nc.tensor.transpose(ps[:, b, f * P:(f + 1) * P], e_hid[:, f * P:(f + 1) * P], ident)
                        last.then_inc(loop_full[b], 1)
                        for s_ in (4, 5):
                            pe.wait_ge(loaded[s_], g * 16 + (expert_s[l][s_] + 16))
                        pe.wait_ge(ehidT_ready, s + 1)
                        for a in range(2):
                            b = begin_l(LB["down"][a], 1)
                            for f in range(2):
                                for j in range(4):
                                    at = ((j % 2) * 2 + f) * DM + a * 512
                                    last = nc.tensor.matmul(ps[32 * j:32 * j + 32, b, :], e_hidT[:, f, 32 * j:32 * j + 32],
                                                            ring[:, 4 + j // 2, at:at + 512], start=(f == 0), stop=(f == 1))
                            last.then_inc(loop_full[b], 1)
                        pe.wait_ge(scatter_ready, s + 1)
                        for i in range(KT):
                            if i % 4 == 0:
                                pe.wait_ge(eout_ready, s * 2 + (i // 4 + 1))
                            b = begin_l(LB["out"][i], L_OUT[i])
                            nc.tensor.matmul(ps[:, b, 0:S2], e_out[:, i * P:(i + 1) * P], scatter[:, :], start=True, stop=True)\
                                .then_inc(loop_full[b], 1)
                pe.wait_ge(mix_ready, 2 * l + 2)
                sum_features(("mu", l, 1), yacc, None, 0)
                sum_features(("va", l, 1), sq, ln_sq, 4 * l + 2)
            pe.wait_ge(ln_done, 4)
            for t in range(2):
                for c in range(2):
                    b = begin("outT", t, c)
                    for a in range(4):
                        last = nc.tensor.transpose(ps[:, b, a * P:(a + 1) * P],
                                                   hx[:, 4 * c + a, t * P:(t + 1) * P], ident)
                    last.then_inc(full[b], 1)

        @block.scalar
        def _(act):
            def filled(*key):
                b, u = tiles[key]
                act.wait_ge(full[b], u)
                return b

            def squares_of(src, width, sem_):
                for a in range(2):
                    nc.scalar.activation(sq[:, 4 * a:4 * a + 4, 0:width], src[:, 4 * a:4 * a + 4, :],
                                         ACT.Square).then_inc(sem_, 1)

            def root(key, width, scale, eps, dst):
                b = filled(*key)
                nc.scalar.activation(dst, ps[:, b, 0:width], ACT.Sqrt, bias=eps, scale=scale).then_inc(free[b], 1)

            def norm_root(n):
                root(("norm", n), S1, 1.0 / DM, eps6[:, :], std[:, 0:S1])
                nc.scalar.drain().then_inc(std_ready, 1)

            def branch_out(name, l):
                for g in range(4):
                    b = filled(name, l, g)
                    y = ps[:, b, :].rearrange("p (a t) -> p a t", a=2)
                    nc.scalar.activation(yT[:, 2 * g:2 * g + 2, 0:S1], y, ACT.Copy)
                    nc.scalar.activation(sq[:, 2 * g:2 * g + 2, 0:S1], y, ACT.Square).then_inc(post_sq, 1)
                    nc.scalar.drain().then_inc(free[b], 1)

            def attention(l, kind):
                base = {"A": 0, "B": 20, "X": 16 if l == 0 else 28}[kind]
                scale = 1.0 / 16 if kind == "X" else 0.125
                n = items(kind)

                def exps(m):
                    act.wait_ge(max_ready, base + m + 1)
                    for c in range(score_tiles(kind)):
                        if kind != "A":
                            b = filled("S", l, kind, m, c)
                        for j in range(2):
                            p = probs[:, m % 3, c, j * S1:(j + 1) * S1]
                            src = p if kind == "A" else ps[:, b, j * S1:(j + 1) * S1]
                            nc.scalar.activation(p, src, ACT.Exp, bias=nmax[:, m % 3, c, j:j + 1], scale=scale,
                                                 accum_out=den[:, m % 3, c, j:j + 1])
                        if kind != "A":
                            nc.scalar.drain().then_inc(free[b], 1)
                    nc.scalar.drain().then_inc(exp_ready, 1)

                exps(0)
                exps(1)
                for m in range(n):
                    b = filled("T", l, kind, m)
                    nc.scalar.activation(probsT[:, m % 2, :], ps[:, b, :], ACT.Copy).then_inc(pt_ready, 1)
                    nc.scalar.drain().then_inc(free[b], 1)
                    if m + 2 < n:
                        exps(m + 2)

            act.wait_ge(memset_done, 2)
            for c in range(4):
                b = filled("xT", c)
                nc.scalar.activation(hx[:, 2 * c:2 * c + 2, :], ps[:, b, :].rearrange("p (a t) -> p a t", a=2),
                                     ACT.Copy).then_inc(x_ready, 1)
                nc.scalar.drain().then_inc(free[b], 1)
            for c in range(4):
                b = filled("memT", c)
                nc.scalar.activation(memn[:, 2 * c:2 * c + 2, :], ps[:, b, :].rearrange("p (a t) -> p a t", a=2),
                                     ACT.Copy)
                nc.scalar.drain().then_inc(free[b], 1)
            b = filled("gT")
            nc.scalar.activation(gains[:, :], ps[:, b, 0:275], ACT.Copy).then_inc(gain_cols, 1)
            nc.scalar.drain().then_inc(free[b], 1)
            squares_of(memn, S1, pre_sq)
            norm_root(0)
            act.wait_ge(rope_args, 1)
            nc.scalar.activation(rope[:, :, :], rope[:, :, :], ACT.Sin).then_inc(rope_ready, 1)
            act.wait_ge(lam_args, 1)
            nc.scalar.activation(lam_parts[:, 2:4], lam_parts[:, 0:2], ACT.Exp).then_inc(lam_exp, 1)
            for l in range(DEPTH):
                kind = "AB"[l]
                n0 = 1 + 6 * l
                if l:
                    act.wait_ge(h_ready, 3 * l)
                squares_of(hx, S1, pre_sq)
                if l == 0:
                    act.wait_ge(memn_ready, 1)
                norm_root(n0)
                for g in range(8):
                    b = filled("qk", l, g)
                    dst = (qT if g < 4 else kT)[:, 2 * (g % 4):2 * (g % 4) + 2, :].rearrange("p a t -> p (a t)")
                    nc.scalar.activation(dst, ps[:, b, :], ACT.Copy).then_inc(q_raw, 1)
                    nc.scalar.drain().then_inc(free[b], 1)
                for c in range(2):
                    for t in range(2):
                        b = filled("v", l, c, t)
                        nc.scalar.activation(vt[:, t, 512 * c:512 * c + 512], ps[:, b, :], ACT.Copy).then_inc(v_ready, 1)
                        nc.scalar.drain().then_inc(free[b], 1)
                attention(l, kind)
                if kind == "B":
                    act.wait_ge(o_ready, O_DONE[(l, kind)])
                    for a in range(2):
                        ins = nc.scalar.activation(sq[:, 4 * a:4 * a + 4, 0:S1], oT[:, 4 * a:4 * a + 4, 0:S1], ACT.Square)
                    ins.then_inc(sub_sq, 1)
                    for c in range(4):
                        b = filled("sub", c)
                        nc.scalar.activation(yT[:, 2 * c:2 * c + 2, 0:S1], ps[:, b, :].rearrange("p (a t) -> p a t", a=2),
                                             ACT.Sqrt, bias=eps6[:, :], scale=1.0 / P).then_inc(sub_std, 1)
                        nc.scalar.drain().then_inc(free[b], 1)
                branch_out("o", l)
                norm_root(n0 + 1)
                for g in range(4):
                    b = filled("mk", l, g)
                    dst = kT[:, 2 * g:2 * g + 2, :].rearrange("p a t -> p (a t)")
                    nc.scalar.activation(dst, ps[:, b, :], ACT.Copy).then_inc(xqk_raw, 1)
                    nc.scalar.drain().then_inc(free[b], 1)
                for c in range(2):
                    for t in range(2):
                        b = filled("mv", l, c, t)
                        nc.scalar.activation(vt[:, t, 512 * c:512 * c + 512], ps[:, b, :], ACT.Copy).then_inc(v_ready, 1)
                        nc.scalar.drain().then_inc(free[b], 1)
                act.wait_ge(h_ready, 3 * l + 1)
                squares_of(hx, S1, pre_sq)
                norm_root(n0 + 2)
                for g in range(4):
                    b = filled("xq", l, g)
                    dst = qT[:, 2 * g:2 * g + 2, :].rearrange("p a t -> p (a t)")
                    nc.scalar.activation(dst, ps[:, b, :], ACT.Copy).then_inc(xqk_raw, 1)
                    nc.scalar.drain().then_inc(free[b], 1)
                attention(l, "X")
                branch_out("xo", l)
                norm_root(n0 + 3)
                act.wait_ge(h_ready, 3 * l + 2)
                squares_of(hx, S1, pre_sq)
                norm_root(n0 + 4)
                for c in range(11):
                    b = filled("g", l, c)
                    nc.scalar.activation(hid[:, 2 * c:2 * c + 2, :], ps[:, b, :].rearrange("p (a t) -> p a t", a=2),
                                         ACT.Silu).then_inc(silu_ready, 1)
                    nc.scalar.drain().then_inc(free[b], 1)
                branch_out("d", l)
                norm_root(n0 + 5)
            b = filled("metaT")
            nc.scalar.activation(hT[:, :, 0:META], ps[:, b, 0:128].rearrange("p (k t) -> p k t", k=KT), ACT.Copy).then_inc(meta_ready, 1)
            nc.scalar.drain().then_inc(free[b], 1)
            act.wait_ge(zeros2, 1)

            def copy_out(key, dst, src, sem_, **kw):
                b = filled(*key)
                nc.scalar.activation(dst, src(b), ACT.Copy, **kw).then_inc(sem_, 1)
                nc.scalar.drain().then_inc(free[b], 1)

            def h4(b, L0, L1):
                return heads(ps[:, b, :])[0:L0, :, 0:L1]

            for l in range(DEPTH):
                b = filled("sm", l)
                nc.scalar.activation(tok[:, 0:2, :], ps[:, b, 0:32].rearrange("p (n c) -> p n c", n=2), ACT.Copy)
                nc.scalar.activation(tok[0:16, 2, :], ps[0:16, b, 32:48], ACT.Copy).then_inc(tok_ready, 1)
                nc.scalar.drain().then_inc(free[b], 1)
                for i in range(12):
                    copy_out(("c", l, i), conv_in[:, i, 3:3 + S2], lambda b: ps[:, b, 0:S2], conv_raw)
                for i in range(4):
                    b = filled("c", l, 12 + i)
                    nc.scalar.activation(z_gate[:, i, :], ps[:, b, 0:S2], ACT.Silu).then_inc(free[b], 1)
                for j, (what, nm, i, jj) in enumerate([t for t in rot_tiles() if t[0] == "proj"]):
                    copy_out(("proj", l, nm, i), dict(sq=qs, sk=ks, iq=iq, ik=ik)[nm][:, i, :], lambda b: ps[:, b, 0:S2], raw2)
                for n, (t0, L) in enumerate(TOK):
                    copy_out(("sv", l, n), vs[0:L, n, :], lambda b: ps[0:L, b, :], vs_ready)
                for i in range(12):
                    act.wait_ge(conv_acc, 12 * l + i + 1)
                    x = cv_qk[:, i, :] if i < 8 else cv_v[:, i - 8, :]
                    nc.scalar.activation(x, x, ACT.Silu).then_inc(conv_out, 1)
                    if i < 8:
                        nc.scalar.drain()
                        nc.scalar.activation(sq[:, i, :], x, ACT.Square).then_inc(l2_sq, 1)
                act.wait_ge(sp_args, l + 1)
                nc.scalar.activation(gate_exp[:, :, :], gate_log[:, :, :], ACT.Exp)
                nc.scalar.activation(neg_a[:, :], rows2[:, l, 36:40], ACT.Exp)
                nc.scalar.drain()
                nc.scalar.activation(gate_log[:, :, 0:4], gate_exp[:, :, 0:4], ACT.Ln, bias=1.0).then_inc(sp_logs, 1)
                for i in range(8):
                    b = filled("l2", l, i)
                    nc.scalar.activation(yT[:, i, :], ps[:, b, 0:S2], ACT.Sqrt, bias=(eps128 if i < 4 else eps6)[:, :],
                                         scale=128.0 if i < 4 else 1.0).then_inc(l2_root, 1)
                    nc.scalar.drain().then_inc(free[b], 1)
                for n, (t0, L) in enumerate(TOK):
                    act.wait_ge(decay_args, 3 * l + n + 1)
                    d = heads(decay)[0:L, :, 0:L]
                    nc.scalar.activation(d, d, ACT.Exp).then_inc(decay_ready, 1)
                    b = filled("gcb", l, n)
                    nc.scalar.activation(heads(egc)[:, :, 0:L], h4(b, P, L), ACT.Exp).then_inc(egc_ready, 1)
                    nc.scalar.drain().then_inc(free[b], 1)
                    act.wait_ge(qk_dec, 3 * l + n + 1)
                act.wait_ge(cum_ready, l + 1)
                nc.scalar.activation(ecum[:, :, :], cum[:, :, :], ACT.Exp).then_inc(ecum_ready, 1)
                for lv in range(1, 7):
                    for n in range(3):
                        if lv < LV[n]:
                            L = TOK[n][1]
                            copy_out(("X", l, lv, n), heads(Xs[:, n, :])[0:L, :, 0:L], lambda b: h4(b, L, L), x_sb)
                for n, (t0, L) in enumerate(TOK):
                    copy_out(("W", l, n), heads(w_T[:, n, :])[:, :, 0:L], lambda b: h4(b, P, L), w_ready, scale=-1.0)
                for n, (t0, L) in enumerate(TOK):
                    copy_out(("vn", l, n), heads(v_new)[0:L], lambda b: h4(b, L, P), vn_ready)
                    copy_out(("od", l, n), oT[:, 0:4, t0:t0 + L], lambda b: h4(b, P, L), od_ready)
                nc.scalar.activation(sq[:, 0:4, :], oT[:, 0:4, :], ACT.Square).then_inc(on_sq, 1)
                for h in range(DH):
                    b = filled("on", l, h)
                    nc.scalar.activation(yT[:, h, :], ps[:, b, 0:S2], ACT.Sqrt, bias=eps6[:, :], scale=1.0 / P).then_inc(on_root, 1)
                    nc.scalar.drain().then_inc(free[b], 1)
                for n, (t0, L) in enumerate(TOK):
                    for h in range(SH):
                        i = 24 * l + 8 * n + h
                        b = filled("ix", l, n, h)
                        if i >= 2:
                            act.wait_ge(relu_used, i - 1)
                        nc.scalar.activation(relu_s[0:L, h % 2, :], ps[0:L, b, 0:S2], ACT.Relu, scale=0.125).then_inc(relu_ready, 1)
                        nc.scalar.drain().then_inc(free[b], 1)

                def exp_unit(m):
                    n, h = units[m]
                    t0, L = TOK[n]
                    act.wait_ge(max2, 24 * l + m + 1)
                    p = probs2[0:L, m % 3, 0:t0 + L]
                    nc.scalar.activation(p, p, ACT.Exp, bias=stat2[0:L, 1, m % 3:m % 3 + 1], scale=0.125,
                                         accum_out=stat2[0:L, 2, m % 3:m % 3 + 1])
                    nc.scalar.drain().then_inc(exp2, 1)
                exp_unit(0)
                exp_unit(1)
                for m in range(24):
                    n, h = units[m]
                    L = TOK[n][1]
                    b = filled("aT", l, m)
                    full_tiles = min(n + 1, 2)
                    ins = nc.scalar.activation(probsT2[:, m % 2, 0:full_tiles, 0:L],
                                               ps[:, b, 0:full_tiles * P].rearrange("p (k t) -> p k t", k=full_tiles)[:, :, 0:L], ACT.Copy)
                    if n == 2:
                        ins = nc.scalar.activation(probsT2[0:16, m % 2, 2, 0:L], ps[0:16, b, 2 * P:2 * P + L], ACT.Copy)
                    ins.then_inc(pt2, 1)
                    nc.scalar.drain().then_inc(free[b], 1)
                    if m + 2 < 24:
                        exp_unit(m + 2)

                def layer_norm_act(j, src):
                    b = filled("mu", l, j)
                    nc.scalar.activation(std[:, :], ps[:, b, 0:S2], ACT.Copy, scale=1.0 / DM).then_inc(mean_ready, 1)
                    nc.scalar.drain().then_inc(free[b], 1)
                    act.wait_ge(cent_ready, 2 * l + j + 1)
                    for a in range(2):
                        nc.scalar.activation(sq[:, 4 * a:4 * a + 4, :], src[:, 4 * a:4 * a + 4, :], ACT.Square).then_inc(ln_sq, 1)
                    b = filled("va", l, j)
                    nc.scalar.activation(std[:, :], ps[:, b, 0:S2], ACT.Sqrt, bias=eps5[:, :], scale=1.0 / DM).then_inc(ln_root, 1)
                    nc.scalar.drain().then_inc(free[b], 1)
                layer_norm_act(0, hT)
                act.wait_ge(rt_args, l + 1)
                nc.scalar.activation(rexp[:, :, 0:5], rexp[:, :, 0:5], ACT.Exp).then_inc(rt_exp, 1)
                for n, (t0, L) in enumerate(TOK):
                    for c in range(2):
                        copy_out(("ht", l, n, c), h_tok[0:L, n, 512 * c:512 * c + 512], lambda b: ps[0:L, b, :], htok_ready)
                act.wait_ge(steps_ready, l + 1)
                with nc.scalar.Fori(0, 8) as g:
                    first_step = act.value_load(steps[0:1, l, bass.ds(g, 1)], min_val=0, max_val=1000)
                    end_step = act.value_load(steps[0:1, l, bass.ds(g + 1, 1)], min_val=1, max_val=1000)
                    with nc.scalar.Fori(first_step, end_step) as s:
                        def copy_l(b, nth, dst, src, sem_):
                            act.wait_ge(loop_full[b], s * L_USES[b] + nth)
                            nc.scalar.activation(dst, src, ACT.Copy).then_inc(sem_, 1)
                            nc.scalar.drain().then_inc(loop_free[b], 1)
                        for a in range(2):
                            b = LB["gather"][a]
                            copy_l(b, 1, x_g[:, 4 * a:4 * a + 4, :], ps[:, b, :].rearrange("p (k c) -> p k c", k=4), xg_ready)
                        b = LB["scatter"]
                        copy_l(b, 1, scatter[:, :], ps[:, b, 0:S2], scatter_ready)
                        b = LB["up"]
                        act.wait_ge(loop_full[b], s * L_USES[b] + 1)
                        nc.scalar.activation(e_silu[:, :], ps[:, b, 0:DE], ACT.Silu).then_inc(esilu_ready, 1)
                        b = LB["hidT"]
                        copy_l(b, 1, e_hidT[:, :, :], ps[:, b, 0:2 * P].rearrange("p (f c) -> p f c", f=2), ehidT_ready)
                        for a in range(2):
                            b = LB["down"][a]
                            copy_l(b, 1, e_out[:, 512 * a:512 * a + 512], ps[:, b, :], eout_ready)
                layer_norm_act(1, yacc)

            for t in range(2):
                for c in range(2):
                    b = filled("outT", t, c)
                    nc.scalar.activation(uT_flat[:, t, 512 * c:512 * c + 512], ps[:, b, :], ACT.Copy).then_inc(out_sb, 1)

        @block.gpsimd
        def _(pool):
            for l in range(DEPTH):
                if l == 0:
                    pool.wait_ge(const2_in[0], 16 * 9)
                for lv in range(7):
                    for n in range(3):
                        if lv >= LV[n]:
                            continue
                        L = TOK[n][1]
                        if lv == 0:
                            pool.wait_ge(lt_ready, 3 * l + n + 1)
                        else:
                            b, u = tiles[("X", l, lv - 1, n)]
                            pool.wait_ge(full[b], u)
                            if lv == 1:
                                pool.wait_ge(t_ready, t_at[l][(0, n)])
                        nc.gpsimd.tensor_tensor(heads(As[:, n, :])[0:L, :, 0:L], heads(LT[:, n, :])[0:L, :, 0:L],
                                                levels[0:L, lv, 0:L].unsqueeze(1).broadcast_to([L, DH, L]), ALU.mult).then_inc(as_ready, 1)

        @block.vector
        def _(dve):
            def settle():
                nc.vector.drain()

            def filled(*key):
                b, u = tiles[key]
                dve.wait_ge(full[b], u)
                return b

            def over(x, n):
                return x.unsqueeze(1).broadcast_to([P, n, x.shape[-1]])

            def pre_norm(n, col):
                settle()
                dve.wait_ge(std_ready, n + 1)
                nc.vector.reciprocal(rstd[:, 0:S1], std[:, 0:S1])
                settle()
                for k in range(KT):
                    nc.vector.scalar_tensor_tensor(out=uT[:, k, 0:S1], in0=hx[:, k, :], scalar=gains[:, col + k:col + k + 1],
                                                   in1=rstd[:, 0:S1], op0=ALU.mult, op1=ALU.mult).then_inc(u_ready, 1)

            def post_norm(n, col):
                settle()
                dve.wait_ge(std_ready, n + 1)
                nc.vector.reciprocal(rstd[:, 0:S1], std[:, 0:S1])
                settle()
                for k in range(KT):
                    nc.vector.scalar_tensor_tensor(out=yT[:, k, 0:S1], in0=yT[:, k, 0:S1], scalar=gains[:, col + k:col + k + 1],
                                                   in1=rstd[:, 0:S1], op0=ALU.mult, op1=ALU.mult)
                settle()
                nc.vector.tensor_tensor(hx[:, :, :], hx[:, :, :], yT[:, :, 0:S1], ALU.add).then_inc(h_ready, 1)

            def attention(l, kind):
                base = {"A": 0, "B": 20, "X": 16 if l == 0 else 28}[kind]
                scale = 1.0 / 16 if kind == "X" else 0.125
                n = items(kind)

                def maxima(m):
                    s = m % 3
                    settle()
                    for c in range(score_tiles(kind)):
                        b = filled("S", l, kind, m, c)
                        src = ps[:, b, :]
                        if kind == "A":
                            nc.vector.tensor_tensor(probs[:, s, 0, :], src, maskA, ALU.add).then_inc(free[b], 1)
                            settle()
                            src = probs[:, s, 0, :]
                        nc.vector.reduce_max(rmax[:, s, c, :], src.rearrange("p (j t) -> p j t", j=2), AX.X)
                    settle()
                    nc.vector.tensor_scalar(nmax[:, s, 0:score_tiles(kind), :], rmax[:, s, 0:score_tiles(kind), :],
                                            -scale, None, ALU.mult).then_inc(max_ready, 1)

                def normalise(m):
                    s = m % 3
                    settle()
                    dve.wait_ge(exp_ready, base + m + 1)
                    nc.vector.reciprocal(rden[:, s, 0:score_tiles(kind), :], den[:, s, 0:score_tiles(kind), :])
                    settle()
                    if kind == "B":
                        nc.vector.tensor_scalar(rden[:, s, 1, :], rden[:, s, 1, :], lam, -1.0, ALU.mult, ALU.mult)
                        settle()
                    for j in range(2):
                        p = probs[:, s, 0, j * S1:(j + 1) * S1]
                        ins = nc.vector.tensor_scalar(p, p, rden[:, s, 0, j:j + 1], None, ALU.mult)
                    if kind == "B":
                        settle()
                        for j in range(2):
                            p = probs[:, s, 0, j * S1:(j + 1) * S1]
                            p1 = probs[:, s, 1, j * S1:(j + 1) * S1]
                            ins = nc.vector.scalar_tensor_tensor(out=p, in0=p1, scalar=rden[:, s, 1, j:j + 1], in1=p,
                                                                 op0=ALU.mult, op1=ALU.add)
                    ins.then_inc(p_ready, 1)

                def heads_out(m):
                    if kind == "A":
                        if m % 2 == 0:
                            return
                        b, u = tiles[("V", l, kind, m - 1)]
                        dve.wait_ge(full[b], u)
                        nc.vector.tensor_copy(oT[:, m // 2, 0:S1], ps[:, b, 0:S1]).then_inc(o_ready, 1)
                    elif kind == "B":
                        b = filled("V", l, kind, m)
                        nc.vector.tensor_copy(oT[:, m, 0:S1], ps[:, b, 0:S1]).then_inc(o_ready, 1)
                    else:
                        b = filled("V", l, kind, m)
                        nc.vector.tensor_copy(oT[:, 2 * m:2 * m + 2, 0:S1],
                                              ps[:, b, :].rearrange("p (a t) -> p a t", a=2)).then_inc(o_ready, 1)
                    nc.vector.drain().then_inc(free[b], 1)

                maxima(0)
                maxima(1)
                for m in range(n):
                    normalise(m)
                    if m + 2 < n:
                        maxima(m + 2)
                    if m:
                        heads_out(m - 1)
                heads_out(n - 1)

            nc.vector.memset(ones[:, :], 1.0).then_inc(memset_done, 1)
            nc.vector.memset(eps6[:, :], 1e-6).then_inc(memset_done, 1)
            dve.wait_ge(const_in, 16 * CONSTS)
            angle, turns = rot_tmp[:, 0:S1], rot_tmp[:, S1:2 * S1]
            nc.vector.tensor_copy(angle, pos_i[:, :])
            settle()
            nc.vector.tensor_scalar(angle, angle, invf, None, ALU.mult)
            settle()
            nc.vector.tensor_scalar(turns, angle, 1.0 / (2 * math.pi), ROUND, ALU.mult, ALU.add)
            settle()
            nc.vector.tensor_scalar(turns, turns, -ROUND, None, ALU.add)
            settle()
            for part in TWO_PI:
                nc.vector.scalar_tensor_tensor(out=angle, in0=turns, scalar=-part, in1=angle, op0=ALU.mult, op1=ALU.add)
                settle()
            nc.vector.tensor_scalar(rope[:, 1, :], angle, math.pi, -math.pi, ALU.min, ALU.max)
            nc.vector.tensor_scalar(angle, angle, math.pi / 2, None, ALU.add)
            settle()
            nc.vector.tensor_scalar(turns, angle, math.pi, -2 * math.pi, ALU.is_gt, ALU.mult)
            settle()
            nc.vector.tensor_tensor(angle, angle, turns, ALU.add)
            settle()
            nc.vector.tensor_scalar(rope[:, 0, :], angle, math.pi, -math.pi, ALU.min, ALU.max).then_inc(rope_args, 1)
            for a in range(2):
                nc.vector.tensor_tensor(lamv[:, 2 * a, :], lamv[:, 2 * a, :], lamv[:, 2 * a + 1, :], ALU.mult)
            settle()
            for a in range(2):
                ins = nc.vector.reduce_sum(lam_parts[:, a:a + 1], lamv[:, 2 * a, :], AX.X)
            ins.then_inc(lam_args, 1)
            dve.wait_ge(lam_exp, 1)
            nc.vector.tensor_tensor(lam, lam_parts[:, 2:3], lam_parts[:, 3:4], ALU.subtract)
            settle()
            nc.vector.tensor_scalar(lam, lam, LAM_INIT, None, ALU.add)
            dve.wait_ge(gain_cols, 1)
            dve.wait_ge(std_ready, 1)
            nc.vector.reciprocal(rstd[:, 0:S1], std[:, 0:S1]).then_inc(memn_ready, 1)
            settle()
            nc.vector.tensor_tensor(memn[:, :, :], memn[:, :, :], over(rstd[:, 0:S1], KT), ALU.mult)
            nc.vector.tensor_scalar(gains[:, 112:113], gains[:, 112:113], 1.0 - LAM_INIT, None, ALU.mult)
            dve.wait_ge(x_ready, 4)
            dve.wait_ge(rope_ready, 1)
            for l in range(DEPTH):
                kind = "AB"[l]
                n0 = 1 + 6 * l
                pre_norm(n0, 8 * l)
                for g in range(8):
                    b = filled("rot", l, g)
                    qk = (qT if g < 4 else kT)[:, 2 * (g % 4):2 * (g % 4) + 2, :]
                    tmp = rot_tmp[:, :].rearrange("p (a t) -> p a t", a=2)
                    nc.vector.tensor_tensor(tmp, ps[:, b, :].rearrange("p (a t) -> p a t", a=2), over(rope[:, 1, :], 2),
                                            ALU.mult).then_inc(free[b], 1)
                    nc.vector.tensor_tensor(qk, qk, over(rope[:, 0, :], 2), ALU.mult)
                    settle()
                    nc.vector.tensor_tensor(qk, qk, tmp, ALU.add).then_inc(qk_ready, 1)
                    settle()
                attention(l, kind)
                if kind == "B":
                    dve.wait_ge(sub_std, 4)
                    nc.vector.reciprocal(yT[:, :, 0:S1], yT[:, :, 0:S1])
                    settle()
                    nc.vector.scalar_tensor_tensor(out=oT[:, :, 0:S1], in0=oT[:, :, 0:S1], scalar=gains[:, 112:113],
                                                   in1=yT[:, :, 0:S1], op0=ALU.mult, op1=ALU.mult).then_inc(sub_done, 1)
                b, u = tiles[("v", l, 1, 1)]
                dve.wait_ge(full[b], u)
                for k in range(KT):
                    ins = nc.vector.tensor_scalar(uT[:, k, 0:S1], memn[:, k, :], gains[:, 48 + 8 * l + k:49 + 8 * l + k],
                                                  None, ALU.mult)
                ins.then_inc(mem_u, 1)
                post_norm(n0 + 1, 16 + 8 * l)
                filled("mv", l, 1, 1)
                pre_norm(n0 + 2, 32 + 8 * l)
                attention(l, "X")
                post_norm(n0 + 3, 64 + 8 * l)
                pre_norm(n0 + 4, 80 + 8 * l)
                for c in range(11):
                    dve.wait_ge(silu_ready, 11 * l + c + 1)
                    b = filled("u", l, c)
                    h2 = hid[:, 2 * c:2 * c + 2, :]
                    nc.vector.tensor_tensor(h2, h2, ps[:, b, :].rearrange("p (a t) -> p a t", a=2),
                                            ALU.mult).then_inc(hid_ready, 1)
                    nc.vector.drain().then_inc(free[b], 1)
                post_norm(n0 + 5, 96 + 8 * l)
            def h4(b, L0, L1):
                return heads(ps[:, b, :])[0:L0, :, 0:L1]

            def per_head(x, L, w):
                return x.unsqueeze(2).broadcast_to([L, DH, w])

            def all_heads(x, L, w):
                return x.unsqueeze(1).broadcast_to([L, DH, w])

            b, u = tiles[("d", 1, 3)]
            dve.wait_ge(full[b], u)
            settle()
            for x in (tok, cum, logits, idxf, ecum):
                nc.vector.memset(x[:], 0.0)
            nc.vector.memset(gate_log[:, :, :], 0.0)
            nc.vector.memset(grp8[:, :, :], NEG)
            nc.vector.memset(eps5[:, :], 1e-5)
            nc.vector.memset(eps128[:, :], 128e-6).then_inc(zeros2, 1)
            nc.vector.memset(chosen[:, :, :], 0.0)
            nc.vector.memset(rank1[:, :, :], 0.0)
            nc.vector.memset(starts[:, :], 0.0)
            for b in range(BANKS):
                nc.vector.drain().then_inc(loop_free[b], 1)
            dve.wait_ge(const2_in[0], 16 * 9)
            for l in range(DEPTH):
                G0 = 113 + 81 * l
                settle()
                nc.vector.memset(conv_in[:, :, 0:3], 0.0)
                dve.wait_ge(tok_ready, l + 1)
                settle()
                nc.vector.tensor_tensor(gate_x[:, :, :], tok[:, :, 12:16], over(rows2[:, l, 40:44], 3), ALU.add)
                nc.vector.tensor_scalar(gate_log[:, :, 4:8], tok[:, :, 8:12], -1.0, None, ALU.mult)
                settle()
                nc.vector.tensor_scalar(gate_log[:, :, 0:4], gate_x[:, :, :], -1.0, None, ALU.mult)
                settle()
                nc.vector.tensor_tensor(gate_log[:, :, 0:4], gate_log[:, :, 0:4], gate_x[:, :, :], ALU.min).then_inc(sp_args, 1)
                nc.vector.tensor_scalar(tok[:, :, 0:8], tok[:, :, 0:8], SH ** -0.5, None, ALU.mult)
                for i in range(12):
                    dve.wait_ge(conv_raw, 12 * l + i + 1)
                    x = cv_qk[:, i, :] if i < 8 else cv_v[:, i - 8, :]
                    nc.vector.tensor_scalar(x, conv_in[:, i, 0:S2], gains[:, G0 + i:G0 + i + 1], None, ALU.mult)
                    for w in range(1, 4):
                        settle()
                        c = G0 + 12 * w + i
                        ins = nc.vector.scalar_tensor_tensor(out=x, in0=conv_in[:, i, w:w + S2], scalar=gains[:, c:c + 1], in1=x,
                                                             op0=ALU.mult, op1=ALU.add)
                    ins.then_inc(conv_acc, 1)
                for what, nm, i, j in [t for t in rot_tiles() if t[0] == "rot2"]:
                    b = filled("rot2", l, nm, i)
                    x = dict(sq=qs, sk=ks, iq=iq, ik=ik)[nm][:, i, :]
                    settle()
                    nc.vector.tensor_tensor(rot2_tmp[:, :], ps[:, b, 0:S2], sin2, ALU.mult).then_inc(free[b], 1)
                    nc.vector.tensor_tensor(x, x, cos2, ALU.mult)
                    settle()
                    nc.vector.tensor_tensor(x, x, rot2_tmp[:, :], ALU.add).then_inc(rot_done, 1)
                dve.wait_ge(sp_logs, l + 1)
                nc.vector.tensor_scalar(gate_x[:, :, :], gate_x[:, :, :], 0.0, None, ALU.max)
                nc.vector.tensor_scalar(neg_a[:, :], neg_a[:, :], -1.0, None, ALU.mult)
                nc.vector.tensor_scalar(gate_exp[:, :, 4:8], gate_exp[:, :, 4:8], 1.0, None, ALU.add)
                settle()
                nc.vector.tensor_tensor(gate_x[:, :, :], gate_x[:, :, :], gate_log[:, :, 0:4], ALU.add)
                nc.vector.reciprocal(beta[:, :, :], gate_exp[:, :, 4:8])
                settle()
                nc.vector.tensor_tensor(g_tok[:, :, :], gate_x[:, :, :], over(neg_a[:, :], 3), ALU.mult).then_inc(gb_ready, 1)
                for i in range(8):
                    dve.wait_ge(l2_root, 8 * l + i + 1)
                    settle()
                    nc.vector.reciprocal(yT[:, i, :], yT[:, i, :])
                    settle()
                    nc.vector.tensor_tensor(cv_qk[:, i, :], cv_qk[:, i, :], yT[:, i, :], ALU.mult).then_inc(qk_unit, 1)
                b = filled("gcc", l)
                settle()
                nc.vector.tensor_copy(cum[:, 0:2, 0:4], ps[:, b, 0:8].rearrange("p (n c) -> p n c", n=2))
                nc.vector.tensor_copy(cum[0:16, 2, 0:4], ps[0:16, b, 8:12]).then_inc(free[b], 1)
                for n, (t0, L) in enumerate(TOK):
                    b = filled("gcb", l, n)
                    d = heads(decay)[0:L, :, 0:L]
                    settle()
                    nc.vector.tensor_copy(cum[:, n, 8:12], heads(ps[:, b, :])[:, :, L - 1])
                    nc.vector.tensor_tensor(d, h4(b, L, L), per_head(cum[0:L, n, 0:4], L, L), ALU.subtract)
                    settle()
                    nc.vector.tensor_tensor(d, d, all_heads(decay_mask[0:L, 0:L], L, L), ALU.add).then_inc(decay_args, 1)
                    b = filled("bb", l, n)
                    bs = heads(beta_strict)[0:L, :, 0:L]
                    nc.vector.tensor_tensor(bs, h4(b, L, L), all_heads(strict[0:L, 0:L], L, L), ALU.mult).then_inc(free[b], 1)
                    dve.wait_ge(decay_ready, 3 * l + n + 1)
                    b = filled("KK", l, n)
                    lt = heads(LT[:, n, :])[0:L, :, 0:L]
                    nc.vector.tensor_tensor(lt, h4(b, L, L), d, ALU.mult).then_inc(free[b], 1)
                    settle()
                    nc.vector.tensor_tensor(lt, lt, bs, ALU.mult).then_inc(lt_ready, 1)
                    b = filled("KQ", l, n)
                    nc.vector.tensor_tensor(heads(QK[:, n, :])[0:L, :, 0:L], h4(b, L, L), d, ALU.mult).then_inc(free[b], 1)
                    dve.wait_ge(egc_ready, 3 * l + n + 1)
                    nc.vector.tensor_tensor(cv_qk[:, 0:4, t0:t0 + L], cv_qk[:, 0:4, t0:t0 + L], heads(egc)[:, :, 0:L], ALU.mult)
                    b = filled("kt", l, n)
                    nc.vector.tensor_copy(k_tok[0:L, n, :], ps[0:L, b, :]).then_inc(free[b], 1)
                    b = filled("vt", l, n)
                    nc.vector.tensor_tensor(heads(v_beta[:, n, :])[0:L], h4(b, L, P), per_head(beta[0:L, n, :], L, P),
                                            ALU.mult).then_inc(free[b], 1)
                    nc.vector.drain().then_inc(qk_dec, 1)
                nc.vector.tensor_tensor(cum[:, :, 4:8], cum[:, :, 8:12], cum[:, :, 0:4], ALU.subtract).then_inc(cum_ready, 1)
                for lv in range(7):
                    for n in range(3):
                        if lv >= LV[n]:
                            continue
                        L = TOK[n][1]
                        tm, tt = heads(Tm[:, n, :])[0:L, :, 0:L], heads(TT[:, n, :])[0:L, :, 0:L]
                        settle()
                        if lv == 0:
                            eye = all_heads(ident[0:L, 0:L], L, L)
                            dve.wait_ge(as_ready, as_at[l][(0, n)])
                            nc.vector.tensor_tensor(tt, eye, heads(As[:, n, :])[0:L, :, 0:L], ALU.subtract)
                            b = filled("X", l, lv, n)
                            nc.vector.tensor_tensor(tm, eye, h4(b, L, L), ALU.subtract).then_inc(free[b], 1)
                        else:
                            b = filled("Y", l, lv, n)
                            nc.vector.tensor_tensor(tm, tm, h4(b, L, L), ALU.subtract).then_inc(free[b], 1)
                            b = filled("Z", l, lv, n)
                            nc.vector.tensor_tensor(tt, tt, h4(b, L, L), ALU.subtract).then_inc(free[b], 1)
                        nc.vector.drain().then_inc(t_ready, 1)
                dve.wait_ge(ecum_ready, l + 1)
                nc.vector.tensor_tensor(ecum[:, :, 0:4], ecum[:, :, 0:4], beta[:, :, :], ALU.mult)
                settle()
                for n, (t0, L) in enumerate(TOK):
                    kt = heads(k_tok[:, n, :])[0:L]
                    nc.vector.tensor_tensor(heads(k_be[:, n, :])[0:L], kt, per_head(ecum[0:L, n, 0:4], L, P), ALU.mult).then_inc(kbe_ready, 1)
                settle()
                for n, (t0, L) in enumerate(TOK):
                    kt = heads(k_tok[:, n, :])[0:L]
                    nc.vector.tensor_tensor(kt, kt, per_head(ecum[0:L, n, 4:8], L, P), ALU.mult)
                nc.vector.drain().then_inc(tokens_ready, 1)
                for n in range(2):
                    b = filled("su", l, n)
                    if n == 0:
                        nc.vector.tensor_copy(state, ps[:, b, :]).then_inc(state_ready, 1)
                    else:
                        for h in range(DH):
                            s_h = state[:, h * P:(h + 1) * P]
                            nc.vector.scalar_tensor_tensor(out=s_h, in0=s_h, scalar=ecum[:, n, 8 + h:9 + h], in1=ps[:, b, h * P:(h + 1) * P],
                                                           op0=ALU.mult, op1=ALU.add)
                        nc.vector.drain().then_inc(state_ready, 1)
                    nc.vector.drain().then_inc(free[b], 1)
                dve.wait_ge(on_root, 4 * l + 4)
                nc.vector.reciprocal(yT[:, 0:4, :], yT[:, 0:4, :])
                settle()
                nc.vector.scalar_tensor_tensor(out=oT[:, 0:4, :], in0=oT[:, 0:4, :], scalar=gains[:, G0 + 48:G0 + 49], in1=yT[:, 0:4, :],
                                               op0=ALU.mult, op1=ALU.mult)
                settle()
                nc.vector.tensor_tensor(oT[:, 0:4, :], oT[:, 0:4, :], z_gate[:, :, :], ALU.mult).then_inc(dn_done, 1)
                for n, (t0, L) in enumerate(TOK):
                    for h in range(SH):
                        i = 24 * l + 8 * n + h
                        dve.wait_ge(relu_ready, i + 1)
                        wi = tok[0:L, n, h:h + 1]
                        settle()
                        if h == 0:
                            nc.vector.tensor_scalar(score[0:L, n, :], relu_s[0:L, h % 2, :], wi, None, ALU.mult).then_inc(relu_used, 1)
                        else:
                            nc.vector.scalar_tensor_tensor(out=score[0:L, n, :], in0=relu_s[0:L, h % 2, :], scalar=wi, in1=score[0:L, n, :],
                                                           op0=ALU.mult, op1=ALU.add).then_inc(relu_used, 1)
                    settle()
                    nc.vector.tensor_tensor(score[0:L, n, :], score[0:L, n, :], causal[0:L, n, :], ALU.add)
                for r in range(TOPK // 8):
                    for n, (t0, L) in enumerate(TOK):
                        settle()
                        nc.vector.max(best[0:L, n, :], score[0:L, n, :])
                        settle()
                        nc.vector.match_replace(out=score[0:L, n, :], in_to_replace=best[0:L, n, :], in_values=score[0:L, n, :], imm_value=-3e38)
                settle()
                for n, (t0, L) in enumerate(TOK):
                    nc.vector.tensor_scalar(score[0:L, n, :], score[0:L, n, :], -2e38, NEG, ALU.is_gt, ALU.mult)
                    settle()
                    nc.vector.tensor_tensor(score[0:L, n, :], score[0:L, n, :], causal[0:L, n, :], ALU.add)

                def max_unit(m):
                    n, h = units[m]
                    t0, L = TOK[n]
                    s = m % 3
                    b = filled("aS", l, m)
                    p = probs2[0:L, s, 0:t0 + L]
                    settle()
                    nc.vector.tensor_tensor(p, ps[0:L, b, 0:t0 + L], score[0:L, n, 0:t0 + L], ALU.add).then_inc(free[b], 1)
                    settle()
                    nc.vector.reduce_max(stat2[0:L, 0, s:s + 1], p, AX.X)
                    settle()
                    nc.vector.tensor_scalar(stat2[0:L, 1, s:s + 1], stat2[0:L, 0, s:s + 1], -0.125, None, ALU.mult).then_inc(max2, 1)

                def norm_unit(m):
                    n, h = units[m]
                    t0, L = TOK[n]
                    s = m % 3
                    settle()
                    dve.wait_ge(exp2, 24 * l + m + 1)
                    nc.vector.reciprocal(stat2[0:L, 3, s:s + 1], stat2[0:L, 2, s:s + 1])
                    settle()
                    p = probs2[0:L, s, 0:t0 + L]
                    nc.vector.tensor_scalar(p, p, stat2[0:L, 3, s:s + 1], None, ALU.mult).then_inc(p2, 1)

                def out_unit(m):
                    if m % 2:
                        n, h = units[m]
                        t0, L = TOK[n]
                        b = filled("aV", l, m - 1)
                        nc.vector.tensor_copy(oT[:, 4 + h // 2, t0:t0 + L], ps[:, b, 0:L]).then_inc(sa_ready, 1)
                        nc.vector.drain().then_inc(free[b], 1)
                max_unit(0)
                max_unit(1)
                for m in range(24):
                    norm_unit(m)
                    if m + 2 < 24:
                        max_unit(m + 2)
                    if m:
                        out_unit(m - 1)
                out_unit(23)

                def layer_norm(j, x, g_at, b_at):
                    dve.wait_ge(mean_ready, 2 * l + j + 1)
                    settle()
                    nc.vector.tensor_tensor(x[:, :, :], x[:, :, :], over(std[:, :], KT), ALU.subtract).then_inc(cent_ready, 1)
                    dve.wait_ge(ln_root, 2 * l + j + 1)
                    nc.vector.reciprocal(rstd[:, :], std[:, :])
                    settle()
                    nc.vector.tensor_tensor(x[:, :, :], x[:, :, :], over(rstd[:, :], KT), ALU.mult)
                    settle()
                    for k in range(KT):
                        nc.vector.tensor_scalar(hT[:, k, :], x[:, k, :], gains[:, g_at + k:g_at + k + 1], gains[:, b_at + k:b_at + k + 1],
                                                ALU.mult, ALU.add)
                    nc.vector.drain().then_inc(ln_done, 1)

                for i in range(KT):
                    b = filled("wo", l, i)
                    if i == 7:
                        settle()
                    nc.vector.scalar_tensor_tensor(out=hT[:, i, :], in0=hT[:, i, :], scalar=ALPHA, in1=ps[:, b, 0:S2],
                                                   op0=ALU.mult, op1=ALU.add).then_inc(free[b], 1)
                nc.vector.drain().then_inc(mix_ready, 1)
                layer_norm(0, hT, G0 + 49, G0 + 57)
                nc.vector.tensor_scalar(yacc[:, :, :], hT[:, :, :], ALPHA, None, ALU.mult)
                b = filled("rt", l)
                nc.vector.tensor_tensor(logits[:, 0:2, :], ps[:, b, 0:72].rearrange("p (n c) -> p n c", n=2), over(rows2[:, l, 0:36], 2), ALU.add)
                nc.vector.tensor_tensor(logits[0:16, 2, :], ps[0:16, b, 72:108], rows2[0:16, l, 0:36], ALU.add).then_inc(free[b], 1)
                settle()
                nc.vector.tensor_copy(grp8[:, :, 0:4], logits[:, :, 0:4])
                settle()
                for n in range(3):
                    nc.vector.max(top8[:, 0, n, :], grp8[:, n, :])
                settle()
                for n in range(3):
                    nc.vector.max_index(idx8[:, 0, n, :], top8[:, 0, n, :], grp8[:, n, :])
                settle()
                nc.vector.tensor_copy(idxf[:, 0, :, :], idx8[:, 0, :, :])
                settle()
                lg = comb[:, 1, :, :]
                for n in range(3):
                    nc.vector.tensor_scalar(lg[:, n, :], group, idxf[:, 0, n, 0:1], None, ALU.is_equal)
                settle()
                nc.vector.tensor_scalar(lg, lg, -NEG, NEG, ALU.mult, ALU.add)
                settle()
                nc.vector.tensor_tensor(lg, lg, logits[:, :, 4:36], ALU.add)
                settle()
                for n in range(3):
                    nc.vector.max(top8[:, 1, n, :], lg[:, n, :])
                settle()
                for n in range(3):
                    nc.vector.max_index(idx8[:, 1, n, :], top8[:, 1, n, :], lg[:, n, :])
                nc.vector.tensor_tensor(rexp[:, :, 0:4], grp8[:, :, 0:4], top8[:, 0, :, 0:1].broadcast_to([P, 3, 4]), ALU.subtract)
                nc.vector.tensor_tensor(rexp[:, :, 4:5], top8[:, 1, :, 1:2], top8[:, 1, :, 0:1], ALU.subtract)
                nc.vector.drain().then_inc(rt_args, 1)
                nc.vector.tensor_copy(idxf[:, 1, :, :], idx8[:, 1, :, :])
                dve.wait_ge(rt_exp, l + 1)
                nc.vector.reduce_sum(gates[:, :, 0:1], rexp[:, :, 0:4], AX.X)
                nc.vector.tensor_scalar(gates[:, :, 1:2], rexp[:, :, 4:5], 1.0, None, ALU.add)
                settle()
                nc.vector.tensor_tensor(gates[:, :, 0:1], gates[:, :, 0:1], gates[:, :, 1:2], ALU.mult)
                settle()
                nc.vector.reciprocal(gates[:, :, 2:3], gates[:, :, 0:1])
                settle()
                nc.vector.tensor_tensor(gates[:, :, 3:4], gates[:, :, 2:3], rexp[:, :, 4:5], ALU.mult)
                settle()
                for a in range(2):
                    for n in range(3):
                        nc.vector.tensor_scalar(comb[:, a, n, :], iota, idxf[:, 1, n, a:a + 1], gates[:, n, 2 + a:3 + a], ALU.is_equal, ALU.mult)
                settle()
                nc.vector.tensor_tensor(comb[:, 0, :, :], comb[:, 0, :, :], comb[:, 1, :, :], ALU.add)
                settle()
                for n, (t0, L) in enumerate(TOK):
                    nc.vector.tensor_scalar(comb[0:L, 1, n, :], iota[0:L], idxf[0:L, 1, n, 0:1], None, ALU.is_equal)
                    settle()
                    nc.vector.scalar_tensor_tensor(out=chosen[0:L, n, :], in0=iota[0:L], scalar=idxf[0:L, 1, n, 1:2], in1=comb[0:L, 1, n, :],
                                                   op0=ALU.is_equal, op1=ALU.add)
                nc.vector.drain().then_inc(comb_ready, 1)
                b = filled("rk", l)
                for n, (t0, L) in enumerate(TOK):
                    nc.vector.scalar_tensor_tensor(out=rank1[0:L, n, :], in0=ps[0:L, b, n * NE:(n + 1) * NE], scalar=1.0, in1=chosen[0:L, n, :],
                                                   op0=ALU.add, op1=ALU.mult)
                nc.vector.reduce_max(group_max[:, :], ps[:, b, 3 * NE:4 * NE].rearrange("p (g j) -> p g j", g=8), AX.X)
                nc.vector.drain().then_inc(free[b], 1)
                nc.vector.tensor_scalar(rank[:, :, :], rank1[:, :, :], -1.0, None, ALU.add)
                nc.vector.tensor_tensor(over_edge[:, :, :], group_max[:, :].unsqueeze(2).broadcast_to([P, 8, 8]),
                                        edges[:, 1:9].unsqueeze(1).broadcast_to([P, 8, 8]), ALU.is_gt)
                if l:
                    nc.vector.tensor_copy(starts[:, 0:1], starts[:, 8:9])
                settle()
                nc.vector.reduce_sum(passes[:, :], over_edge[:, :, :], AX.X)
                settle()
                for g in range(8):
                    nc.vector.scalar_tensor_tensor(out=starts[:, g + 1:g + 2], in0=passes[:, g:g + 1], scalar=1.0, in1=starts[:, g:g + 1],
                                                   op0=ALU.add, op1=ALU.add)
                    settle()
                nc.vector.tensor_copy(steps[:, l, 0:9], starts[:, :]).then_inc(steps_ready, 1)
                settle()
                dve.wait_ge(steps_ready, l + 1)
                with nc.vector.Fori(0, 8) as g:
                    first_step = dve.value_load(steps[0:1, l, bass.ds(g, 1)], min_val=0, max_val=1000)
                    end_step = dve.value_load(steps[0:1, l, bass.ds(g + 1, 1)], min_val=1, max_val=1000)
                    settle()
                    nc.vector.memset(pass_at[:, :], 0.0)
                    with nc.vector.Fori(first_step, end_step) as s:
                        settle()
                        for n in range(3):
                            nc.vector.scalar_tensor_tensor(
                                out=sel[:, n, :].rearrange("p (j c) -> p j c", j=4), in0=iota.unsqueeze(1).broadcast_to([P, 4, 32]),
                                scalar=pass_at[:, :],
                                in1=rank[:, n, bass.ds(g * 4, 4)].unsqueeze(2).broadcast_to([P, 4, 32]), op0=ALU.add, op1=ALU.is_equal)
                        settle()
                        for n in range(3):
                            nc.vector.tensor_tensor(sel_gate[:, n, :].rearrange("p (j c) -> p j c", j=4),
                                                    sel[:, n, :].rearrange("p (j c) -> p j c", j=4),
                                                    comb[:, 0, n, bass.ds(g * 4, 4)].unsqueeze(2).broadcast_to([P, 4, 32]), ALU.mult)
                        nc.vector.drain().then_inc(sel_ready, 1)
                        nc.vector.tensor_scalar(pass_at[:, :], pass_at[:, :], 32.0, None, ALU.add)
                        b = LB["up"]
                        dve.wait_ge(esilu_ready, s + 1)
                        nc.vector.tensor_tensor(e_hid[:, :], e_silu[:, :], ps[:, b, DE:2 * DE], ALU.mult).then_inc(ehid_ready, 1)
                        nc.vector.drain().then_inc(loop_free[b], 1)
                        for i in range(KT):
                            b = LB["out"][i]
                            dve.wait_ge(loop_full[b], s * L_USES[b] + L_OUT[i])
                            nc.vector.tensor_tensor(yacc[:, i, :], yacc[:, i, :], ps[:, b, 0:S2], ALU.add).then_inc(loop_free[b], 1)
                nc.vector.drain().then_inc(mix_ready, 1)
                layer_norm(1, yacc, G0 + 65, G0 + 73)


NAMES = ["x", "mem", "positions", "mix_pre_g", "mix_post_g", "mem_pre_g", "mem_kv_g", "mem_post_g", "ffn_pre_g",
         "ffn_post_g", "a_w_in", "a_w_out", "b_w_in", "b_w_out", "b_lam_q1", "b_lam_k1", "b_lam_q2", "b_lam_k2",
         "b_sub_g", "x_wq", "x_wkv", "x_wo", "w_gate_up", "w_down", "meta_tokens_2",
         "w_in_2", "conv_w_2", "a_log_2", "dt_bias_2", "dn_norm_g_2", "w_out_2", "ln1_g_2", "ln1_b_2", "w_grp_2",
         "b_grp_2", "w_rtr_2", "b_rtr_2", "w1_2", "w3_2", "w2_2", "ln2_g_2", "ln2_b_2"]


def kernel(**inputs):
    import concourse.bacc as bacc
    from concourse.bass_utils import run_bass_kernel_spmd

    nc = bacc.Bacc("TRN2", target_bir_lowering=False, num_devices=1)
    given = {name: np.ascontiguousarray(inputs[name]) for name in NAMES}
    given["tables1"], given["tables2"] = tables()
    arrays, access = {}, {}
    for name, a in given.items():
        arrays[f"in_{name}"] = a
        access[name] = nc.dram_tensor(f"in_{name}", a.shape, mybir.dt.from_np(a.dtype), kind="ExternalInput").ap()
    out = nc.dram_tensor("out", (1, S1, DM), F32, kind="ExternalOutput").ap()
    build(nc, access, out)
    result = run_bass_kernel_spmd(nc, [arrays], core_ids=[0])
    return result.results[0]["out"]
```

```python
import math
from contextlib import ExitStack

import numpy as np
import concourse.bass as bass
from concourse import mybir

F32 = mybir.dt.float32
I32 = mybir.dt.int32
F32R = mybir.dt.float32r
ALU = mybir.AluOpType
ACT = mybir.ActivationFunctionType
AX = mybir.AxisListType

P = 128
DM = 1024
KT = DM // P
S1 = 256
META = 16
S2 = S1 + META
DEPTH = 2
DFF = 2816
FT = DFF // P
HD = 64
SLOTS = 6
SLOT_W = 4096
BANKS = 8
RAW, HIGH = 6, 4
BANK_W = 512
NEG = -1e30
SPLIT = dict(dq=0, dk=512, dv=1024, dz=1536, db=2048, da=2052, sq=2056, sk=2568, sv=3080,
             iq=3592, ik=4104, iw=4168)
D_IN = 4176
DH = 4
SH = 8
TOPK = 64
NE = 32
DE = 256
ALPHA = (2.0 * DEPTH) ** 0.25
TOK = [(0, 128), (128, 128), (256, 16)]
LAM_INIT = 0.8 - 0.6 * math.exp(-0.3 * 1)
PATTERNS = ((128, 1), (512, 4), (2048, 16))

MAX_STEPS = DEPTH * (8 + 2 * S2 // 32) + 1

TABLES = dict(ident=128, rot1=128, rot2=128, invf=1, maskA=512)
TABLES2 = dict(triu=128, cos2=272, sin2=272, causal=816, decay=128, strict=128,
               levels=7 * 128, iota=32, group=32, edges=9, count=MAX_STEPS)


def offsets(widths):
    at, out = 0, {}
    for k, w in widths.items():
        out[k] = (at, w)
        at += w
    return out, at


def tables():
    i = np.arange(128)
    one = {k: np.zeros((128, w), np.float32) for k, w in TABLES.items()}
    two = {k: np.zeros((128, w), np.float32) for k, w in TABLES2.items()}
    one["ident"][i, i] = 1.0
    for m in range(128):
        r = m % 64
        if r < 8:
            one["rot1"][m + 8, m] = -1.0
        elif r < 16:
            one["rot1"][m - 8, m] = 1.0
        if r < 32:
            one["rot2"][m + 32, m] = -1.0
        else:
            one["rot2"][m - 32, m] = 1.0
    inv = (np.float32(500000.0) ** (-np.arange(0, 16, 2, dtype=np.float32) / np.float32(16))).astype(np.float32)
    one["invf"][:, 0] = np.where(i % 64 < 16, inv[i % 8], 0.0)
    q, k = np.arange(S1)[:, None], np.arange(S1)[None, :]
    count = sum(((abs(q - k) % d == 0) & (abs(q - k) // d <= w // (2 * d))).astype(np.float64)
                for w, d in PATTERNS)
    m = np.where(count > 0, np.log(np.maximum(count, 1)) * math.sqrt(HD), NEG).astype(np.float32)
    one["maskA"][:] = m.reshape(2, 128, S1).transpose(1, 0, 2).reshape(128, 512)
    t, j = i[:, None], i[None, :]
    two["triu"][:] = t <= j
    inv2 = (1.0 / (np.float32(10000.0) ** (np.arange(0, 64, 2, dtype=np.float32) / np.float32(64)))).astype(np.float32)
    ang = (np.arange(S2, dtype=np.float32)[None, :] * inv2[i % 32][:, None]).astype(np.float32)
    two["cos2"][:] = np.cos(ang)
    two["sin2"][:] = np.sin(ang)
    for n, (t0, c) in enumerate(TOK):
        two["causal"][:c, n * S2:(n + 1) * S2] = np.where(np.arange(S2)[None, :] <= t0 + np.arange(c)[:, None], 0, NEG)
    two["decay"][:] = np.where(j >= t, 0, NEG)
    two["strict"][:] = j > t
    for n in range(7):
        s = 1 << n
        two["levels"][:, n * 128:(n + 1) * 128] = (t // (2 * s) == j // (2 * s)) & (t % (2 * s) < s) & (j % (2 * s) >= s)
    two["iota"][:] = np.arange(NE)
    two["edges"][:] = 32 * np.arange(9)
    two["count"][:] = np.arange(MAX_STEPS)
    two["group"][:] = np.arange(NE) // 8
    return (np.concatenate(list(one.values()), 1), np.concatenate(list(two.values()), 1))


ROUND = 12582912.0
TWO_PI = (6.28125, 8117 / 4194304, 2 * math.pi - 6.28125 - 8117 / 4194304)
CONSTS = 26
O_DONE = {(0, "A"): 8, (0, "X"): 12, (1, "B"): 20, (1, "X"): 24}


def build(nc, A, out):
    ctx = ExitStack()
    with ctx:
        def sb(name, shape, dt=F32, stack=ctx):
            return stack.enter_context(nc.sbuf_tensor(name, shape, dt))

        def sem(name):
            return ctx.enter_context(nc.semaphore(name))

        O1, W1 = offsets(TABLES)
        O2, W2 = offsets(TABLES2)

        twins = {}

        def two_views(name, shape, stack=ctx):
            with ExitStack() as once:
                x = sb(name, shape, stack=once)
            twins[name] = sb(name + "_12", shape, F32R, stack=stack)
            return x

        ring = two_views("weight_ring", [P, SLOTS, SLOT_W])
        hT = sb("hT", [P, KT, S2])
        tab1 = sb("tables1", [P, W1])
        ones = sb("ones", [P, P])
        eps6 = sb("eps6", [P, 1])
        gains = sb("gains", [P, 113 + 2 * 81])
        std = sb("std", [P, S2])
        rstd = sb("rstd", [P, S2])
        uT = two_views("uT", [P, KT, S2])
        yT = sb("yT", [P, KT, S2])
        sq = sb("sq", [P, KT, S2])
        oT = two_views("oT", [P, KT, S2])
        first = ExitStack()
        memn = sb("memn", [P, KT, S1], stack=first)
        probs = two_views("probs", [P, 3, 2, 2 * S1], stack=first)
        probsT = two_views("probsT", [P, 2, 2 * S1], stack=first)
        rope = sb("rope", [P, 2, S1], stack=first)
        rot_tmp = sb("rot_tmp", [P, 2 * S1], stack=first)
        small = sb("small", [P, 64], stack=first)
        lamv = sb("lamv", [P, 4, HD], stack=first)
        pos_i = sb("pos_i", [P, S1], I32, stack=first)
        grows = sb("gain_rows", [P, 3, P], stack=first)
        qkv = two_views("qkv", [P, 3, KT * S1], stack=first)
        first.close()
        bays = ring[:, :, :].rearrange("p s n -> p (s n)").rearrange("p (b n) -> p b n", b=RAW + HIGH + 2)
        raw, high = bays[:, 0:RAW], bays[:, RAW:RAW + HIGH]
        uH, oH = (bays[:, RAW + HIGH + a].rearrange("p (k t) -> p k t", k=KT) for a in range(2))

        def r12(x):
            return bass.AP(tensor=twins[x.tensor.name], offset=x.offset, ap=x.ap)

        ident = tab1[:, O1["ident"][0]:O1["ident"][0] + P]
        rot1 = tab1[:, O1["rot1"][0]:O1["rot1"][0] + P]
        rot2 = tab1[:, O1["rot2"][0]:O1["rot2"][0] + P]
        invf = tab1[:, O1["invf"][0]:O1["invf"][0] + 1]
        maskA = tab1[:, O1["maskA"][0]:O1["maskA"][0] + 2 * S1]
        hx = hT[:, :, META:S2]
        qT = qkv[:, 0, :].rearrange("p (k t) -> p k t", k=KT)
        kT = qkv[:, 1, :].rearrange("p (k t) -> p k t", k=KT)
        vt = qkv[:, 2, :].rearrange("p (t n) -> p t n", t=2)
        probs_tiles = probs[:, :, :, :].rearrange("p a c (j t) -> p (a c j) t", j=2)
        probsT_tiles = probsT[:, :, :].rearrange("p a (j t) -> p (a j) t", j=2)

        def hidH(f, n=1):
            area, f = (probs_tiles, f) if f < 12 else (probsT_tiles, f - 12) if f < 16 else (oH, f - 16)
            return area[:, f:f + n, :]

        hid = qkv[:, :, :].rearrange("p a n -> p (a n)")[:, 0:FT * S1].rearrange("p (f t) -> p f t", f=FT)
        flat = lambda x: x[:, :, :].rearrange("p k t -> p (k t)")[:, 0:2 * DM].rearrange("p (t n) -> p t n", t=2)
        xin, memin, uT_flat = flat(yT), flat(oT), flat(uT)
        rmax = small[:, 0:12].rearrange("p (a c j) -> p a c j", a=3, c=2)
        nmax = small[:, 12:24].rearrange("p (a c j) -> p a c j", a=3, c=2)
        den = small[:, 24:36].rearrange("p (a c j) -> p a c j", a=3, c=2)
        rden = small[:, 36:48].rearrange("p (a c j) -> p a c j", a=3, c=2)
        lam = small[:, 48:49]
        lam_parts = small[:, 50:54]
        ps = ctx.enter_context(nc.psum_tensor("ps", [P, BANKS, BANK_W], F32))

        second = ExitStack()
        tab2 = sb("tables2", [P, W2], stack=second)
        small_w = sb("small_w", [P, KT, 144], stack=second)
        router_w = sb("router_w", [P, KT, 36], stack=second)
        rows2 = sb("rows2", [P, DEPTH, 44], stack=second)
        z_gate = sb("z_gate", [P, DH, S2], stack=second)
        chosen = sb("chosen", [P, 3, NE], stack=second)
        rank1 = sb("rank1", [P, 3, NE], stack=second)
        rank = sb("rank", [P, 3, NE], stack=second)
        group_max = sb("group_max", [P, 8], stack=second)
        over_edge = sb("over_edge", [P, 8, 8], stack=second)
        passes = sb("passes", [P, 8], stack=second)
        starts = sb("starts", [P, 9], stack=second)
        steps = sb("steps", [P, DEPTH, 18], I32, stack=second)
        tok = sb("tok", [P, 3, 16], stack=second)
        gate_log = sb("gate_log", [P, 3, 8], stack=second)
        gate_exp = sb("gate_exp", [P, 3, 8], stack=second)
        gate_x = sb("gate_x", [P, 3, 4], stack=second)
        g_tok = sb("g_tok", [P, 3, 4], stack=second)
        beta = sb("beta", [P, 3, 4], stack=second)
        neg_a = sb("neg_a", [P, 4], stack=second)
        cum = sb("cum", [P, 3, 12], stack=second)
        ecum = sb("ecum", [P, 3, 12], stack=second)
        logits = sb("logits", [P, 3, 36], stack=second)
        grp8 = sb("grp8", [P, 3, 8], stack=second)
        top8 = sb("top8", [P, 2, 3, 8], stack=second)
        idx8 = sb("idx8", [P, 2, 3, 8], mybir.dt.uint32, stack=second)
        idxf = sb("idxf", [P, 2, 3, 8], stack=second)
        rexp = sb("rexp", [P, 3, 8], stack=second)
        gates = sb("gates", [P, 3, 4], stack=second)
        comb = sb("comb", [P, 2, 3, NE], stack=second)
        stat2 = sb("stat2", [P, 4, 5], stack=second)
        score = sb("score", [P, 3, S2], stack=second)
        best = sb("best", [P, 3, 8], stack=second)
        eps5 = sb("eps5", [P, 1], stack=second)
        eps128 = sb("eps128", [P, 1], stack=second)
        middle = ExitStack()
        qs = sb("qs", [P, 4, S2], stack=middle)
        ks = sb("ks", [P, 4, S2], stack=middle)
        vs = sb("vs", [P, 3, 512], stack=middle)
        iq = sb("iq", [P, 4, S2], stack=middle)
        ik = sb("ik", [P, 1, S2], stack=middle)
        rot2_tmp = sb("rot2_tmp", [P, S2], stack=middle)
        work = sb("work", [P, 3072], stack=middle)
        middle.close()
        h_tok = sb("h_tok", [P, 3, DM], stack=second)
        x_g = sb("x_g", [P, KT, P], stack=second)
        sel = sb("sel", [P, 3, P], stack=second)
        sel_gate = sb("sel_gate", [P, 3, P], stack=second)
        scatter = sb("scatter", [P, S2], stack=second)
        step_group = sb("step_group", [P, MAX_STEPS], I32, stack=second)
        started = sb("started", [P, MAX_STEPS, 8], stack=second)
        spans = sb("spans", [P, 8], stack=second)
        group_at = sb("group_at", [P, MAX_STEPS], stack=second)
        pass_at = sb("pass_at", [P, MAX_STEPS], stack=second)
        e_out = sb("e_out", [P, DM], stack=second)
        e_silu = sb("e_silu", [P, DE], stack=second)
        e_hid = sb("e_hid", [P, DE], stack=second)
        e_hidT = sb("e_hidT", [P, 2, P], stack=second)
        second.close()
        AHEAD = 4
        AHEAD1 = AHEAD + 1
        meta_rows = z_gate[:, :, :].rearrange("p h t -> p (h t)")[0:META, 0:DM]

        def T2(name):
            return tab2[:, O2[name][0]:O2[name][0] + O2[name][1]]

        heads = lambda x: x.rearrange("p (h t) -> p h t", h=DH)
        count = T2("count")
        triu, decay_mask, strict = T2("triu"), T2("decay"), T2("strict")
        cos2, sin2, iota, group, edges = T2("cos2"), T2("sin2"), T2("iota"), T2("group"), T2("edges")
        causal = T2("causal").rearrange("p (n t) -> p n t", n=3)
        levels = T2("levels").rearrange("p (s t) -> p s t", s=7)
        relu_s = work[:, 0:544].rearrange("p (a t) -> p a t", a=2)
        probs2 = work[:, 0:AHEAD1 * S2].rearrange("p (a t) -> p a t", a=AHEAD1)
        probsT2 = work[:, AHEAD1 * S2:AHEAD1 * S2 + 768].rearrange("p (a k t) -> p a k t", a=2, k=3)
        LT = work[:, 0:1536].rearrange("p (n c) -> p n c", n=3)
        QK = work[:, 1536:3072].rearrange("p (n c) -> p n c", n=3)
        dn = ring[:, 4:6, :].rearrange("p s n -> p (s n)")
        conv_in = dn[:, 0:3300].rearrange("p (i t) -> p i t", i=12)
        Tm = dn[:, 0:1536].rearrange("p (n c) -> p n c", n=3)
        TT = dn[:, 1536:3072].rearrange("p (n c) -> p n c", n=3)
        cv_v = dn[:, 3300:4388].rearrange("p (i t) -> p i t", i=4)
        v_new = dn[:, 3300:3812]
        k_tok = dn[:, 4388:5924].rearrange("p (n c) -> p n c", n=3)
        v_beta = dn[:, 5924:7460].rearrange("p (n c) -> p n c", n=3)
        state = dn[:, 7460:7972]
        cv_qk = uT
        yflat = yT[:, :, :].rearrange("p k t -> p (k t)")
        sflat = sq[:, :, :].rearrange("p k t -> p (k t)")
        oflat = oT[:, :, :].rearrange("p k t -> p (k t)")
        Xs = yflat[:, 0:1536].rearrange("p (n c) -> p n c", n=3)
        decay = yflat[:, 1536:2048]
        As = sflat[:, 0:1536].rearrange("p (n c) -> p n c", n=3)
        k_be = As
        w_T = LT
        egc = sflat[:, 1536:2048]
        beta_strict = oflat[:, 1088:1600]
        yacc = yT

        full = [sem(f"psum_full{b}") for b in range(BANKS)]
        free = [sem(f"psum_free{b}") for b in range(BANKS)]
        loaded = [sem(f"weights_loaded{s}") for s in range(SLOTS)]
        bay_loaded = [sem(f"bay_loaded{b}") for b in range(RAW)]
        full.append(sem("down_part"))
        high_ready = sem("high_ready")
        rest_ready = sem("rest_ready")
        const_in = sem("const_in")
        memset_done = sem("memset_done")
        gain_cols = sem("gain_cols")
        rope_ready = sem("rope_ready")
        rope_args = sem("rope_args")
        x_in = sem("x_in")
        mem_in = sem("mem_in")
        x_ready = sem("x_ready")
        pre_sq = sem("pre_sq")
        post_sq = sem("post_sq")
        std_ready = sem("std_ready")
        u_ready = sem("u_ready")
        mem_u = sem("mem_u")
        memn_ready = sem("memn_ready")
        h_ready = sem("h_ready")
        q_raw = sem("q_raw")
        qk_ready = sem("qk_ready")
        xqk_raw = sem("xqk_raw")
        v_ready = sem("v_ready")
        max_ready = sem("max_ready")
        exp_ready = sem("exp_ready")
        p_ready = sem("p_ready")
        pt_ready = sem("pt_ready")
        o_ready = sem("o_ready")
        lam_args = sem("lam_args")
        lam_exp = sem("lam_exp")
        sub_sq = sem("sub_sq")
        sub_std = sem("sub_std")
        sub_done = sem("sub_done")
        silu_ready = sem("silu_ready")
        hid_ready = sem("hid_ready")
        out_sb = sem("out_sb")
        stored = sem("stored")
        const2_in = [sem(f"const2_in{l}") for l in range(DEPTH)]
        small_in = sem("small_in")
        router_in = sem("router_in")
        meta_in = sem("meta_in")
        meta_ready = sem("meta_ready")
        zeros2 = sem("zeros2")
        ready2 = sem("ready2")
        tok_ready = sem("tok_ready")
        sp_args = sem("sp_args")
        sp_logs = sem("sp_logs")
        gb_ready = sem("gb_ready")
        conv_raw = sem("conv_raw")
        conv_acc = sem("conv_acc")
        conv_out = sem("conv_out")
        l2_sq = sem("l2_sq")
        l2_root = sem("l2_root")
        qk_unit = sem("qk_unit")
        cum_ready = sem("cum_ready")
        ecum_ready = sem("ecum_ready")
        decay_args = sem("decay_args")
        decay_ready = sem("decay_ready")
        egc_ready = sem("egc_ready")
        qk_dec = sem("qk_dec")
        lt_ready = sem("lt_ready")
        as_ready = sem("as_ready")
        x_sb = sem("x_sb")
        t_ready = sem("t_ready")
        kbe_ready = sem("kbe_ready")
        tokens_ready = sem("tokens_ready")
        w_ready = sem("w_ready")
        vn_ready = sem("vn_ready")
        state_ready = sem("state_ready")
        od_ready = sem("od_ready")
        on_sq = sem("on_sq")
        on_root = sem("on_root")
        dn_done = sem("dn_done")
        raw2 = sem("raw2")
        rot_done = sem("rot_done")
        vs_ready = sem("vs_ready")
        relu_ready = sem("relu_ready")
        relu_used = sem("relu_used")
        max2 = sem("max2")
        exp2 = sem("exp2")
        p2 = sem("p2")
        pt2 = sem("pt2")
        sa_ready = sem("sa_ready")
        mix_ready = sem("mix_ready")
        mean_ready = sem("mean_ready")
        cent_ready = sem("cent_ready")
        ln_sq = sem("ln_sq")
        ln_root = sem("ln_root")
        ln_done = sem("ln_done")
        rt_args = sem("rt_args")
        rt_exp = sem("rt_exp")
        comb_ready = sem("comb_ready")
        htok_ready = sem("htok_ready")
        steps_ready = sem("steps_ready")
        loop_full = [sem(f"loop_full{b}") for b in range(BANKS)]
        loop_free = [sem(f"loop_free{b}") for b in range(BANKS)]
        sel_ready = sem("sel_ready")
        xg_ready = sem("xg_ready")
        esilu_ready = sem("esilu_ready")
        ehid_ready = sem("ehid_ready")
        ehidT_ready = sem("ehidT_ready")
        scatter_ready = sem("scatter_ready")
        eout_ready = sem("eout_ready")
        group_done = sem("group_done")

        use = [0] * BANKS
        tiles = {}
        turn = [0]

        def take(*key, bank=None):
            if bank is None:
                bank = turn[0] % BANKS
                turn[0] += 1
            use[bank] += 1
            tiles[key] = (bank, use[bank])

        slot_loads = [0] * SLOTS
        chunks = {}
        chunk_order = []
        last_tile = [None] * SLOTS

        bay_order = []
        bay_of = {}
        parts_used = [0]

        def bay_chunk(key, src, last, k=KT):
            bay_of[key] = len(bay_order)
            bay_order.append((k, src, last))

        def chunk(key, parts, last, slot=None):
            slot_loads[slot] += 16 * len(parts)
            chunks[key] = (slot, slot_loads[slot])
            chunk_order.append((slot, parts, last_tile[slot]))
            last_tile[slot] = last

        def items(kind):
            return {"A": 16, "B": 8, "X": 4}[kind]

        def ahead(kind):
            return 2 if kind == "B" else 4

        def place(kind, m, c=0):
            m %= ahead(kind) + 1
            return (m, c) if kind == "B" else (m // 2, m % 2)

        def attention_order(kind):
            n, lead = items(kind), ahead(kind) + 1
            order = [("S", m) for m in range(min(lead, n))]
            for m in range(n):
                order.append(("T", m))
                if m + lead < n:
                    order.append(("S", m + lead))
                if m:
                    order.append(("V", m - 1))
            return order + [("V", n - 1)]

        def score_tiles(kind):
            return 2 if kind == "B" else 1

        def plan_attention(l, kind):
            for what, m in attention_order(kind):
                if what == "S":
                    for c in range(score_tiles(kind)):
                        take("S", l, kind, m, c)
                elif what == "T":
                    take("T", l, kind, m)
                elif kind != "A" or m % 2 == 0:
                    take("V", l, kind, m)

        def rotary_order():
            order = []
            for g in range(8):
                order.append(("qk", g))
                if g:
                    order.append(("rot", g - 1))
            return order + [("rot", 7)]

        def cols(w, a, b):
            return w[:, a:b].rearrange("(k p) n -> p k n", p=P)

        for c in range(4):
            take("xT", c)
        for c in range(4):
            take("memT", c)
        take("gT")
        take("norm", 0)
        for l in range(DEPTH):
            kind = "AB"[l]
            w_in = A["a_w_in"][0] if l == 0 else A["b_w_in"][0]
            w_out = A["a_w_out"][0] if l == 0 else A["b_w_out"][0]
            n0 = 1 + 6 * l
            take("norm", n0)
            for what, g in rotary_order():
                take(what, l, g)
            for c in range(4):
                take("v", l, c)
            for g in range(8):
                bay_chunk(("qk", l, g), cols(w_in, 256 * g, 256 * g + 256), ("qk", l, g))
            for c in range(4):
                bay_chunk(("v", l, c), cols(w_in, 2048 + 256 * c, 2304 + 256 * c), ("v", l, c))
            plan_attention(l, kind)
            wkv = A["x_wkv"][l]
            for g in range(4):
                take("mk", l, g)
                bay_chunk(("mk", l, g), cols(wkv, 256 * g, 256 * g + 256), ("mk", l, g))
                if kind == "B" and g == 0:
                    for c in range(4):
                        take("sub", c)
            for g in range(4):
                take("o", l, g)
                bay_chunk(("o", l, g), cols(w_out, 256 * g, 256 * g + 256), ("o", l, g))
            take("norm", n0 + 1)
            for c in range(4):
                if c == 3:
                    take("norm", n0 + 2)
                take("mv", l, c)
                bay_chunk(("mv", l, c), cols(wkv, 1024 + 256 * c, 1280 + 256 * c), ("mv", l, c))
            for g in range(4):
                take("xq", l, g)
                bay_chunk(("xq", l, g), cols(A["x_wq"][l], 256 * g, 256 * g + 256), ("xq", l, g))
            plan_attention(l, "X")
            for g in range(4):
                take("xo", l, g)
                bay_chunk(("xo", l, g), cols(A["x_wo"][l], 256 * g, 256 * g + 256), ("xo", l, g))
            take("norm", n0 + 3)
            take("norm", n0 + 4)
            gu = A["w_gate_up"][l]
            for c in range(11):
                take("g", l, c)
                take("u", l, c)
                bay_chunk(("g", l, c), cols(gu, 256 * c, 256 * c + 256), ("g", l, c))
                bay_chunk(("u", l, c), cols(gu, DFF + 256 * c, DFF + 256 * c + 256), ("u", l, c))
            wd = A["w_down"][l]
            for g in range(4):
                take("d", l, g)
                for a in range(3):
                    last = ("d", l, g)
                    if a < 2:
                        last = ("part", l, g, a)
                        parts_used[0] += 1
                        tiles[last] = (BANKS, parts_used[0])
                    k0, k1 = 8 * a, min(8 * a + 8, FT)
                    bay_chunk(("d", l, g, a), cols(wd[P * k0:P * k1], 256 * g, 256 * g + 256), last, k1 - k0)
            take("norm", n0 + 5)

        last_tile = [("d", 1, 3)] * SLOTS
        take("metaT")
        chunk_order.append(("second", None, None))
        PROJ = [("dq", 0), ("dk", 4), ("dv", 8), ("dz", 12)]
        INDEX, ROT = [("iq", 4), ("ik", 1)], [("sq", 4), ("sk", 4)]
        LV = [7, 7, 4]
        units = [(n, h) for n in range(3) for h in range(SH)]
        loop_entry = {}
        expert_s = {}
        LB = dict(gather=(0, 1), up=2, hidT=3, scatter=4, down=(5, 6), out=(7, 0, 1, 2, 7, 0, 1, 2))
        L_USES = [3, 3, 3, 1, 1, 1, 1, 2]
        LEAD_BANKS = (0, 1, 4)
        L_OUT = [1, 2, 2, 2, 2, 3, 3, 3]
        as_at, t_at, x_at = [{}, {}], [{}, {}], [{}, {}]

        def unit_order():
            order = [("S", m) for m in range(AHEAD1)]
            for m in range(len(units)):
                order.append(("T", m))
                if m + AHEAD1 < len(units):
                    order.append(("S", m + AHEAD1))
                if m:
                    order.append(("V", m - 1))
            return order + [("V", len(units) - 1)]

        def rot_tiles(which):
            names = [(nm, i) for nm, cnt in which for i in range(cnt)]
            base = 0 if which is INDEX else 5
            order = []
            for j, key in enumerate(names, base):
                order.append(("proj",) + key + (j,))
                if j > base:
                    order.append(("rot2",) + names[j - 1 - base] + (j - 1,))
            return order + [("rot2",) + names[-1] + (base + len(names) - 1,)]

        for l in range(DEPTH):
            w2in = A["w_in_2"][l]
            take("sm", l)
            for what, nm, i, j in rot_tiles(INDEX):
                take(what, l, nm, i)
            for n in range(3):
                for h in range(SH):
                    take("ix", l, n, h)
            for nm, at in PROJ:
                for i in range(4):
                    take("c", l, at + i)
            for i in range(8):
                take("l2", l, i)
            for what, nm, i, j in rot_tiles(ROT):
                take(what, l, nm, i)
            for n in range(3):
                take("sv", l, n)
            lasts = dict(iq=("proj", l, "iq", 3), sq=("proj", l, "sq", 3), sk=("proj", l, "sk", 3), sv=("sv", l, 2))
            for nm, at in PROJ:
                lasts[nm] = ("c", l, at + 3)
            for turn_, nm in enumerate(("iq", "dq", "dk", "dv", "dz", "sq", "sk", "sv")):
                chunk((nm, l), [(0, 8, 512, cols(w2in, SPLIT[nm], SPLIT[nm] + 512))], lasts[nm], slot=turn_ % 4)
            take("gcc", l)
            for n in range(3):
                take("gcb", l, n)
                take("bb", l, n)
                take("KK", l, n)
                take("KQ", l, n)
                take("kt", l, n)
                take("vt", l, n)
            for lv in range(7):
                for n in range(3):
                    if lv < LV[n]:
                        as_at[l][(lv, n)] = t_at[l][(lv, n)] = sum(LV) * l + len(as_at[l]) + 1
                        if lv:
                            x_at[l][(lv, n)] = (sum(LV) - 3) * l + len(x_at[l]) + 1
                        take("X", l, lv, n)
                if lv:
                    for n in range(3):
                        if lv < LV[n]:
                            take("Y", l, lv, n)
                            take("Z", l, lv, n)
            for n in range(3):
                take("W", l, n)
            for n in range(3):
                take("vn", l, n)
                take("od", l, n)
                if n < 2:
                    take("su", l, n)
            for h in range(DH):
                take("on", l, h)
            for what, m in unit_order():
                if what != "V" or m % 2 == 0:
                    take("a" + what, l, m)
            for c in range(2):
                for i in range(4):
                    take("wo", l, 4 * c + i)
                chunk(("wo", l, c), [(0, 8, 512, cols(A["w_out_2"][l], 512 * c, 512 * c + 512))], ("wo", l, 4 * c + 3), slot=c)
            take("mu", l, 0)
            take("va", l, 0)
            take("rt", l)
            for n in range(3):
                for c in range(2):
                    take("ht", l, n, c)
            take("rk", l)
            expert_s[l] = list(slot_loads)
            loop_entry[l] = list(use)
            chunk_order.append(("experts", l, list(last_tile)))
            for s_ in range(SLOTS):
                slot_loads[s_] += 8 * (16 if s_ >= 4 else 32)
                last_tile[s_] = ("mu", l, 1)
            take("mu", l, 1)
            take("va", l, 1)
        for t in range(2):
            for c in range(2):
                take("outT", t, c)

        block = ctx.enter_context(nc.Block())

        @block.sync
        def _(sp):
            sp.dma_start(tab1[:, :], A["tables1"]).then_inc(const_in, 16)
            sp.dma_start(xin, A["x"][0].rearrange("(t p) n -> p t n", p=P)).then_inc(x_in, 16)
            sp.dma_start(memin, A["mem"][0].rearrange("(t p) n -> p t n", p=P)).then_inc(mem_in, 16)
            for n, name in enumerate(("mix_pre_g", "mix_post_g", "mem_pre_g", "mem_kv_g", "mem_post_g",
                                      "ffn_pre_g", "ffn_post_g")):
                sp.dma_start(grows[16 * n:16 * n + 16, 0, :],
                             A[name].rearrange("l (k p) -> (l k) p", p=P)).then_inc(const_in, 16)
            sp.dma_start(grows[112:113, 0, :], A["b_sub_g"]).then_inc(const_in, 16)
            for l in range(DEPTH):
                sp.dma_start(grows[0:48, 1 + l, :],
                             A["conv_w_2"][l].rearrange("w (t p) -> (w t) p", p=P)).then_inc(const_in, 16)
                sp.dma_start(grows[48:49, 1 + l, :], A["dn_norm_g_2"][l:l + 1]).then_inc(const_in, 16)
                for n, name in enumerate(("ln1_g_2", "ln1_b_2", "ln2_g_2", "ln2_b_2")):
                    sp.dma_start(grows[49 + 8 * n:57 + 8 * n, 1 + l, :],
                                 A[name][l].rearrange("(k p) -> k p", p=P)).then_inc(const_in, 16)
            sp.dma_start(pos_i[:, :], A["positions"][0:1, :].to_broadcast([P, S1])).then_inc(const_in, 16)
            for n, name in enumerate(("b_lam_q1", "b_lam_k1", "b_lam_q2", "b_lam_k2")):
                sp.dma_start(lamv[:, n, :], A[name].to_broadcast([P, HD])).then_inc(const_in, 16)
            for n, (k, src, _) in enumerate(bay_order):
                if n >= RAW:
                    b, u = tiles[bay_order[n - RAW][2]]
                    sp.wait_ge(full[b], u)
                sp.dma_start(raw[:, n % RAW, 0:k * 256].rearrange("p (k n) -> p k n", k=k), src)\
                    .then_inc(bay_loaded[n % RAW], 16)
            def narrow_weights(l):
                w = A["w_in_2"][l]
                for at, c0, n in ((0, SPLIT["ik"], 64), (64, SPLIT["ik"], 72), (136, SPLIT["db"], 8)):
                    sp.dma_start(small_w[:, :, at:at + n], cols(w, c0, c0 + n)).then_inc(small_in, 16)
                sp.dma_start(router_w[:, :, 0:4], cols(A["w_grp_2"][l], 0, 4)).then_inc(router_in, 16)
                sp.dma_start(router_w[:, :, 4:36], cols(A["w_rtr_2"][l], 0, NE)).then_inc(router_in, 16)
            for slot, parts, last, *more in chunk_order:
                if slot == "second":
                    b, u = tiles[("d", 1, 3)]
                    sp.wait_ge(full[b], u)
                    sp.dma_start(tab2[:, :], A["tables2"]).then_inc(const2_in[0], 16)
                    for l in range(DEPTH):
                        for at, name, n in ((0, "b_grp_2", 4), (4, "b_rtr_2", NE), (36, "a_log_2", 4), (40, "dt_bias_2", 4)):
                            sp.dma_start(rows2[:, l, at:at + n], A[name][l:l + 1, :].to_broadcast([P, n])).then_inc(const2_in[0], 16)
                    sp.dma_start(meta_rows, A["meta_tokens_2"]).then_inc(meta_in, 16)
                    narrow_weights(0)
                    continue
                if slot == "experts":
                    l, before = parts, last

                    def expert_loads(g):
                        for s_ in range(SLOTS):
                            if s_ < 4:
                                for at, name in ((0, "w1_2"), (2048, "w3_2")):
                                    src = A[name][l, bass.ds(g * 4 + s_, 1)].rearrange("o (k p) n -> p (o k) n", p=P)
                                    sp.dma_start(ring[:, s_, at:at + 2048].rearrange("p (k n) -> p k n", k=KT), src)\
                                        .then_inc(loaded[s_], 16)
                            else:
                                src = A["w2_2"][l, bass.ds(g * 4 + 2 * (s_ - 4), 2)].rearrange("e (k p) n -> p (e k) n", p=P)
                                sp.dma_start(ring[:, s_, :].rearrange("p (k n) -> p k n", k=4), src).then_inc(loaded[s_], 16)
                            yield s_
                    for s_ in range(4):
                        b, u = tiles[before[s_]]
                        sp.wait_ge(full[b], u)
                    b, u = tiles[("wo", l, 7)]
                    sp.wait_ge(full[b], u)
                    for _ in expert_loads(0):
                        pass
                    sp.wait_ge(steps_ready, l + 1)
                    with nc.sync.Fori(1, 8) as g:
                        end = sp.value_load(steps[0:1, l, bass.ds(g, 1)], min_val=1, max_val=1000)
                        last = sp.value_load(steps[0:1, l, bass.ds(g + 9, 1)], min_val=0, max_val=1000)
                        sp.wait_ge(loop_full[LB["up"]], last * L_USES[LB["up"]] + 1)
                        for s_ in expert_loads(g):
                            if s_ == 3:
                                sp.wait_ge(loop_full[LB["down"][1]], end)
                    if l == 0:
                        b, u = tiles[("rt", 0)]
                        sp.wait_ge(full[b], u)
                        narrow_weights(1)
                    continue
                if last is not None:
                    b, u = tiles[last]
                    sp.wait_ge(full[b], u)
                for at, k, width, src in parts:
                    sp.dma_start(ring[:, slot, at:at + k * width].rearrange("p (k n) -> p k n", k=k),
                                 src).then_inc(loaded[slot], 16)

            for t in range(2):
                sp.wait_ge(out_sb, 2 * t + 2)
                sp.dma_start(out[0, P * t:P * t + P, :], uT_flat[:, t, :]).then_inc(stored, 16)
            sp.wait_ge(stored, 32)

        @block.tensor
        def _(pe):
            def begin(*key):
                b, u = tiles[key]
                if u > 1:
                    pe.wait_ge(free[b], u - 1)
                return b

            def weights(*key):
                s, n = chunks[key]
                pe.wait_ge(loaded[s], n)
                return s

            def split_weights(*key):
                n = bay_of[key]
                pe.wait_ge(rest_ready, n + 1)
                return r12(high[:, n % HIGH, :]), r12(raw[:, n % RAW, :])

            def split_products(o, wa, xa, **kw):
                (wh, wr), (xh, xr) = wa, xa
                start, stop = kw["start"], kw["stop"]
                nc.tensor.matmul(o, wh, xh, start=start, stop=False)
                nc.tensor.matmul(o, wh, xr, start=False, stop=False)
                return nc.tensor.matmul(o, wr, xh, start=False, stop=stop)

            def project(key, src):
                w = split_weights(*key)
                b = begin(*key)
                for nt in range(2):
                    for k in range(KT):
                        at = k * 256 + nt * P
                        last = split_products(ps[:, b, nt * S1:(nt + 1) * S1], [x[:, at:at + P] for x in w],
                                              src(k), start=(k == 0), stop=(k == KT - 1))
                last.then_inc(full[b], 1)

            def project_values(key):
                w = split_weights(*key)
                b = begin(*key)
                for t in range(2):
                    for k in range(KT):
                        last = split_products(ps[:, b, t * S1:(t + 1) * S1],
                                              [r12(x[:, k, t * P:(t + 1) * P]) for x in (uH, uT)],
                                              [x[:, k * 256:k * 256 + 256] for x in w], start=(k == 0), stop=(k == KT - 1))
                last.then_inc(full[b], 1)

            def project_tok(key, slot, src, t0, tn):
                b = begin(*key)
                for k in range(KT):
                    last = nc.tensor.matmul(ps[0:tn, b, :], src[:, k, t0:t0 + tn],
                                            ring[:, slot, k * 512:k * 512 + 512], start=(k == 0), stop=(k == KT - 1))
                last.then_inc(full[b], 1)

            def sum_squares(n, sem_, base, groups, width):
                b = begin("norm", n)
                for k in range(KT):
                    if k % (KT // groups) == 0:
                        pe.wait_ge(sem_, base + k // (KT // groups) + 1)
                    last = nc.tensor.matmul(ps[:, b, 0:width], ones[:, :], sq[:, k, 0:width],
                                            start=(k == 0), stop=(k == KT - 1))
                last.then_inc(full[b], 1)

            def attention(l, kind):
                base_s = {"A": 0, "B": 20, "X": 16 if l == 0 else 28}[kind]
                for what, m in attention_order(kind):
                    if what == "S":
                        for c in range(score_tiles(kind)):
                            b = begin("S", l, kind, m, c)
                            for j in range(2):
                                o = ps[:, b, j * S1:(j + 1) * S1]
                                if kind == "X":
                                    for a in range(2):
                                        last = nc.tensor.matmul(o, qT[:, 2 * m + a, j * P:(j + 1) * P],
                                                                kT[:, 2 * m + a, :], start=(a == 0), stop=(a == 1))
                                else:
                                    ft, p0 = (m // 2, HD * (m % 2)) if kind == "A" else (m, HD * c)
                                    last = nc.tensor.matmul(o, qT[p0:p0 + HD, ft, j * P:(j + 1) * P],
                                                            kT[p0:p0 + HD, ft, :], start=True, stop=True)
                            last.then_inc(full[b], 1)
                    elif what == "T":
                        pe.wait_ge(p_ready, base_s + m + 1)
                        b = begin("T", l, kind, m)
                        s, c = place(kind, m)
                        for j in range(2):
                            for kt in range(2):
                                last = nc.tensor.transpose(ps[:, b, kt * S1 + j * P:kt * S1 + (j + 1) * P],
                                                           probs[:, s, c, j * S1 + kt * P:j * S1 + (kt + 1) * P],
                                                           ident)
                        last.then_inc(full[b], 1)
                    else:
                        pe.wait_ge(pt_ready, base_s + m + 1)
                        pT = probsT[:, m % 2, :]
                        if kind == "A":
                            p0 = HD * (m % 2)
                            b = begin("V", l, kind, m) if m % 2 == 0 else tiles[("V", l, kind, m - 1)][0]
                            for kt in range(2):
                                last = nc.tensor.matmul(ps[p0:p0 + HD, b, 0:S1], vt[:, kt, HD * m:HD * m + HD],
                                                        pT[:, kt * S1:(kt + 1) * S1], start=(kt == 0), stop=(kt == 1))
                            if m % 2:
                                last.then_inc(full[b], 1)
                        else:
                            b = begin("V", l, kind, m)
                            nv = 1 if kind == "B" else 2
                            for nt in range(nv):
                                for kt in range(2):
                                    v0 = P * (nv * m + nt)
                                    last = nc.tensor.matmul(ps[:, b, nt * S1:(nt + 1) * S1], vt[:, kt, v0:v0 + P],
                                                            pT[:, kt * S1:(kt + 1) * S1], start=(kt == 0), stop=(kt == 1))
                            last.then_inc(full[b], 1)

            pe.wait_ge(const_in, 16 * CONSTS)
            for name, src, arrived in (("xT", xin, x_in), ("memT", memin, mem_in)):
                pe.wait_ge(arrived, 16)
                for c in range(4):
                    b = begin(name, c)
                    for a in range(2):
                        for t in range(2):
                            last = nc.tensor.transpose(ps[:, b, a * S1 + t * P:a * S1 + (t + 1) * P],
                                                       src[:, t, (2 * c + a) * P:(2 * c + a + 1) * P], ident)
                    last.then_inc(full[b], 1)
            b = begin("gT")
            nc.tensor.transpose(ps[:, b, 0:113], grows[0:113, 0, :], ident[0:113, 0:113])
            for l in range(DEPTH):
                last = nc.tensor.transpose(ps[:, b, 113 + 81 * l:194 + 81 * l], grows[0:81, 1 + l, :], ident[0:81, 0:81])
            last.then_inc(full[b], 1)
            pe.wait_ge(memset_done, 1)
            sum_squares(0, pre_sq, 0, 2, S1)

            def u_of(k):
                return r12(uH[:, k, :]), r12(uT[:, k, 0:S1])

            def o_src(k):
                return r12(oH[:, k, :]), r12(oT[:, k, 0:S1])

            for l in range(DEPTH):
                kind = "AB"[l]
                n0 = 1 + 6 * l
                p0 = 1 + 3 * l

                def u_tiles(p):
                    seen = set()

                    def src(k):
                        if k % 2 == 0 and k not in seen:
                            seen.add(k)
                            pe.wait_ge(u_ready, 4 * p + k // 2 + 1)
                        return u_of(k)
                    return src

                sum_squares(n0, pre_sq, 2 * p0, 2, S1)
                src = u_tiles(p0 - 1)
                for what, g in rotary_order():
                    if what == "qk":
                        project(("qk", l, g), src)
                    else:
                        pe.wait_ge(q_raw, 8 * l + g + 1)
                        b = begin("rot", l, g)
                        qk = (qT if g < 4 else kT)[:, 2 * (g % 4):2 * (g % 4) + 2, :].rearrange("p a t -> p (a t)")
                        nc.tensor.matmul(ps[:, b, :], rot1, qk, start=True, stop=True).then_inc(full[b], 1)
                for c in range(4):
                    project_values(("v", l, c))
                pe.wait_ge(qk_ready, 8 * l + 8)
                pe.wait_ge(v_ready, 8 * l + 4)
                attention(l, kind)
                pe.wait_ge(mem_u, 4 * l + 4)
                for g in range(4):
                    project(("mk", l, g), u_of)
                    if kind == "B" and g == 0:
                        pe.wait_ge(sub_sq, 1)
                        for c in range(4):
                            b = begin("sub", c)
                            nc.tensor.matmul(ps[:, b, :].rearrange("p (a t) -> p a t", a=2), ones[:, :],
                                             sq[:, 2 * c:2 * c + 2, 0:S1], start=True, stop=True).then_inc(full[b], 1)
                if kind == "B":
                    pe.wait_ge(sub_done, 4)
                else:
                    pe.wait_ge(o_ready, 8)
                for g in range(4):
                    project(("o", l, g), o_src)
                sum_squares(n0 + 1, post_sq, 4 * (3 * l), 4, S1)
                for c in range(4):
                    if c == 3:
                        sum_squares(n0 + 2, pre_sq, 2 * (p0 + 1), 2, S1)
                    project_values(("mv", l, c))
                src = u_tiles(p0)
                for g in range(4):
                    project(("xq", l, g), src)
                pe.wait_ge(xqk_raw, 8 * l + 8)
                pe.wait_ge(v_ready, 8 * l + 8)
                attention(l, "X")
                pe.wait_ge(o_ready, O_DONE[(l, "X")])
                for g in range(4):
                    project(("xo", l, g), o_src)
                sum_squares(n0 + 3, post_sq, 4 * (3 * l + 1), 4, S1)
                sum_squares(n0 + 4, pre_sq, 2 * (p0 + 2), 2, S1)
                src = u_tiles(p0 + 1)
                for c in range(11):
                    project(("g", l, c), src)
                    project(("u", l, c), src)
                for g in range(4):
                    b = begin("d", l, g)
                    for a in range(3):
                        w = split_weights("d", l, g, a)
                        for nt in range(2):
                            for k in range(8 * a, min(8 * a + 8, FT)):
                                if g == 0 and nt == 0 and k % 2 == 0:
                                    pe.wait_ge(hid_ready, 11 * l + k // 2 + 1)
                                at = (k - 8 * a) * 256 + nt * P
                                last = split_products(ps[:, b, nt * S1:(nt + 1) * S1], [x[:, at:at + P] for x in w],
                                                      (r12(hidH(k)[:, 0, :]), r12(hid[:, k, :])),
                                                      start=(k == 0 and nt == 0), stop=(k == FT - 1 and nt == 1))
                        last.then_inc(full[b] if a == 2 else full[BANKS], 1)
                sum_squares(n0 + 5, post_sq, 4 * (3 * l + 2), 4, S1)
            pe.wait_ge(const2_in[0], 16 * 9)
            pe.wait_ge(meta_in, 16)
            b = begin("metaT")
            for k in range(KT):
                last = nc.tensor.transpose(ps[:, b, 16 * k:16 * k + 16], meta_rows[:, k * P:(k + 1) * P], ident[0:16, 0:16])
            last.then_inc(full[b], 1)

            def project2(key, slot, at, step, dst_n=S2):
                b = begin(*key)
                for k in range(KT):
                    last = nc.tensor.matmul(ps[:, b, 0:S2], ring[:, slot, at + k * step:at + k * step + P], hT[:, k, :],
                                            start=(k == 0), stop=(k == KT - 1))
                last.then_inc(full[b], 1)

            def each_head(key, fn):
                b = begin(*key)
                for h in range(DH):
                    last = fn(b, h)
                last.then_inc(full[b], 1)

            def sum_features(key, src, arrived, base, each=4):
                b = begin(*key)
                for k in range(KT):
                    if k % each == 0:
                        pe.wait_ge(arrived, base + k // each + 1)
                    last = nc.tensor.matmul(ps[:, b, 0:S2], ones[:, :], src[:, k, :], start=(k == 0), stop=(k == KT - 1))
                last.then_inc(full[b], 1)

            for l in range(DEPTH):
                if l == 0:
                    pe.wait_ge(h_ready, 12)
                    pe.wait_ge(meta_ready, 1)
                else:
                    pe.wait_ge(ln_done, 2)
                pe.wait_ge(small_in, 48 * (l + 1))
                b = begin("sm", l)
                for n, (t0, L) in enumerate(TOK):
                    for k in range(KT):
                        last = nc.tensor.matmul(ps[0:L, b, 16 * n:16 * n + 16], hT[:, k, t0:t0 + L], small_w[:, k, 128:144],
                                                start=(k == 0), stop=(k == KT - 1))
                last.then_inc(full[b], 1)
                def rotated(which):
                    for what, nm, i, j in rot_tiles(which):
                        if what == "proj":
                            if nm == "ik":
                                b = begin("proj", l, nm, i)
                                for k in range(KT):
                                    last = nc.tensor.matmul(ps[:, b, 0:S2], small_w[:, k, 0:P], hT[:, k, :], start=(k == 0), stop=(k == KT - 1))
                                last.then_inc(full[b], 1)
                            else:
                                project2(("proj", l, nm, i), weights(nm, l), i * P, 512)
                        else:
                            pe.wait_ge(raw2, 13 * l + j + 1)
                            b = begin("rot2", l, nm, i)
                            nc.tensor.matmul(ps[:, b, 0:S2], rot2, dict(sq=qs, sk=ks, iq=iq, ik=ik)[nm][:, i, :],
                                             start=True, stop=True).then_inc(full[b], 1)

                rotated(INDEX)
                pe.wait_ge(rot_done, 13 * l + 5)
                for n, (t0, L) in enumerate(TOK):
                    for h in range(SH):
                        p0 = HD * (h % 2)
                        b = begin("ix", l, n, h)
                        nc.tensor.matmul(ps[0:L, b, 0:S2], iq[p0:p0 + HD, h // 2, t0:t0 + L], ik[p0:p0 + HD, 0, :],
                                         start=True, stop=True).then_inc(full[b], 1)
                for nm, at in PROJ:
                    s = weights(nm, l)
                    for i in range(4):
                        project2(("c", l, at + i), s, i * P, 512)
                for i in range(8):
                    pe.wait_ge(l2_sq, 8 * l + i + 1)
                    b = begin("l2", l, i)
                    nc.tensor.matmul(ps[:, b, 0:S2], ones[:, :], sq[:, i, :], start=True, stop=True).then_inc(full[b], 1)
                rotated(ROT)
                s = weights("sv", l)
                for n, (t0, L) in enumerate(TOK):
                    project_tok(("sv", l, n), s, hT, t0, L)
                pe.wait_ge(gb_ready, l + 1)
                b = begin("gcc", l)
                for n, (t0, L) in enumerate(TOK):
                    last = nc.tensor.matmul(ps[0:L, b, 4 * n:4 * n + 4], triu[0:L, 0:L], g_tok[0:L, n, :], start=True, stop=True)
                last.then_inc(full[b], 1)
                pe.wait_ge(conv_out, 12 * l + 12)
                pe.wait_ge(qk_unit, 8 * l + 8)
                for n, (t0, L) in enumerate(TOK):
                    each_head(("gcb", l, n), lambda b, h: nc.tensor.matmul(
                        ps[:, b, h * P:h * P + L], g_tok[0:L, n, h:h + 1].broadcast_to([L, P]), triu[0:L, 0:L], start=True, stop=True))
                    each_head(("bb", l, n), lambda b, h: nc.tensor.matmul(
                        ps[:, b, h * P:h * P + L], beta[0:L, n, h:h + 1].broadcast_to([L, P]), ident[0:L, 0:L], start=True, stop=True))
                    each_head(("KK", l, n), lambda b, h: nc.tensor.matmul(
                        ps[0:L, b, h * P:h * P + L], cv_qk[:, 4 + h, t0:t0 + L], cv_qk[:, 4 + h, t0:t0 + L], start=True, stop=True))
                    each_head(("KQ", l, n), lambda b, h: nc.tensor.matmul(
                        ps[0:L, b, h * P:h * P + L], cv_qk[:, 4 + h, t0:t0 + L], cv_qk[:, h, t0:t0 + L], start=True, stop=True))
                    each_head(("kt", l, n), lambda b, h: nc.tensor.transpose(
                        ps[0:L, b, h * P:(h + 1) * P], cv_qk[:, 4 + h, t0:t0 + L], ident))
                    each_head(("vt", l, n), lambda b, h: nc.tensor.transpose(
                        ps[0:L, b, h * P:(h + 1) * P], cv_v[:, h, t0:t0 + L], ident))
                asn, tn, xn = as_at[l], t_at[l], x_at[l]
                for lv in range(7):
                    live = [n for n in range(3) if lv < LV[n]]
                    for n in live:
                        L = TOK[n][1]
                        pe.wait_ge(as_ready, asn[(lv, n)])
                        if lv:
                            pe.wait_ge(t_ready, tn[(lv - 1, n)])
                        each_head(("X", l, lv, n), lambda b, h: nc.tensor.matmul(
                            ps[0:L, b, h * P:h * P + L], As[0:L, n, h * P:h * P + L],
                            ident[0:L, 0:L] if lv == 0 else Tm[0:L, n, h * P:h * P + L], start=True, stop=True))
                    if lv:
                        for n in live:
                            L = TOK[n][1]
                            pe.wait_ge(x_sb, xn[(lv, n)])
                            each_head(("Y", l, lv, n), lambda b, h: nc.tensor.matmul(
                                ps[0:L, b, h * P:h * P + L], TT[0:L, n, h * P:h * P + L], Xs[0:L, n, h * P:h * P + L], start=True, stop=True))
                            each_head(("Z", l, lv, n), lambda b, h: nc.tensor.matmul(
                                ps[0:L, b, h * P:h * P + L], Xs[0:L, n, h * P:h * P + L], TT[0:L, n, h * P:h * P + L], start=True, stop=True))
                pe.wait_ge(t_ready, sum(LV) * (l + 1))
                for n, (t0, L) in enumerate(TOK):
                    pe.wait_ge(kbe_ready, 3 * l + n + 1)
                    each_head(("W", l, n), lambda b, h: nc.tensor.matmul(
                        ps[:, b, h * P:h * P + L], k_be[0:L, n, h * P:(h + 1) * P], TT[0:L, n, h * P:h * P + L], start=True, stop=True))
                pe.wait_ge(tokens_ready, l + 1)
                for n, (t0, L) in enumerate(TOK):
                    if n:
                        pe.wait_ge(w_ready, 3 * l + n + 1)
                        pe.wait_ge(state_ready, 2 * l + n)

                    def new_values(b, h):
                        o = ps[0:L, b, h * P:(h + 1) * P]
                        last = nc.tensor.matmul(o, TT[0:L, n, h * P:h * P + L], v_beta[0:L, n, h * P:(h + 1) * P], start=True, stop=(n == 0))
                        if n:
                            last = nc.tensor.matmul(o, w_T[:, n, h * P:h * P + L], state[:, h * P:(h + 1) * P], start=False, stop=True)
                        return last
                    each_head(("vn", l, n), new_values)
                    pe.wait_ge(vn_ready, 3 * l + n + 1)

                    def outputs(b, h):
                        o = ps[:, b, h * P:h * P + L]
                        if n:
                            nc.tensor.matmul(o, state[:, h * P:(h + 1) * P], cv_qk[:, h, t0:t0 + L], start=True, stop=False)
                        return nc.tensor.matmul(o, v_new[0:L, h * P:(h + 1) * P], QK[0:L, n, h * P:h * P + L], start=(n == 0), stop=True)
                    each_head(("od", l, n), outputs)
                    if n < 2:
                        each_head(("su", l, n), lambda b, h: nc.tensor.matmul(
                            ps[:, b, h * P:(h + 1) * P], k_tok[0:L, n, h * P:(h + 1) * P], v_new[0:L, h * P:(h + 1) * P], start=True, stop=True))
                pe.wait_ge(on_sq, l + 1)
                for h in range(DH):
                    b = begin("on", l, h)
                    nc.tensor.matmul(ps[:, b, 0:S2], ones[:, :], sq[:, h, :], start=True, stop=True).then_inc(full[b], 1)
                pe.wait_ge(rot_done, 13 * l + 13)
                pe.wait_ge(vs_ready, 3 * l + 3)
                for what, m in unit_order():
                    n, h = units[m]
                    t0, L = TOK[n]
                    p0 = HD * (h % 2)
                    if what == "S":
                        b = begin("aS", l, m)
                        nc.tensor.matmul(ps[0:L, b, 0:t0 + L], qs[p0:p0 + HD, h // 2, t0:t0 + L], ks[p0:p0 + HD, h // 2, 0:t0 + L],
                                         start=True, stop=True).then_inc(full[b], 1)
                    elif what == "T":
                        pe.wait_ge(p2, 24 * l + m + 1)
                        b = begin("aT", l, m)
                        for kt in range(n + 1):
                            kl = TOK[kt][1]
                            last = nc.tensor.transpose(ps[0:kl, b, kt * P:kt * P + L], probs2[0:L, m % AHEAD1, kt * P:kt * P + kl], ident[0:L, 0:L])
                        last.then_inc(full[b], 1)
                    else:
                        pe.wait_ge(pt2, 24 * l + m + 1)
                        b = begin("aV", l, m) if m % 2 == 0 else tiles[("aV", l, m - 1)][0]
                        for kt in range(n + 1):
                            kl = TOK[kt][1]
                            last = nc.tensor.matmul(ps[p0:p0 + HD, b, 0:L], vs[0:kl, kt, HD * h:HD * h + HD], probsT2[0:kl, m % 2, kt, 0:L],
                                                    start=(kt == 0), stop=(kt == n))
                        if m % 2:
                            last.then_inc(full[b], 1)
                pe.wait_ge(dn_done, 4 * l + 4)
                pe.wait_ge(sa_ready, 12 * l + 12)
                for c in range(2):
                    s = weights("wo", l, c)
                    for i in range(4):
                        b = begin("wo", l, 4 * c + i)
                        for k in range(KT):
                            last = nc.tensor.matmul(ps[:, b, 0:S2], ring[:, s, k * 512 + i * P:k * 512 + i * P + P], oT[:, k, :],
                                                    start=(k == 0), stop=(k == KT - 1))
                        last.then_inc(full[b], 1)
                sum_features(("mu", l, 0), hT, mix_ready, 9 * l, each=1)
                sum_features(("va", l, 0), sq, ln_sq, 4 * l)
                pe.wait_ge(ln_done, 2 * l + 1)
                pe.wait_ge(router_in, 32 * (l + 1))
                b = begin("rt", l)
                for n, (t0, L) in enumerate(TOK):
                    for k in range(KT):
                        last = nc.tensor.matmul(ps[0:L, b, 36 * n:36 * n + 36], hT[:, k, t0:t0 + L], router_w[:, k, :],
                                                start=(k == 0), stop=(k == KT - 1))
                last.then_inc(full[b], 1)
                for n, (t0, L) in enumerate(TOK):
                    for c in range(2):
                        b = begin("ht", l, n, c)
                        for k in range(4):
                            last = nc.tensor.transpose(ps[0:L, b, k * P:(k + 1) * P], hT[:, 4 * c + k, t0:t0 + L], ident)
                        last.then_inc(full[b], 1)
                pe.wait_ge(comb_ready, l + 1)
                b = begin("rk", l)
                for a, (_, La) in enumerate(TOK):
                    for a1 in range(a + 1):
                        last = nc.tensor.matmul(ps[0:La, b, a * NE:(a + 1) * NE], (strict if a1 == a else ones)[0:TOK[a1][1], 0:La],
                                                chosen[0:TOK[a1][1], a1, :], start=(a1 == 0), stop=(a1 == a))
                for a, (_, La) in enumerate(TOK):
                    last = nc.tensor.matmul(ps[:, b, 3 * NE:4 * NE], ones[0:La, :], chosen[0:La, a, :], start=(a == 0), stop=(a == 2))
                last.then_inc(full[b], 1)
                for b in range(BANKS):
                    pe.wait_ge(free[b], loop_entry[l][b])
                pe.wait_ge(steps_ready, l + 1)
                pe.wait_ge(htok_ready, 6 * (l + 1))
                extra = lambda b: l + 1 if b in LEAD_BANKS else 0

                def begin_l(b, before):
                    pe.wait_ge(loop_free[b], before + 1)
                    return b

                def gather(before):
                    for a in range(2):
                        b = begin_l(LB["gather"][a], before(LB["gather"][a]))
                        for k in range(4):
                            for n, (t0, L) in enumerate(TOK):
                                last = nc.tensor.matmul(ps[:, b, k * P:(k + 1) * P], h_tok[0:L, n, (4 * a + k) * P:(4 * a + k + 1) * P],
                                                        sel[0:L, n, :], start=(n == 0), stop=(n == 2))
                        last.then_inc(loop_full[b], 1)
                    b = begin_l(LB["scatter"], before(LB["scatter"]))
                    for n, (t0, L) in enumerate(TOK):
                        last = nc.tensor.transpose(ps[:, b, t0:t0 + L], sel_gate[0:L, n, :], ident[0:L, 0:L])
                    last.then_inc(loop_full[b], 1)

                start = pe.value_load(steps[0:1, l, 0:1], min_val=0, max_val=MAX_STEPS // 2)
                stop = pe.value_load(steps[0:1, l, 8:9], min_val=1, max_val=MAX_STEPS - 1)
                pe.wait_ge(sel_ready, start + (l + 1))
                gather(lambda b: start * L_USES[b] + l)
                with nc.tensor.Fori(start, stop) as s:
                    g = pe.value_load(step_group[0:1, bass.ds(s, 1)], min_val=0, max_val=7)
                    b = begin_l(LB["up"], s * L_USES[LB["up"]])
                    for j in range(4):
                        pe.wait_ge(loaded[j], g * 32 + (expert_s[l][j] + 32))
                    for k in range(KT):
                        if k % 4 == 0:
                            pe.wait_ge(xg_ready, s * 2 + (2 * l + k // 4 + 1))
                        for j in range(4):
                            last = nc.tensor.matmul(ps[32 * j:32 * j + 32, b, :].rearrange("p (a n) -> p a n", a=2),
                                                    x_g[:, k, 32 * j:32 * j + 32],
                                                    ring[:, j, :].rearrange("p (a k n) -> p k a n", a=2, k=KT)[:, k],
                                                    start=(k == 0), stop=(k == KT - 1))
                    last.then_inc(loop_full[b], 1)
                    pe.wait_ge(sel_ready, s + (l + 2))
                    gather(lambda b: s * L_USES[b] + extra(b))
                    pe.wait_ge(ehid_ready, s + 1)
                    b = begin_l(LB["hidT"], s)
                    for f in range(2):
                        last = nc.tensor.transpose(ps[:, b, f * P:(f + 1) * P], e_hid[:, f * P:(f + 1) * P], ident)
                    last.then_inc(loop_full[b], 1)
                    for s_ in (4, 5):
                        pe.wait_ge(loaded[s_], g * 16 + (expert_s[l][s_] + 16))
                    pe.wait_ge(ehidT_ready, s + 1)
                    for a in range(2):
                        b = begin_l(LB["down"][a], s)
                        for f in range(2):
                            for j in range(4):
                                at = ((j % 2) * 2 + f) * DM + a * 512
                                last = nc.tensor.matmul(ps[32 * j:32 * j + 32, b, :], e_hidT[:, f, 32 * j:32 * j + 32],
                                                        ring[:, 4 + j // 2, at:at + 512], start=(f == 0), stop=(f == 1))
                        last.then_inc(loop_full[b], 1)
                    pe.wait_ge(scatter_ready, s + 1)
                    for i in range(KT):
                        if i % 4 == 0:
                            pe.wait_ge(eout_ready, s * 2 + (i // 4 + 1))
                        b = begin_l(LB["out"][i], s * L_USES[LB["out"][i]] + (extra(LB["out"][i]) + L_OUT[i] - 1))
                        nc.tensor.matmul(ps[:, b, 0:S2], e_out[:, i * P:(i + 1) * P], scatter[:, :], start=True, stop=True)\
                            .then_inc(loop_full[b], 1)
                sum_features(("mu", l, 1), yacc, mix_ready, 9 * l + 8, each=KT)
                sum_features(("va", l, 1), sq, ln_sq, 4 * l + 2)
            pe.wait_ge(ln_done, 4)
            for t in range(2):
                for c in range(2):
                    b = begin("outT", t, c)
                    for a in range(4):
                        last = nc.tensor.transpose(ps[:, b, a * P:(a + 1) * P],
                                                   hx[:, 4 * c + a, t * P:(t + 1) * P], ident)
                    last.then_inc(full[b], 1)

        @block.scalar
        def _(act):
            def filled(*key):
                b, u = tiles[key]
                act.wait_ge(full[b], u)
                return b

            split = [0]

            def high_until(last):
                while split[0] < len(bay_order):
                    n = split[0]
                    if last is not None and n >= HIGH and n - HIGH > max(i for i, c in enumerate(bay_order) if c[2] == last):
                        return
                    if last is None and n >= HIGH:
                        return
                    if n >= HIGH:
                        b, u = tiles[bay_order[n - HIGH][2]]
                        act.wait_ge(full[b], u)
                    act.wait_ge(bay_loaded[n % RAW], 16 * (n // RAW + 1))
                    w = bay_order[n][0] * 256
                    nc.scalar.activation(r12(high[:, n % HIGH, 0:w]), raw[:, n % RAW, 0:w], ACT.Copy).then_inc(high_ready, 1)
                    split[0] += 1

            def squares_of(src, width, sem_, arrived=None):
                for a in range(2):
                    if arrived is not None:
                        act.wait_ge(h_ready, arrived + a + 1)
                    nc.scalar.activation(sq[:, 4 * a:4 * a + 4, 0:width], src[:, 4 * a:4 * a + 4, :],
                                         ACT.Square).then_inc(sem_, 1)

            def root(key, width, scale, eps, dst):
                b = filled(*key)
                nc.scalar.activation(dst, ps[:, b, 0:width], ACT.Sqrt, bias=eps, scale=scale).then_inc(free[b], 1)

            def norm_root(n):
                root(("norm", n), S1, 1.0 / DM, eps6[:, :], std[:, 0:S1])
                nc.scalar.drain().then_inc(std_ready, 1)

            def value_out(name, l, c):
                b = filled(name, l, c)
                nc.scalar.activation(vt[:, :, 256 * c:256 * c + 256], ps[:, b, :].rearrange("p (t n) -> p t n", t=2),
                                     ACT.Copy).then_inc(v_ready, 1)
                nc.scalar.drain().then_inc(free[b], 1)
                high_until((name, l, c))

            def branch_out(name, l):
                for g in range(4):
                    if name == "d":
                        for a in range(2):
                            high_until(("part", l, g, a))
                    b = filled(name, l, g)
                    y = ps[:, b, :].rearrange("p (a t) -> p a t", a=2)
                    nc.scalar.activation(yT[:, 2 * g:2 * g + 2, 0:S1], y, ACT.Copy)
                    nc.scalar.activation(sq[:, 2 * g:2 * g + 2, 0:S1], y, ACT.Square).then_inc(post_sq, 1)
                    nc.scalar.drain().then_inc(free[b], 1)
                    if g < 3:
                        high_until((name, l, g))

            def attention(l, kind):
                base = {"A": 0, "B": 20, "X": 16 if l == 0 else 28}[kind]
                scale = 1.0 / 16 if kind == "X" else 0.125
                n = items(kind)

                def exps(m):
                    act.wait_ge(max_ready, base + m + 1)
                    for t in range(score_tiles(kind)):
                        s, c = place(kind, m, t)
                        if kind != "A":
                            b = filled("S", l, kind, m, t)
                        for j in range(2):
                            p = probs[:, s, c, j * S1:(j + 1) * S1]
                            src = p if kind == "A" else ps[:, b, j * S1:(j + 1) * S1]
                            nc.scalar.activation(p, src, ACT.Exp, bias=nmax[:, s, c, j:j + 1], scale=scale,
                                                 accum_out=den[:, s, c, j:j + 1])
                        if kind != "A":
                            nc.scalar.drain().then_inc(free[b], 1)
                    nc.scalar.drain().then_inc(exp_ready, 1)

                for m in range(min(ahead(kind), n)):
                    exps(m)
                for m in range(n):
                    b = filled("T", l, kind, m)
                    nc.scalar.activation(probsT[:, m % 2, :], ps[:, b, :], ACT.Copy).then_inc(pt_ready, 1)
                    nc.scalar.drain().then_inc(free[b], 1)
                    if m + ahead(kind) < n:
                        exps(m + ahead(kind))

            act.wait_ge(memset_done, 2)
            for c in range(4):
                b = filled("xT", c)
                nc.scalar.activation(hx[:, 2 * c:2 * c + 2, :], ps[:, b, :].rearrange("p (a t) -> p a t", a=2),
                                     ACT.Copy).then_inc(x_ready, 1)
                nc.scalar.drain().then_inc(free[b], 1)
            for c in range(4):
                b = filled("memT", c)
                nc.scalar.activation(memn[:, 2 * c:2 * c + 2, :], ps[:, b, :].rearrange("p (a t) -> p a t", a=2),
                                     ACT.Copy)
                nc.scalar.drain().then_inc(free[b], 1)
            b = filled("gT")
            nc.scalar.activation(gains[:, :], ps[:, b, 0:275], ACT.Copy).then_inc(gain_cols, 1)
            nc.scalar.drain().then_inc(free[b], 1)
            squares_of(memn, S1, pre_sq)
            norm_root(0)
            for l in range(DEPTH):
                kind = "AB"[l]
                n0 = 1 + 6 * l
                squares_of(hx, S1, pre_sq, 6 * l - 2 if l else None)
                if l == 0:
                    high_until(None)
                    act.wait_ge(memn_ready, 1)
                norm_root(n0)
                if l == 0:
                    act.wait_ge(rope_args, 1)
                    nc.scalar.activation(rope[:, :, :], rope[:, :, :], ACT.Sin).then_inc(rope_ready, 1)
                    act.wait_ge(lam_args, 1)
                    nc.scalar.activation(lam_parts[:, 2:4], lam_parts[:, 0:2], ACT.Exp).then_inc(lam_exp, 1)
                for g in range(8):
                    b = filled("qk", l, g)
                    dst = (qT if g < 4 else kT)[:, 2 * (g % 4):2 * (g % 4) + 2, :].rearrange("p a t -> p (a t)")
                    nc.scalar.activation(dst, ps[:, b, :], ACT.Copy).then_inc(q_raw, 1)
                    nc.scalar.drain().then_inc(free[b], 1)
                    high_until(("qk", l, g))
                for c in range(4):
                    value_out("v", l, c)
                attention(l, kind)
                if kind == "B":
                    act.wait_ge(o_ready, O_DONE[(l, kind)])
                    for a in range(2):
                        ins = nc.scalar.activation(sq[:, 4 * a:4 * a + 4, 0:S1], oT[:, 4 * a:4 * a + 4, 0:S1], ACT.Square)
                    ins.then_inc(sub_sq, 1)
                for g in range(4):
                    b = filled("mk", l, g)
                    dst = kT[:, 2 * g:2 * g + 2, :].rearrange("p a t -> p (a t)")
                    nc.scalar.activation(dst, ps[:, b, :], ACT.Copy).then_inc(xqk_raw, 1)
                    nc.scalar.drain().then_inc(free[b], 1)
                    if kind == "B" and g == 0:
                        for c in range(4):
                            b = filled("sub", c)
                            nc.scalar.activation(yT[:, 2 * c:2 * c + 2, 0:S1], ps[:, b, :].rearrange("p (a t) -> p a t", a=2),
                                                 ACT.Sqrt, bias=eps6[:, :], scale=1.0 / P).then_inc(sub_std, 1)
                            nc.scalar.drain().then_inc(free[b], 1)
                    high_until(("mk", l, g))
                branch_out("o", l)
                norm_root(n0 + 1)
                high_until(("o", l, 3))
                for c in range(4):
                    value_out("mv", l, c)
                    if c == 1:
                        squares_of(hx, S1, pre_sq, 6 * l)
                    if c == 2:
                        norm_root(n0 + 2)
                for g in range(4):
                    b = filled("xq", l, g)
                    dst = qT[:, 2 * g:2 * g + 2, :].rearrange("p a t -> p (a t)")
                    nc.scalar.activation(dst, ps[:, b, :], ACT.Copy).then_inc(xqk_raw, 1)
                    nc.scalar.drain().then_inc(free[b], 1)
                    high_until(("xq", l, g))
                attention(l, "X")
                branch_out("xo", l)
                norm_root(n0 + 3)
                high_until(("xo", l, 3))
                squares_of(hx, S1, pre_sq, 6 * l + 2)
                norm_root(n0 + 4)
                for c in range(11):
                    b = filled("g", l, c)
                    nc.scalar.activation(hid[:, 2 * c:2 * c + 2, :], ps[:, b, :].rearrange("p (a t) -> p a t", a=2),
                                         ACT.Silu).then_inc(silu_ready, 1)
                    nc.scalar.drain().then_inc(free[b], 1)
                    high_until(("g", l, c))
                branch_out("d", l)
                norm_root(n0 + 5)
                high_until(("d", l, 3))
            b = filled("metaT")
            nc.scalar.activation(hT[:, :, 0:META], ps[:, b, 0:128].rearrange("p (k t) -> p k t", k=KT), ACT.Copy).then_inc(meta_ready, 1)
            nc.scalar.drain().then_inc(free[b], 1)
            act.wait_ge(zeros2, 1)

            def copy_out(key, dst, src, sem_, **kw):
                b = filled(*key)
                nc.scalar.activation(dst, src(b), ACT.Copy, **kw).then_inc(sem_, 1)
                nc.scalar.drain().then_inc(free[b], 1)

            def h4(b, L0, L1):
                return heads(ps[:, b, :])[0:L0, :, 0:L1]

            for l in range(DEPTH):
                b = filled("sm", l)
                nc.scalar.activation(tok[:, 0:2, :], ps[:, b, 0:32].rearrange("p (n c) -> p n c", n=2), ACT.Copy)
                nc.scalar.activation(tok[0:16, 2, :], ps[0:16, b, 32:48], ACT.Copy).then_inc(tok_ready, 1)
                nc.scalar.drain().then_inc(free[b], 1)
                act.wait_ge(sp_args, l + 1)
                nc.scalar.activation(gate_exp[:, :, :], gate_log[:, :, :], ACT.Exp)
                nc.scalar.activation(neg_a[:, :], rows2[:, l, 36:40], ACT.Exp)
                nc.scalar.drain()
                nc.scalar.activation(gate_log[:, :, 0:4], gate_exp[:, :, 0:4], ACT.Ln, bias=1.0).then_inc(sp_logs, 1)
                for what, nm, i, j in [t for t in rot_tiles(INDEX) if t[0] == "proj"]:
                    copy_out(("proj", l, nm, i), dict(sq=qs, sk=ks, iq=iq, ik=ik)[nm][:, i, :], lambda b: ps[:, b, 0:S2], raw2)
                for n, (t0, L) in enumerate(TOK):
                    for h in range(SH):
                        i = 24 * l + 8 * n + h
                        b = filled("ix", l, n, h)
                        if i >= 2:
                            act.wait_ge(relu_used, i - 1)
                        nc.scalar.activation(relu_s[0:L, h % 2, :], ps[0:L, b, 0:S2], ACT.Relu, scale=0.125).then_inc(relu_ready, 1)
                        nc.scalar.drain().then_inc(free[b], 1)

                for i in range(12):
                    copy_out(("c", l, i), conv_in[:, i, 3:3 + S2], lambda b: ps[:, b, 0:S2], conv_raw)
                for i in range(4):
                    b = filled("c", l, 12 + i)
                    nc.scalar.activation(z_gate[:, i, :], ps[:, b, 0:S2], ACT.Silu).then_inc(free[b], 1)
                for i in range(12):
                    act.wait_ge(conv_acc, 12 * l + i + 1)
                    x = cv_qk[:, i, :] if i < 8 else cv_v[:, i - 8, :]
                    nc.scalar.activation(x, x, ACT.Silu).then_inc(conv_out, 1)
                    if i < 8:
                        nc.scalar.drain()
                        nc.scalar.activation(sq[:, i, :], x, ACT.Square).then_inc(l2_sq, 1)
                for i in range(8):
                    b = filled("l2", l, i)
                    nc.scalar.activation(yT[:, i, :], ps[:, b, 0:S2], ACT.Sqrt, bias=(eps128 if i < 4 else eps6)[:, :],
                                         scale=128.0 if i < 4 else 1.0).then_inc(l2_root, 1)
                    nc.scalar.drain().then_inc(free[b], 1)
                for what, nm, i, j in [t for t in rot_tiles(ROT) if t[0] == "proj"]:
                    copy_out(("proj", l, nm, i), dict(sq=qs, sk=ks, iq=iq, ik=ik)[nm][:, i, :], lambda b: ps[:, b, 0:S2], raw2)
                for n, (t0, L) in enumerate(TOK):
                    copy_out(("sv", l, n), vs[0:L, n, :], lambda b: ps[0:L, b, :], vs_ready)
                for n, (t0, L) in enumerate(TOK):
                    act.wait_ge(decay_args, 3 * l + n + 1)
                    d = heads(decay)[0:L, :, 0:L]
                    nc.scalar.activation(d, d, ACT.Exp).then_inc(decay_ready, 1)
                    b = filled("gcb", l, n)
                    nc.scalar.activation(heads(egc)[:, :, 0:L], h4(b, P, L), ACT.Exp).then_inc(egc_ready, 1)
                    nc.scalar.drain().then_inc(free[b], 1)
                    act.wait_ge(qk_dec, 3 * l + n + 1)
                act.wait_ge(cum_ready, l + 1)
                nc.scalar.activation(ecum[:, :, :], cum[:, :, :], ACT.Exp).then_inc(ecum_ready, 1)
                for lv in range(1, 7):
                    for n in range(3):
                        if lv < LV[n]:
                            L = TOK[n][1]
                            copy_out(("X", l, lv, n), heads(Xs[:, n, :])[0:L, :, 0:L], lambda b: h4(b, L, L), x_sb)
                for n, (t0, L) in enumerate(TOK):
                    copy_out(("W", l, n), heads(w_T[:, n, :])[:, :, 0:L], lambda b: h4(b, P, L), w_ready, scale=-1.0)
                for n, (t0, L) in enumerate(TOK):
                    copy_out(("vn", l, n), heads(v_new)[0:L], lambda b: h4(b, L, P), vn_ready)
                    copy_out(("od", l, n), oT[:, 0:4, t0:t0 + L], lambda b: h4(b, P, L), od_ready)
                nc.scalar.activation(sq[:, 0:4, :], oT[:, 0:4, :], ACT.Square).then_inc(on_sq, 1)
                for h in range(DH):
                    b = filled("on", l, h)
                    nc.scalar.activation(yT[:, h, :], ps[:, b, 0:S2], ACT.Sqrt, bias=eps6[:, :], scale=1.0 / P).then_inc(on_root, 1)
                    nc.scalar.drain().then_inc(free[b], 1)
                def exp_unit(m):
                    n, h = units[m]
                    t0, L = TOK[n]
                    act.wait_ge(max2, 24 * l + m + 1)
                    p = probs2[0:L, m % AHEAD1, 0:t0 + L]
                    nc.scalar.activation(p, p, ACT.Exp, bias=stat2[0:L, 1, m % AHEAD1:m % AHEAD1 + 1], scale=0.125,
                                         accum_out=stat2[0:L, 2, m % AHEAD1:m % AHEAD1 + 1])
                    nc.scalar.drain().then_inc(exp2, 1)
                for m in range(AHEAD):
                    exp_unit(m)
                for m in range(24):
                    n, h = units[m]
                    L = TOK[n][1]
                    b = filled("aT", l, m)
                    full_tiles = min(n + 1, 2)
                    ins = nc.scalar.activation(probsT2[:, m % 2, 0:full_tiles, 0:L],
                                               ps[:, b, 0:full_tiles * P].rearrange("p (k t) -> p k t", k=full_tiles)[:, :, 0:L], ACT.Copy)
                    if n == 2:
                        ins = nc.scalar.activation(probsT2[0:16, m % 2, 2, 0:L], ps[0:16, b, 2 * P:2 * P + L], ACT.Copy)
                    ins.then_inc(pt2, 1)
                    nc.scalar.drain().then_inc(free[b], 1)
                    if m + AHEAD < 24:
                        exp_unit(m + AHEAD)

                def layer_norm_act(j, src):
                    b = filled("mu", l, j)
                    nc.scalar.activation(std[:, :], ps[:, b, 0:S2], ACT.Copy, scale=1.0 / DM).then_inc(mean_ready, 1)
                    nc.scalar.drain().then_inc(free[b], 1)
                    for a in range(2):
                        act.wait_ge(cent_ready, 4 * l + 2 * j + a + 1)
                        nc.scalar.activation(sq[:, 4 * a:4 * a + 4, :], src[:, 4 * a:4 * a + 4, :], ACT.Square).then_inc(ln_sq, 1)
                    b = filled("va", l, j)
                    nc.scalar.activation(std[:, :], ps[:, b, 0:S2], ACT.Sqrt, bias=eps5[:, :], scale=1.0 / DM).then_inc(ln_root, 1)
                    nc.scalar.drain().then_inc(free[b], 1)
                layer_norm_act(0, hT)
                for n, (t0, L) in enumerate(TOK):
                    for c in range(2):
                        copy_out(("ht", l, n, c), h_tok[0:L, n, 512 * c:512 * c + 512], lambda b: ps[0:L, b, :], htok_ready)
                act.wait_ge(rt_args, l + 1)
                nc.scalar.activation(rexp[:, :, 0:5], rexp[:, :, 0:5], ACT.Exp).then_inc(rt_exp, 1)
                act.wait_ge(steps_ready, l + 1)
                extra = lambda b: l + 1 if b in LEAD_BANKS else 0

                def copy_l(b, use_, dst, src, sem_):
                    act.wait_ge(loop_full[b], use_)
                    nc.scalar.activation(dst, src, ACT.Copy).then_inc(sem_, 1)
                    nc.scalar.drain().then_inc(loop_free[b], 1)

                def gathered(use_of):
                    for a in range(2):
                        b = LB["gather"][a]
                        copy_l(b, use_of(b), x_g[:, 4 * a:4 * a + 4, :], ps[:, b, :].rearrange("p (k c) -> p k c", k=4), xg_ready)

                start = act.value_load(steps[0:1, l, 0:1], min_val=0, max_val=MAX_STEPS // 2)
                stop = act.value_load(steps[0:1, l, 8:9], min_val=1, max_val=MAX_STEPS - 1)
                gathered(lambda b: start * L_USES[b] + (l + 1))
                with nc.scalar.Fori(start, stop) as s:
                    b = LB["up"]
                    act.wait_ge(loop_full[b], s * L_USES[b] + 1)
                    nc.scalar.activation(e_silu[:, :], ps[:, b, 0:DE], ACT.Silu).then_inc(esilu_ready, 1)
                    b = LB["scatter"]
                    copy_l(b, s + (l + 1), scatter[:, :], ps[:, b, 0:S2], scatter_ready)
                    gathered(lambda b: s * L_USES[b] + (l + 2))
                    b = LB["hidT"]
                    copy_l(b, s + 1, e_hidT[:, :, :], ps[:, b, 0:2 * P].rearrange("p (f c) -> p f c", f=2), ehidT_ready)
                    for a in range(2):
                        b = LB["down"][a]
                        copy_l(b, s + 1, e_out[:, 512 * a:512 * a + 512], ps[:, b, :], eout_ready)
                b = LB["scatter"]
                act.wait_ge(loop_full[b], stop + (l + 1))
                nc.scalar.activation(e_silu[:, 0:1], ps[:, b, 0:1], ACT.Copy).then_inc(loop_free[b], 1)
                layer_norm_act(1, yacc)

            for t in range(2):
                for c in range(2):
                    b = filled("outT", t, c)
                    nc.scalar.activation(uT_flat[:, t, 512 * c:512 * c + 512], ps[:, b, :], ACT.Copy).then_inc(out_sb, 1)

        @block.gpsimd
        def _(pool):
            for n, (k, _, _) in enumerate(bay_order):
                pool.wait_ge(high_ready, n + 1)
                w = raw[:, n % RAW, 0:k * 256]
                nc.gpsimd.tensor_tensor(r12(w), w, r12(high[:, n % HIGH, 0:k * 256]).bitcast(F32), ALU.subtract).then_inc(rest_ready, 1)
            for l in range(DEPTH):
                if l == 0:
                    pool.wait_ge(const2_in[0], 16 * 9)
                for lv in range(7):
                    for n in range(3):
                        if lv >= LV[n]:
                            continue
                        L = TOK[n][1]
                        if lv == 0:
                            pool.wait_ge(lt_ready, 3 * l + n + 1)
                        else:
                            b, u = tiles[("X", l, lv - 1, n)]
                            pool.wait_ge(full[b], u)
                            if lv == 1:
                                pool.wait_ge(t_ready, t_at[l][(0, n)])
                        nc.gpsimd.tensor_tensor(heads(As[:, n, :])[0:L, :, 0:L], heads(LT[:, n, :])[0:L, :, 0:L],
                                                levels[0:L, lv, 0:L].unsqueeze(1).broadcast_to([L, DH, L]), ALU.mult).then_inc(as_ready, 1)

        @block.vector
        def _(dve):
            def settle():
                nc.vector.drain()

            def filled(*key):
                b, u = tiles[key]
                dve.wait_ge(full[b], u)
                return b

            def over(x, n):
                return x.unsqueeze(1).broadcast_to([P, n, x.shape[-1]])

            def split_in_place(x, xh):
                settle()
                nc.vector.tensor_copy(r12(xh), x)
                settle()
                return nc.vector.tensor_tensor(r12(x), x, r12(xh).bitcast(F32), ALU.subtract)

            def split_out(x, xh, src):
                settle()
                nc.vector.tensor_copy(r12(xh), src)
                settle()
                return nc.vector.tensor_tensor(r12(x), src, r12(xh).bitcast(F32), ALU.subtract)

            def pre_norm(n, col):
                settle()
                dve.wait_ge(std_ready, n + 1)
                nc.vector.reciprocal(rstd[:, 0:S1], std[:, 0:S1])
                settle()
                for a in range(0, KT, 2):
                    for k in (a, a + 1):
                        nc.vector.scalar_tensor_tensor(out=uT[:, k, 0:S1], in0=hx[:, k, :], scalar=gains[:, col + k:col + k + 1],
                                                       in1=rstd[:, 0:S1], op0=ALU.mult, op1=ALU.mult)
                    split_in_place(uT[:, a:a + 2, 0:S1], uH[:, a:a + 2, :]).then_inc(u_ready, 1)

            def post_norm(n, col):
                settle()
                dve.wait_ge(std_ready, n + 1)
                nc.vector.reciprocal(rstd[:, 0:S1], std[:, 0:S1])
                settle()
                for a in range(2):
                    half = slice(4 * a, 4 * a + 4)
                    for k in range(4 * a, 4 * a + 4):
                        nc.vector.scalar_tensor_tensor(out=yT[:, k, 0:S1], in0=yT[:, k, 0:S1], scalar=gains[:, col + k:col + k + 1],
                                                       in1=rstd[:, 0:S1], op0=ALU.mult, op1=ALU.mult)
                    settle()
                    nc.vector.tensor_tensor(hx[:, half, :], hx[:, half, :], yT[:, half, 0:S1], ALU.add).then_inc(h_ready, 1)

            def memory_input(l, c):
                b, u = tiles[("v", l, 3)]
                dve.wait_ge(full[b], u)
                for k in (2 * c, 2 * c + 1):
                    nc.vector.tensor_scalar(uT[:, k, 0:S1], memn[:, k, :], gains[:, 48 + 8 * l + k:49 + 8 * l + k],
                                            None, ALU.mult)
                split_in_place(uT[:, 2 * c:2 * c + 2, 0:S1], uH[:, 2 * c:2 * c + 2, :]).then_inc(mem_u, 1)

            def attention(l, kind):
                base = {"A": 0, "B": 20, "X": 16 if l == 0 else 28}[kind]
                scale = 1.0 / 16 if kind == "X" else 0.125
                n = items(kind)

                def maxima(m):
                    settle()
                    for t in range(score_tiles(kind)):
                        s, c = place(kind, m, t)
                        b = filled("S", l, kind, m, t)
                        src = ps[:, b, :]
                        if kind == "A":
                            nc.vector.tensor_tensor(probs[:, s, c, :], src, maskA, ALU.add).then_inc(free[b], 1)
                            settle()
                            src = probs[:, s, c, :]
                        nc.vector.reduce_max(rmax[:, s, c, :], src.rearrange("p (j t) -> p j t", j=2), AX.X)
                    settle()
                    c0 = place(kind, m)[1]
                    nc.vector.tensor_scalar(nmax[:, s, c0:c + 1, :], rmax[:, s, c0:c + 1, :],
                                            -scale, None, ALU.mult).then_inc(max_ready, 1)

                def normalise(m):
                    s, c = place(kind, m)
                    c1 = c + score_tiles(kind)
                    settle()
                    dve.wait_ge(exp_ready, base + m + 1)
                    nc.vector.reciprocal(rden[:, s, c:c1, :], den[:, s, c:c1, :])
                    settle()
                    if kind == "B":
                        nc.vector.tensor_scalar(rden[:, s, 1, :], rden[:, s, 1, :], lam, -1.0, ALU.mult, ALU.mult)
                        settle()
                    for j in range(2):
                        p = probs[:, s, c, j * S1:(j + 1) * S1]
                        ins = nc.vector.tensor_scalar(p, p, rden[:, s, c, j:j + 1], None, ALU.mult)
                    if kind == "B":
                        settle()
                        for j in range(2):
                            p = probs[:, s, 0, j * S1:(j + 1) * S1]
                            p1 = probs[:, s, 1, j * S1:(j + 1) * S1]
                            ins = nc.vector.scalar_tensor_tensor(out=p, in0=p1, scalar=rden[:, s, 1, j:j + 1], in1=p,
                                                                 op0=ALU.mult, op1=ALU.add)
                    ins.then_inc(p_ready, 1)

                def heads_out(m):
                    if kind == "A":
                        if m % 2 == 0:
                            return
                        b, u = tiles[("V", l, kind, m - 1)]
                        dve.wait_ge(full[b], u)
                        split_out(oT[:, m // 2, 0:S1], oH[:, m // 2, :], ps[:, b, 0:S1]).then_inc(o_ready, 1)
                    elif kind == "B":
                        b = filled("V", l, kind, m)
                        nc.vector.tensor_copy(oT[:, m, 0:S1], ps[:, b, 0:S1]).then_inc(o_ready, 1)
                    else:
                        b = filled("V", l, kind, m)
                        split_out(oT[:, 2 * m:2 * m + 2, 0:S1], oH[:, 2 * m:2 * m + 2, :],
                                  ps[:, b, :].rearrange("p (a t) -> p a t", a=2)).then_inc(o_ready, 1)
                    nc.vector.drain().then_inc(free[b], 1)

                for m in range(min(ahead(kind), n)):
                    maxima(m)
                for m in range(n):
                    normalise(m)
                    if m + ahead(kind) < n:
                        maxima(m + ahead(kind))
                    if m > 1:
                        heads_out(m - 2)
                    if kind != "X" and m < 4:
                        memory_input(l, m)
                heads_out(n - 2)
                heads_out(n - 1)

            nc.vector.memset(ones[:, :], 1.0).then_inc(memset_done, 1)
            nc.vector.memset(eps6[:, :], 1e-6).then_inc(memset_done, 1)
            dve.wait_ge(const_in, 16 * CONSTS)
            angle, turns = rot_tmp[:, 0:S1], rot_tmp[:, S1:2 * S1]
            nc.vector.tensor_copy(angle, pos_i[:, :])
            settle()
            nc.vector.tensor_scalar(angle, angle, invf, None, ALU.mult)
            settle()
            nc.vector.tensor_scalar(turns, angle, 1.0 / (2 * math.pi), ROUND, ALU.mult, ALU.add)
            settle()
            nc.vector.tensor_scalar(turns, turns, -ROUND, None, ALU.add)
            settle()
            for part in TWO_PI:
                nc.vector.scalar_tensor_tensor(out=angle, in0=turns, scalar=-part, in1=angle, op0=ALU.mult, op1=ALU.add)
                settle()
            nc.vector.tensor_scalar(rope[:, 1, :], angle, math.pi, -math.pi, ALU.min, ALU.max)
            nc.vector.tensor_scalar(angle, angle, math.pi / 2, None, ALU.add)
            settle()
            nc.vector.tensor_scalar(turns, angle, math.pi, -2 * math.pi, ALU.is_gt, ALU.mult)
            settle()
            nc.vector.tensor_tensor(angle, angle, turns, ALU.add)
            settle()
            nc.vector.tensor_scalar(rope[:, 0, :], angle, math.pi, -math.pi, ALU.min, ALU.max).then_inc(rope_args, 1)
            for a in range(2):
                nc.vector.tensor_tensor(lamv[:, 2 * a, :], lamv[:, 2 * a, :], lamv[:, 2 * a + 1, :], ALU.mult)
            settle()
            for a in range(2):
                ins = nc.vector.reduce_sum(lam_parts[:, a:a + 1], lamv[:, 2 * a, :], AX.X)
            ins.then_inc(lam_args, 1)
            dve.wait_ge(gain_cols, 1)
            dve.wait_ge(std_ready, 1)
            nc.vector.reciprocal(rstd[:, 0:S1], std[:, 0:S1]).then_inc(memn_ready, 1)
            settle()
            nc.vector.tensor_tensor(memn[:, :, :], memn[:, :, :], over(rstd[:, 0:S1], KT), ALU.mult)
            nc.vector.tensor_scalar(gains[:, 112:113], gains[:, 112:113], 1.0 - LAM_INIT, None, ALU.mult)
            dve.wait_ge(x_ready, 4)
            for l in range(DEPTH):
                kind = "AB"[l]
                n0 = 1 + 6 * l
                pre_norm(n0, 8 * l)
                if l == 0:
                    dve.wait_ge(rope_ready, 1)
                    dve.wait_ge(lam_exp, 1)
                    nc.vector.tensor_tensor(lam, lam_parts[:, 2:3], lam_parts[:, 3:4], ALU.subtract)
                    settle()
                    nc.vector.tensor_scalar(lam, lam, LAM_INIT, None, ALU.add)
                for g in range(8):
                    b = filled("rot", l, g)
                    qk = (qT if g < 4 else kT)[:, 2 * (g % 4):2 * (g % 4) + 2, :]
                    tmp = rot_tmp[:, :].rearrange("p (a t) -> p a t", a=2)
                    nc.vector.tensor_tensor(tmp, ps[:, b, :].rearrange("p (a t) -> p a t", a=2), over(rope[:, 1, :], 2),
                                            ALU.mult).then_inc(free[b], 1)
                    nc.vector.tensor_tensor(qk, qk, over(rope[:, 0, :], 2), ALU.mult)
                    settle()
                    nc.vector.tensor_tensor(qk, qk, tmp, ALU.add).then_inc(qk_ready, 1)
                    settle()
                attention(l, kind)
                if kind == "B":
                    for c in range(4):
                        two = slice(2 * c, 2 * c + 2)
                        dve.wait_ge(sub_std, c + 1)
                        nc.vector.reciprocal(yT[:, two, 0:S1], yT[:, two, 0:S1])
                        settle()
                        nc.vector.scalar_tensor_tensor(out=oT[:, two, 0:S1], in0=oT[:, two, 0:S1], scalar=gains[:, 112:113],
                                                       in1=yT[:, two, 0:S1], op0=ALU.mult, op1=ALU.mult)
                        split_in_place(oT[:, two, 0:S1], oH[:, two, :]).then_inc(sub_done, 1)
                post_norm(n0 + 1, 16 + 8 * l)
                filled("mv", l, 3)
                pre_norm(n0 + 2, 32 + 8 * l)
                attention(l, "X")
                post_norm(n0 + 3, 64 + 8 * l)
                pre_norm(n0 + 4, 80 + 8 * l)
                for c in range(11):
                    dve.wait_ge(silu_ready, 11 * l + c + 1)
                    b = filled("u", l, c)
                    h2 = hid[:, 2 * c:2 * c + 2, :]
                    nc.vector.tensor_tensor(h2, h2, ps[:, b, :].rearrange("p (a t) -> p a t", a=2), ALU.mult)
                    nc.vector.drain().then_inc(free[b], 1)
                    split_in_place(h2, hidH(2 * c, 2)).then_inc(hid_ready, 1)
                post_norm(n0 + 5, 96 + 8 * l)
            def h4(b, L0, L1):
                return heads(ps[:, b, :])[0:L0, :, 0:L1]

            def per_head(x, L, w):
                return x.unsqueeze(2).broadcast_to([L, DH, w])

            def all_heads(x, L, w):
                return x.unsqueeze(1).broadcast_to([L, DH, w])

            b, u = tiles[("d", 1, 3)]
            dve.wait_ge(full[b], u)
            settle()
            for x in (tok, cum, logits, idxf, ecum):
                nc.vector.memset(x[:], 0.0)
            nc.vector.memset(gate_log[:, :, :], 0.0)
            nc.vector.memset(grp8[:, :, :], NEG)
            nc.vector.memset(eps5[:, :], 1e-5)
            nc.vector.memset(eps128[:, :], 128e-6).then_inc(zeros2, 1)
            nc.vector.memset(chosen[:, :, :], 0.0)
            nc.vector.memset(rank1[:, :, :], 0.0)
            nc.vector.memset(starts[:, :], 0.0)
            for b in range(BANKS):
                nc.vector.drain().then_inc(loop_free[b], 1)
            dve.wait_ge(const2_in[0], 16 * 9)
            for l in range(DEPTH):
                G0 = 113 + 81 * l
                settle()
                nc.vector.memset(conv_in[:, :, 0:3], 0.0)
                dve.wait_ge(tok_ready, l + 1)
                settle()
                nc.vector.tensor_tensor(gate_x[:, :, :], tok[:, :, 12:16], over(rows2[:, l, 40:44], 3), ALU.add)
                nc.vector.tensor_scalar(gate_log[:, :, 4:8], tok[:, :, 8:12], -1.0, None, ALU.mult)
                settle()
                nc.vector.tensor_scalar(gate_log[:, :, 0:4], gate_x[:, :, :], -1.0, None, ALU.mult)
                settle()
                nc.vector.tensor_tensor(gate_log[:, :, 0:4], gate_log[:, :, 0:4], gate_x[:, :, :], ALU.min).then_inc(sp_args, 1)
                nc.vector.tensor_scalar(tok[:, :, 0:8], tok[:, :, 0:8], SH ** -0.5, None, ALU.mult)
                def rotate(which):
                    for what, nm, i, j in [t for t in rot_tiles(which) if t[0] == "rot2"]:
                        b = filled("rot2", l, nm, i)
                        x = dict(sq=qs, sk=ks, iq=iq, ik=ik)[nm][:, i, :]
                        settle()
                        nc.vector.tensor_tensor(rot2_tmp[:, :], ps[:, b, 0:S2], sin2, ALU.mult).then_inc(free[b], 1)
                        nc.vector.tensor_tensor(x, x, cos2, ALU.mult)
                        settle()
                        nc.vector.tensor_tensor(x, x, rot2_tmp[:, :], ALU.add).then_inc(rot_done, 1)

                rotate(INDEX)
                dve.wait_ge(sp_logs, l + 1)
                nc.vector.tensor_scalar(gate_x[:, :, :], gate_x[:, :, :], 0.0, None, ALU.max)
                nc.vector.tensor_scalar(neg_a[:, :], neg_a[:, :], -1.0, None, ALU.mult)
                nc.vector.tensor_scalar(gate_exp[:, :, 4:8], gate_exp[:, :, 4:8], 1.0, None, ALU.add)
                settle()
                nc.vector.tensor_tensor(gate_x[:, :, :], gate_x[:, :, :], gate_log[:, :, 0:4], ALU.add)
                nc.vector.reciprocal(beta[:, :, :], gate_exp[:, :, 4:8])
                settle()
                nc.vector.tensor_tensor(g_tok[:, :, :], gate_x[:, :, :], over(neg_a[:, :], 3), ALU.mult).then_inc(gb_ready, 1)
                for n, (t0, L) in enumerate(TOK):
                    for h in range(SH):
                        i = 24 * l + 8 * n + h
                        dve.wait_ge(relu_ready, i + 1)
                        wi = tok[0:L, n, h:h + 1]
                        settle()
                        if h == 0:
                            nc.vector.tensor_scalar(score[0:L, n, :], relu_s[0:L, h % 2, :], wi, None, ALU.mult).then_inc(relu_used, 1)
                        else:
                            nc.vector.scalar_tensor_tensor(out=score[0:L, n, :], in0=relu_s[0:L, h % 2, :], scalar=wi, in1=score[0:L, n, :],
                                                           op0=ALU.mult, op1=ALU.add).then_inc(relu_used, 1)
                    settle()
                    nc.vector.tensor_tensor(score[0:L, n, :], score[0:L, n, :], causal[0:L, n, :], ALU.add)
                for r in range(TOPK // 8):
                    for n, (t0, L) in enumerate(TOK):
                        settle()
                        nc.vector.max(best[0:L, n, :], score[0:L, n, :])
                        settle()
                        nc.vector.match_replace(out=score[0:L, n, :], in_to_replace=best[0:L, n, :], in_values=score[0:L, n, :], imm_value=-3e38)
                settle()
                for n, (t0, L) in enumerate(TOK):
                    nc.vector.tensor_scalar(score[0:L, n, :], score[0:L, n, :], -2e38, NEG, ALU.is_gt, ALU.mult)
                    settle()
                    nc.vector.tensor_tensor(score[0:L, n, :], score[0:L, n, :], causal[0:L, n, :], ALU.add)

                for i in range(12):
                    dve.wait_ge(conv_raw, 12 * l + i + 1)
                    x = cv_qk[:, i, :] if i < 8 else cv_v[:, i - 8, :]
                    nc.vector.tensor_scalar(x, conv_in[:, i, 0:S2], gains[:, G0 + i:G0 + i + 1], None, ALU.mult)
                    for w in range(1, 4):
                        settle()
                        c = G0 + 12 * w + i
                        ins = nc.vector.scalar_tensor_tensor(out=x, in0=conv_in[:, i, w:w + S2], scalar=gains[:, c:c + 1], in1=x,
                                                             op0=ALU.mult, op1=ALU.add)
                    ins.then_inc(conv_acc, 1)
                for i in range(8):
                    dve.wait_ge(l2_root, 8 * l + i + 1)
                    settle()
                    nc.vector.reciprocal(yT[:, i, :], yT[:, i, :])
                    settle()
                    nc.vector.tensor_tensor(cv_qk[:, i, :], cv_qk[:, i, :], yT[:, i, :], ALU.mult).then_inc(qk_unit, 1)
                rotate(ROT)
                b = filled("gcc", l)
                settle()
                nc.vector.tensor_copy(cum[:, 0:2, 0:4], ps[:, b, 0:8].rearrange("p (n c) -> p n c", n=2))
                nc.vector.tensor_copy(cum[0:16, 2, 0:4], ps[0:16, b, 8:12]).then_inc(free[b], 1)
                for n, (t0, L) in enumerate(TOK):
                    b = filled("gcb", l, n)
                    d = heads(decay)[0:L, :, 0:L]
                    settle()
                    nc.vector.tensor_copy(cum[:, n, 8:12], heads(ps[:, b, :])[:, :, L - 1])
                    nc.vector.tensor_tensor(d, h4(b, L, L), per_head(cum[0:L, n, 0:4], L, L), ALU.subtract)
                    settle()
                    nc.vector.tensor_tensor(d, d, all_heads(decay_mask[0:L, 0:L], L, L), ALU.add).then_inc(decay_args, 1)
                    b = filled("bb", l, n)
                    bs = heads(beta_strict)[0:L, :, 0:L]
                    nc.vector.tensor_tensor(bs, h4(b, L, L), all_heads(strict[0:L, 0:L], L, L), ALU.mult).then_inc(free[b], 1)
                    dve.wait_ge(decay_ready, 3 * l + n + 1)
                    b = filled("KK", l, n)
                    lt = heads(LT[:, n, :])[0:L, :, 0:L]
                    nc.vector.tensor_tensor(lt, h4(b, L, L), d, ALU.mult).then_inc(free[b], 1)
                    settle()
                    nc.vector.tensor_tensor(lt, lt, bs, ALU.mult).then_inc(lt_ready, 1)
                    b = filled("KQ", l, n)
                    nc.vector.tensor_tensor(heads(QK[:, n, :])[0:L, :, 0:L], h4(b, L, L), d, ALU.mult).then_inc(free[b], 1)
                    dve.wait_ge(egc_ready, 3 * l + n + 1)
                    nc.vector.tensor_tensor(cv_qk[:, 0:4, t0:t0 + L], cv_qk[:, 0:4, t0:t0 + L], heads(egc)[:, :, 0:L], ALU.mult)
                    b = filled("kt", l, n)
                    nc.vector.tensor_copy(k_tok[0:L, n, :], ps[0:L, b, :]).then_inc(free[b], 1)
                    b = filled("vt", l, n)
                    nc.vector.tensor_tensor(heads(v_beta[:, n, :])[0:L], h4(b, L, P), per_head(beta[0:L, n, :], L, P),
                                            ALU.mult).then_inc(free[b], 1)
                    nc.vector.drain().then_inc(qk_dec, 1)
                nc.vector.tensor_tensor(cum[:, :, 4:8], cum[:, :, 8:12], cum[:, :, 0:4], ALU.subtract).then_inc(cum_ready, 1)
                for lv in range(7):
                    for n in range(3):
                        if lv >= LV[n]:
                            continue
                        L = TOK[n][1]
                        tm, tt = heads(Tm[:, n, :])[0:L, :, 0:L], heads(TT[:, n, :])[0:L, :, 0:L]
                        settle()
                        if lv == 0:
                            eye = all_heads(ident[0:L, 0:L], L, L)
                            dve.wait_ge(as_ready, as_at[l][(0, n)])
                            nc.vector.tensor_tensor(tt, eye, heads(As[:, n, :])[0:L, :, 0:L], ALU.subtract)
                            b = filled("X", l, lv, n)
                            nc.vector.tensor_tensor(tm, eye, h4(b, L, L), ALU.subtract).then_inc(free[b], 1)
                        else:
                            b = filled("Y", l, lv, n)
                            nc.vector.tensor_tensor(tm, tm, h4(b, L, L), ALU.subtract).then_inc(free[b], 1)
                            b = filled("Z", l, lv, n)
                            nc.vector.tensor_tensor(tt, tt, h4(b, L, L), ALU.subtract).then_inc(free[b], 1)
                        nc.vector.drain().then_inc(t_ready, 1)
                dve.wait_ge(ecum_ready, l + 1)
                nc.vector.tensor_tensor(ecum[:, :, 0:4], ecum[:, :, 0:4], beta[:, :, :], ALU.mult)
                settle()
                for n, (t0, L) in enumerate(TOK):
                    kt = heads(k_tok[:, n, :])[0:L]
                    nc.vector.tensor_tensor(heads(k_be[:, n, :])[0:L], kt, per_head(ecum[0:L, n, 0:4], L, P), ALU.mult).then_inc(kbe_ready, 1)
                settle()
                for n, (t0, L) in enumerate(TOK):
                    kt = heads(k_tok[:, n, :])[0:L]
                    nc.vector.tensor_tensor(kt, kt, per_head(ecum[0:L, n, 4:8], L, P), ALU.mult)
                nc.vector.drain().then_inc(tokens_ready, 1)
                for n in range(2):
                    b = filled("su", l, n)
                    if n == 0:
                        nc.vector.tensor_copy(state, ps[:, b, :]).then_inc(state_ready, 1)
                    else:
                        for h in range(DH):
                            s_h = state[:, h * P:(h + 1) * P]
                            nc.vector.scalar_tensor_tensor(out=s_h, in0=s_h, scalar=ecum[:, n, 8 + h:9 + h], in1=ps[:, b, h * P:(h + 1) * P],
                                                           op0=ALU.mult, op1=ALU.add)
                        nc.vector.drain().then_inc(state_ready, 1)
                    nc.vector.drain().then_inc(free[b], 1)
                def delta_head(h):
                    dve.wait_ge(on_root, 4 * l + h + 1)
                    nc.vector.reciprocal(yT[:, h, :], yT[:, h, :])
                    settle()
                    nc.vector.scalar_tensor_tensor(out=oT[:, h, :], in0=oT[:, h, :], scalar=gains[:, G0 + 48:G0 + 49], in1=yT[:, h, :],
                                                   op0=ALU.mult, op1=ALU.mult)
                    settle()
                    nc.vector.tensor_tensor(oT[:, h, :], oT[:, h, :], z_gate[:, h, :], ALU.mult).then_inc(dn_done, 1)

                def max_unit(m):
                    n, h = units[m]
                    t0, L = TOK[n]
                    s = m % AHEAD1
                    b = filled("aS", l, m)
                    p = probs2[0:L, s, 0:t0 + L]
                    settle()
                    nc.vector.tensor_tensor(p, ps[0:L, b, 0:t0 + L], score[0:L, n, 0:t0 + L], ALU.add).then_inc(free[b], 1)
                    settle()
                    nc.vector.reduce_max(stat2[0:L, 0, s:s + 1], p, AX.X)
                    settle()
                    nc.vector.tensor_scalar(stat2[0:L, 1, s:s + 1], stat2[0:L, 0, s:s + 1], -0.125, None, ALU.mult).then_inc(max2, 1)

                def norm_unit(m):
                    n, h = units[m]
                    t0, L = TOK[n]
                    s = m % AHEAD1
                    settle()
                    dve.wait_ge(exp2, 24 * l + m + 1)
                    nc.vector.reciprocal(stat2[0:L, 3, s:s + 1], stat2[0:L, 2, s:s + 1])
                    settle()
                    p = probs2[0:L, s, 0:t0 + L]
                    nc.vector.tensor_scalar(p, p, stat2[0:L, 3, s:s + 1], None, ALU.mult).then_inc(p2, 1)

                def out_unit(m):
                    if m % 2:
                        n, h = units[m]
                        t0, L = TOK[n]
                        b = filled("aV", l, m - 1)
                        nc.vector.tensor_copy(oT[:, 4 + h // 2, t0:t0 + L], ps[:, b, 0:L]).then_inc(sa_ready, 1)
                        nc.vector.drain().then_inc(free[b], 1)
                for m in range(AHEAD):
                    max_unit(m)
                for m in range(24):
                    norm_unit(m)
                    if m + AHEAD < 24:
                        max_unit(m + AHEAD)
                    if m % 5 == 3 and m < 5 * DH:
                        delta_head(m // 5)
                    if m > 1:
                        out_unit(m - 2)
                out_unit(22)
                out_unit(23)

                def layer_norm(j, x, g_at, b_at):
                    dve.wait_ge(mean_ready, 2 * l + j + 1)
                    settle()
                    for a in range(2):
                        half = x[:, 4 * a:4 * a + 4, :]
                        nc.vector.tensor_tensor(half, half, over(std[:, :], 4), ALU.subtract).then_inc(cent_ready, 1)
                    dve.wait_ge(ln_root, 2 * l + j + 1)
                    nc.vector.reciprocal(rstd[:, :], std[:, :])
                    settle()
                    nc.vector.tensor_tensor(x[:, :, :], x[:, :, :], over(rstd[:, :], KT), ALU.mult)
                    settle()
                    for k in range(KT):
                        nc.vector.tensor_scalar(hT[:, k, :], x[:, k, :], gains[:, g_at + k:g_at + k + 1], gains[:, b_at + k:b_at + k + 1],
                                                ALU.mult, ALU.add)
                    nc.vector.drain().then_inc(ln_done, 1)

                for i in range(KT):
                    b = filled("wo", l, i)
                    nc.vector.scalar_tensor_tensor(out=hT[:, i, :], in0=hT[:, i, :], scalar=ALPHA, in1=ps[:, b, 0:S2],
                                                   op0=ALU.mult, op1=ALU.add).then_inc(mix_ready, 1)
                    nc.vector.drain().then_inc(free[b], 1)
                layer_norm(0, hT, G0 + 49, G0 + 57)
                nc.vector.tensor_scalar(yacc[:, :, :], hT[:, :, :], ALPHA, None, ALU.mult)
                b = filled("rt", l)
                nc.vector.tensor_tensor(logits[:, 0:2, :], ps[:, b, 0:72].rearrange("p (n c) -> p n c", n=2), over(rows2[:, l, 0:36], 2), ALU.add)
                nc.vector.tensor_tensor(logits[0:16, 2, :], ps[0:16, b, 72:108], rows2[0:16, l, 0:36], ALU.add).then_inc(free[b], 1)
                settle()
                nc.vector.tensor_copy(grp8[:, :, 0:4], logits[:, :, 0:4])
                settle()
                for n in range(3):
                    nc.vector.max(top8[:, 0, n, :], grp8[:, n, :])
                settle()
                for n in range(3):
                    nc.vector.max_index(idx8[:, 0, n, :], top8[:, 0, n, :], grp8[:, n, :])
                settle()
                nc.vector.tensor_copy(idxf[:, 0, :, :], idx8[:, 0, :, :])
                settle()
                lg = comb[:, 1, :, :]
                for n in range(3):
                    nc.vector.tensor_scalar(lg[:, n, :], group, idxf[:, 0, n, 0:1], None, ALU.is_equal)
                settle()
                nc.vector.tensor_scalar(lg, lg, -NEG, NEG, ALU.mult, ALU.add)
                settle()
                nc.vector.tensor_tensor(lg, lg, logits[:, :, 4:36], ALU.add)
                settle()
                for n in range(3):
                    nc.vector.max(top8[:, 1, n, :], lg[:, n, :])
                settle()
                for n in range(3):
                    nc.vector.max_index(idx8[:, 1, n, :], top8[:, 1, n, :], lg[:, n, :])
                nc.vector.tensor_tensor(rexp[:, :, 0:4], grp8[:, :, 0:4], top8[:, 0, :, 0:1].broadcast_to([P, 3, 4]), ALU.subtract)
                nc.vector.tensor_tensor(rexp[:, :, 4:5], top8[:, 1, :, 1:2], top8[:, 1, :, 0:1], ALU.subtract)
                nc.vector.drain().then_inc(rt_args, 1)
                nc.vector.tensor_copy(idxf[:, 1, :, :], idx8[:, 1, :, :])
                dve.wait_ge(rt_exp, l + 1)
                nc.vector.reduce_sum(gates[:, :, 0:1], rexp[:, :, 0:4], AX.X)
                nc.vector.tensor_scalar(gates[:, :, 1:2], rexp[:, :, 4:5], 1.0, None, ALU.add)
                settle()
                nc.vector.tensor_tensor(gates[:, :, 0:1], gates[:, :, 0:1], gates[:, :, 1:2], ALU.mult)
                settle()
                nc.vector.reciprocal(gates[:, :, 2:3], gates[:, :, 0:1])
                settle()
                nc.vector.tensor_tensor(gates[:, :, 3:4], gates[:, :, 2:3], rexp[:, :, 4:5], ALU.mult)
                settle()
                for a in range(2):
                    for n in range(3):
                        nc.vector.tensor_scalar(comb[:, a, n, :], iota, idxf[:, 1, n, a:a + 1], gates[:, n, 2 + a:3 + a], ALU.is_equal, ALU.mult)
                settle()
                nc.vector.tensor_tensor(comb[:, 0, :, :], comb[:, 0, :, :], comb[:, 1, :, :], ALU.add)
                settle()
                for n, (t0, L) in enumerate(TOK):
                    nc.vector.tensor_scalar(comb[0:L, 1, n, :], iota[0:L], idxf[0:L, 1, n, 0:1], None, ALU.is_equal)
                    settle()
                    nc.vector.scalar_tensor_tensor(out=chosen[0:L, n, :], in0=iota[0:L], scalar=idxf[0:L, 1, n, 1:2], in1=comb[0:L, 1, n, :],
                                                   op0=ALU.is_equal, op1=ALU.add)
                nc.vector.drain().then_inc(comb_ready, 1)
                b = filled("rk", l)
                for n, (t0, L) in enumerate(TOK):
                    nc.vector.scalar_tensor_tensor(out=rank1[0:L, n, :], in0=ps[0:L, b, n * NE:(n + 1) * NE], scalar=1.0, in1=chosen[0:L, n, :],
                                                   op0=ALU.add, op1=ALU.mult)
                nc.vector.reduce_max(group_max[:, :], ps[:, b, 3 * NE:4 * NE].rearrange("p (g j) -> p g j", g=8), AX.X)
                nc.vector.drain().then_inc(free[b], 1)
                nc.vector.tensor_scalar(rank[:, :, :], rank1[:, :, :], -1.0, None, ALU.add)
                nc.vector.tensor_tensor(over_edge[:, :, :], group_max[:, :].unsqueeze(2).broadcast_to([P, 8, 8]),
                                        edges[:, 1:9].unsqueeze(1).broadcast_to([P, 8, 8]), ALU.is_gt)
                if l:
                    nc.vector.tensor_copy(starts[:, 0:1], starts[:, 8:9])
                settle()
                nc.vector.reduce_sum(passes[:, :], over_edge[:, :, :], AX.X)
                settle()
                for g in range(8):
                    nc.vector.scalar_tensor_tensor(out=starts[:, g + 1:g + 2], in0=passes[:, g:g + 1], scalar=1.0, in1=starts[:, g:g + 1],
                                                   op0=ALU.add, op1=ALU.add)
                    settle()
                nc.vector.tensor_copy(steps[:, l, 0:9], starts[:, :])
                nc.vector.tensor_scalar(steps[:, l, 9:18], starts[:, :], -1.0, None, ALU.add)
                nc.vector.tensor_tensor(started[:, :, :], count.unsqueeze(2).broadcast_to([P, MAX_STEPS, 8]),
                                        starts[:, 1:9].unsqueeze(1).broadcast_to([P, MAX_STEPS, 8]), ALU.is_ge)
                nc.vector.tensor_tensor(spans[:, :], starts[:, 1:9], starts[:, 0:8], ALU.subtract)
                settle()
                nc.vector.reduce_sum(group_at[:, :], started[:, :, :], AX.X)
                settle()
                nc.vector.tensor_tensor(started[:, :, :], started[:, :, :], spans[:, :].unsqueeze(1).broadcast_to([P, MAX_STEPS, 8]), ALU.mult)
                nc.vector.tensor_scalar(group_at[:, :], group_at[:, :], 7.0, None, ALU.min)
                settle()
                nc.vector.reduce_sum(pass_at[:, :], started[:, :, :], AX.X)
                nc.vector.tensor_copy(step_group[:, :], group_at[:, :])
                settle()
                nc.vector.scalar_tensor_tensor(out=pass_at[:, :], in0=pass_at[:, :], scalar=starts[:, 0:1], in1=count,
                                               op0=ALU.add, op1=ALU.subtract)
                settle()
                nc.vector.tensor_scalar(pass_at[:, :], pass_at[:, :], -32.0, None, ALU.mult)
                nc.vector.drain().then_inc(steps_ready, 1)
                settle()
                dve.wait_ge(steps_ready, l + 1)
                extra = lambda b: l + 1 if b in LEAD_BANKS else 0

                def select(s, g):
                    for n in range(3):
                        nc.vector.scalar_tensor_tensor(
                            out=sel[:, n, :].rearrange("p (j c) -> p j c", j=4), in0=iota.unsqueeze(1).broadcast_to([P, 4, 32]),
                            scalar=pass_at[:, bass.ds(s, 1)],
                            in1=rank[:, n, bass.ds(g * 4, 4)].unsqueeze(2).broadcast_to([P, 4, 32]), op0=ALU.add, op1=ALU.is_equal)
                    settle()
                    for n in range(3):
                        nc.vector.tensor_tensor(sel_gate[:, n, :].rearrange("p (j c) -> p j c", j=4),
                                                sel[:, n, :].rearrange("p (j c) -> p j c", j=4),
                                                comb[:, 0, n, bass.ds(g * 4, 4)].unsqueeze(2).broadcast_to([P, 4, 32]), ALU.mult)
                    nc.vector.drain().then_inc(sel_ready, 1)

                start = dve.value_load(steps[0:1, l, 0:1], min_val=0, max_val=MAX_STEPS // 2)
                stop = dve.value_load(steps[0:1, l, 8:9], min_val=1, max_val=MAX_STEPS - 1)
                settle()
                select(start, 0)
                with nc.vector.Fori(start, stop) as s:
                    g = dve.value_load(step_group[0:1, bass.ds(s + 1, 1)], min_val=0, max_val=7)
                    settle()
                    dve.wait_ge(loop_full[LB["scatter"]], s + (l + 1))
                    select(s + 1, g)
                    b = LB["up"]
                    dve.wait_ge(esilu_ready, s + 1)
                    nc.vector.tensor_tensor(e_hid[:, :], e_silu[:, :], ps[:, b, DE:2 * DE], ALU.mult).then_inc(ehid_ready, 1)
                    nc.vector.drain().then_inc(loop_free[b], 1)
                    for i in range(KT):
                        b = LB["out"][i]
                        dve.wait_ge(loop_full[b], s * L_USES[b] + (extra(b) + L_OUT[i]))
                        nc.vector.tensor_tensor(yacc[:, i, :], yacc[:, i, :], ps[:, b, 0:S2], ALU.add).then_inc(loop_free[b], 1)
                nc.vector.drain().then_inc(mix_ready, 1)
                layer_norm(1, yacc, G0 + 65, G0 + 73)


NAMES = ["x", "mem", "positions", "mix_pre_g", "mix_post_g", "mem_pre_g", "mem_kv_g", "mem_post_g", "ffn_pre_g",
         "ffn_post_g", "a_w_in", "a_w_out", "b_w_in", "b_w_out", "b_lam_q1", "b_lam_k1", "b_lam_q2", "b_lam_k2",
         "b_sub_g", "x_wq", "x_wkv", "x_wo", "w_gate_up", "w_down", "meta_tokens_2",
         "w_in_2", "conv_w_2", "a_log_2", "dt_bias_2", "dn_norm_g_2", "w_out_2", "ln1_g_2", "ln1_b_2", "w_grp_2",
         "b_grp_2", "w_rtr_2", "b_rtr_2", "w1_2", "w3_2", "w2_2", "ln2_g_2", "ln2_b_2"]


def kernel(**inputs):
    import concourse.bacc as bacc
    from concourse.bass_utils import run_bass_kernel_spmd

    nc = bacc.Bacc("TRN2", target_bir_lowering=False, num_devices=1)
    given = {name: np.ascontiguousarray(inputs[name]) for name in NAMES}
    given["tables1"], given["tables2"] = tables()
    arrays, access = {}, {}
    for name, a in given.items():
        arrays[f"in_{name}"] = a
        access[name] = nc.dram_tensor(f"in_{name}", a.shape, mybir.dt.from_np(a.dtype), kind="ExternalInput").ap()
    out = nc.dram_tensor("out", (1, S1, DM), F32, kind="ExternalOutput").ap()
    build(nc, access, out)
    result = run_bass_kernel_spmd(nc, [arrays], core_ids=[0])
    return result.results[0]["out"]
```
